# Optimizing a Trainium2 kernel written in Bass

```python
import jax, jax.numpy as jnp
from jax import lax
import numpy as np
import math

D_MODEL = 1024
BATCH = 1
SEQ = 512
DEPTH = 2

HEAD_DIM = 64
N_ATTN_HEADS = 8
ATTN_WIDTH = N_ATTN_HEADS * HEAD_DIM
DILATED_PATTERNS = ((128, 1), (512, 4), (2048, 16))
ROPE_THETA = 10000.0
NEG_INF = -1e30

N_DELTA_HEADS = 4
DELTA_DK = 128
DELTA_DV = 128
DELTA_K_WIDTH = N_DELTA_HEADS * DELTA_DK
DELTA_V_WIDTH = N_DELTA_HEADS * DELTA_DV
DELTA_CONV = 4
DELTA_CHUNK = 64

MIX_WIDTH = ATTN_WIDTH + DELTA_V_WIDTH
IN_COLS = 3 * ATTN_WIDTH + 2 * DELTA_K_WIDTH + 2 * DELTA_V_WIDTH + 2 * N_DELTA_HEADS

D_FF = 2816
FFN_CONV = 3
EPS = 1e-6


def rms_norm(x, w):
    xf = x.astype(jnp.float32)
    y = xf * lax.rsqrt(jnp.mean(xf * xf, axis=-1, keepdims=True) + EPS)
    return (y * w.astype(jnp.float32)).astype(x.dtype)

def rope_tables(seq, dim):
    inv = 1.0 / (ROPE_THETA ** (jnp.arange(0, dim, 2, dtype=jnp.float32) / dim))
    ang = jnp.arange(seq, dtype=jnp.float32)[:, None] * inv[None, :]
    return jnp.cos(ang), jnp.sin(ang)

def apply_rope(x, cos, sin):
    x1, x2 = jnp.split(x, 2, axis=-1)
    c = cos[None, :, None, :]
    s = sin[None, :, None, :]
    return jnp.concatenate([x1 * c - x2 * s, x1 * s + x2 * c], axis=-1)

def causal_dwconv(x, w):
    K, C = w.shape
    return lax.conv_general_dilated(
        x, w[:, None, :].astype(x.dtype), window_strides=(1,), padding=[(K - 1, 0)],
        dimension_numbers=('NWC', 'WIO', 'NWC'), feature_group_count=C)

def dilated_branch(q, k, v, window, dilation):
    B, S, H, D = q.shape
    n = window // dilation
    L = S // dilation
    nb = -(-L // n)
    Lp = nb * n

    def split(t):
        return t.reshape(B, L, dilation, H, D).transpose(0, 2, 3, 1, 4)

    qs = jnp.pad(split(q), ((0, 0), (0, 0), (0, 0), (0, Lp - L), (0, 0)))
    qs = qs.reshape(B, dilation, H, nb, n, D)

    def kv_blocks(t):
        tp = jnp.pad(split(t), ((0, 0), (0, 0), (0, 0), (n, Lp - L), (0, 0)))
        prev = tp[:, :, :, :Lp].reshape(B, dilation, H, nb, n, D)
        cur = tp[:, :, :, n:].reshape(B, dilation, H, nb, n, D)
        return jnp.concatenate([prev, cur], axis=4)

    kb = kv_blocks(k)
    vb = kv_blocks(v)
    s = jnp.einsum('brhnqd,brhnkd->brhnqk', qs, kb) * (D ** -0.5)
    a = jnp.arange(n)[:, None]
    c = jnp.arange(2 * n)[None, :]
    key_pos = (jnp.arange(nb)[:, None, None] - 1) * n + c[None]
    valid = ((c >= a) & (c <= a + n))[None] & (key_pos >= 0)
    s = jnp.where(valid, s, NEG_INF)
    m = jnp.max(s, axis=-1, keepdims=True)
    e = jnp.exp(s - m)
    l = jnp.sum(e, axis=-1, keepdims=True)
    o = jnp.einsum('brhnqk,brhnkd->brhnqd', e, vb) / l
    lse = (m + jnp.log(l))[..., 0]

    o = o.reshape(B, dilation, H, Lp, D)[:, :, :, :L]
    o = o.transpose(0, 3, 1, 2, 4).reshape(B, S, H, D)
    lse = lse.reshape(B, dilation, H, Lp)[:, :, :, :L]
    lse = lse.transpose(0, 3, 1, 2).reshape(B, S, H)
    return o, lse

def dilated_attention(q, k, v):
    outs, lses = [], []
    for window, dilation in DILATED_PATTERNS:
        o, lse = dilated_branch(q, k, v, window, dilation)
        outs.append(o)
        lses.append(lse)
    wts = jax.nn.softmax(jnp.stack(lses, axis=0), axis=0)
    return jnp.sum(wts[..., None] * jnp.stack(outs, axis=0), axis=0)

def gated_delta_rule(q, k, v, beta, g):
    B, S, H, K = q.shape
    V = v.shape[-1]
    C = DELTA_CHUNK
    N = S // C
    q = q * lax.rsqrt(jnp.sum(q * q, axis=-1, keepdims=True) + EPS) * (K ** -0.5)
    k = k * lax.rsqrt(jnp.sum(k * k, axis=-1, keepdims=True) + EPS)

    def chunk(t):
        return jnp.moveaxis(t.reshape((B, N, C, H) + t.shape[3:]), 3, 1)

    q, k, v, beta, g = chunk(q), chunk(k), chunk(v), chunk(beta), chunk(g)
    g = jnp.cumsum(g, axis=-1)
    tril = jnp.tril(jnp.ones((C, C), dtype=bool))
    strict = jnp.tril(jnp.ones((C, C), dtype=bool), -1)
    decay = jnp.exp(jnp.where(tril, g[..., :, None] - g[..., None, :], -jnp.inf))
    kb = k * beta[..., None]
    A = jnp.where(strict, jnp.einsum('bhnik,bhnjk->bhnij', kb, k) * decay, 0.0)
    eye = jnp.eye(C, dtype=A.dtype)
    T = lax.linalg.triangular_solve(A + eye, jnp.broadcast_to(eye, A.shape), left_side=True,
                                    lower=True, unit_diagonal=True)
    u = jnp.einsum('bhnij,bhnjv->bhniv', T, v * beta[..., None])
    w = jnp.einsum('bhnij,bhnjk->bhnik', T, kb * jnp.exp(g)[..., None])
    qk = jnp.einsum('bhnik,bhnjk->bhnij', q, k) * decay
    q_dec = q * jnp.exp(g)[..., None]
    k_dec = k * jnp.exp(g[..., -1:] - g)[..., None]
    g_last = jnp.exp(g[..., -1])

    def step(state, xs):
        q_i, k_i, u_i, w_i, qk_i, gl = xs
        v_new = u_i - jnp.einsum('bhck,bhkv->bhcv', w_i, state)
        o = jnp.einsum('bhck,bhkv->bhcv', q_i, state) + jnp.einsum('bhij,bhjv->bhiv', qk_i, v_new)
        state = state * gl[..., None, None] + jnp.einsum('bhck,bhcv->bhkv', k_i, v_new)
        return state, o

    xs = (jnp.moveaxis(q_dec, 2, 0), jnp.moveaxis(k_dec, 2, 0), jnp.moveaxis(u, 2, 0),
          jnp.moveaxis(w, 2, 0), jnp.moveaxis(qk, 2, 0), jnp.moveaxis(g_last, 2, 0))
    _, o = lax.scan(step, jnp.zeros((B, H, K, V), jnp.float32), xs)
    return jnp.transpose(o, (1, 0, 3, 2, 4)).reshape(B, S, H, V)

def hybrid_mixer(h, w_in, dn_conv_w, dn_a_log, dn_dt_bias, dn_norm_w, w_out, cos, sin):
    B, S, _ = h.shape
    proj = h @ w_in
    cuts = [ATTN_WIDTH, 2 * ATTN_WIDTH, 3 * ATTN_WIDTH,
            3 * ATTN_WIDTH + 2 * DELTA_K_WIDTH + DELTA_V_WIDTH,
            3 * ATTN_WIDTH + 2 * DELTA_K_WIDTH + 2 * DELTA_V_WIDTH,
            3 * ATTN_WIDTH + 2 * DELTA_K_WIDTH + 2 * DELTA_V_WIDTH + N_DELTA_HEADS]
    aq, ak, av, dn_qkv, dn_z, dn_b, dn_a = jnp.split(proj, cuts, axis=-1)

    aq = apply_rope(aq.reshape(B, S, N_ATTN_HEADS, HEAD_DIM).astype(jnp.float32), cos, sin)
    ak = apply_rope(ak.reshape(B, S, N_ATTN_HEADS, HEAD_DIM).astype(jnp.float32), cos, sin)
    av = av.reshape(B, S, N_ATTN_HEADS, HEAD_DIM).astype(jnp.float32)
    attn_out = dilated_attention(aq, ak, av).reshape(B, S, ATTN_WIDTH).astype(h.dtype)

    qkv = jax.nn.silu(causal_dwconv(dn_qkv, dn_conv_w)).astype(jnp.float32)
    dq, dk, dv = jnp.split(qkv, [DELTA_K_WIDTH, 2 * DELTA_K_WIDTH], axis=-1)
    beta = jax.nn.sigmoid(dn_b.astype(jnp.float32))
    g = -jnp.exp(dn_a_log.astype(jnp.float32)) * jax.nn.softplus(
        dn_a.astype(jnp.float32) + dn_dt_bias.astype(jnp.float32))
    o = gated_delta_rule(dq.reshape(B, S, N_DELTA_HEADS, DELTA_DK),
                         dk.reshape(B, S, N_DELTA_HEADS, DELTA_DK),
                         dv.reshape(B, S, N_DELTA_HEADS, DELTA_DV), beta, g)
    z = dn_z.reshape(B, S, N_DELTA_HEADS, DELTA_DV).astype(jnp.float32)
    dn_out = (rms_norm(o, dn_norm_w) * jax.nn.silu(z)).reshape(B, S, DELTA_V_WIDTH).astype(h.dtype)

    return jnp.concatenate([attn_out, dn_out], axis=-1) @ w_out

def conv_glu_ffn(h, ffn_w_in, ffn_conv_w, ffn_conv_b, ffn_w_out):
    u = causal_dwconv(h @ ffn_w_in, ffn_conv_w) + ffn_conv_b
    gate, up = jnp.split(u, 2, axis=-1)
    return (jax.nn.gelu(gate, approximate=True) * up) @ ffn_w_out

def first_inputs(seed: int = 0) -> dict:
    key = jax.random.key(seed)
    ks = jax.random.split(key, 16)
    f32 = jnp.float32
    nrm = lambda k, shape, scale: jax.random.normal(k, shape, f32) * scale
    dt = jnp.exp(jax.random.uniform(ks[4], (DEPTH, N_DELTA_HEADS), f32) *
                 (jnp.log(0.1) - jnp.log(0.001)) + jnp.log(0.001))
    return {
        'x': nrm(ks[0], (BATCH, SEQ, D_MODEL), 1.0),
        'w_in': nrm(ks[1], (DEPTH, D_MODEL, IN_COLS), D_MODEL ** -0.5),
        'dn_conv_w': nrm(ks[2], (DEPTH, DELTA_CONV, 2 * DELTA_K_WIDTH + DELTA_V_WIDTH), DELTA_CONV ** -0.5),
        'dn_a_log': jnp.log(jax.random.uniform(ks[3], (DEPTH, N_DELTA_HEADS), f32, 1.0, 16.0)),
        'dn_dt_bias': dt + jnp.log(-jnp.expm1(-dt)),
        'dn_norm_w': 1.0 + nrm(ks[5], (DEPTH, DELTA_DV), 0.05),
        'w_out': nrm(ks[6], (DEPTH, MIX_WIDTH, D_MODEL), MIX_WIDTH ** -0.5),
        'ffn_w_in': nrm(ks[7], (DEPTH, D_MODEL, 2 * D_FF), D_MODEL ** -0.5),
        'ffn_conv_w': nrm(ks[8], (DEPTH, FFN_CONV, 2 * D_FF), FFN_CONV ** -0.5),
        'ffn_conv_b': nrm(ks[9], (DEPTH, 2 * D_FF), 0.01),
        'ffn_w_out': nrm(ks[10], (DEPTH, D_FF, D_MODEL), D_FF ** -0.5),
        'norm_pre_mix': 1.0 + nrm(ks[11], (DEPTH, D_MODEL), 0.05),
        'norm_post_mix': 1.0 + nrm(ks[12], (DEPTH, D_MODEL), 0.05),
        'norm_pre_ffn': 1.0 + nrm(ks[13], (DEPTH, D_MODEL), 0.05),
        'norm_post_ffn': 1.0 + nrm(ks[14], (DEPTH, D_MODEL), 0.05),
    }

def first_block(x, w_in, dn_conv_w, dn_a_log, dn_dt_bias, dn_norm_w, w_out, ffn_w_in, ffn_conv_w,
              ffn_conv_b, ffn_w_out, norm_pre_mix, norm_post_mix, norm_pre_ffn, norm_post_ffn):
    cos, sin = rope_tables(x.shape[1], HEAD_DIM)
    for l in range(DEPTH):
        h = rms_norm(x, norm_pre_mix[l])
        mix = hybrid_mixer(h, w_in[l], dn_conv_w[l], dn_a_log[l], dn_dt_bias[l], dn_norm_w[l],
                           w_out[l], cos, sin)
        x = x + rms_norm(mix, norm_post_mix[l]).astype(x.dtype)
        h = rms_norm(x, norm_pre_ffn[l])
        f = conv_glu_ffn(h, ffn_w_in[l], ffn_conv_w[l], ffn_conv_b[l], ffn_w_out[l])
        x = x + rms_norm(f, norm_post_ffn[l]).astype(x.dtype)
    return x


CHUNK = 64
POOL_WIDTH = D_MODEL // 2
POOL_WINDOWS = (2, 4, 8, 16)
N_POOL_GROUPS = len(POOL_WINDOWS)
POOL_GROUP = POOL_WIDTH // N_POOL_GROUPS
ATTN_WIDTH_2 = D_MODEL - POOL_WIDTH
N_HEADS = ATTN_WIDTH_2 // HEAD_DIM
ROPE_DIM = HEAD_DIM // 4
ROPE_THETA_2 = 500000.0
IDX_HEADS = 8
IDX_DIM = 64
IDX_ROPE_DIM = IDX_DIM // 4
TOPK_MAX = 256
Q_BLOCK = 64
D_FF_2 = 4 * D_MODEL

SPLITS = (POOL_WIDTH, ATTN_WIDTH_2, ATTN_WIDTH_2, ATTN_WIDTH_2, IDX_HEADS * IDX_DIM, IDX_DIM, IDX_HEADS)
IN_WIDTH = sum(SPLITS)
SPLIT_POINTS = tuple(int(v) for v in np.cumsum(SPLITS)[:-1])


def rms_norm_2(x, g):
    xf = x.astype(jnp.float32)
    y = xf * lax.rsqrt(jnp.mean(xf * xf, axis=-1, keepdims=True) + EPS)
    return (y * g.astype(jnp.float32)).astype(x.dtype)

def rope_partial(x, pos, rot_dim):
    half = rot_dim // 2
    inv = ROPE_THETA_2 ** (-jnp.arange(half, dtype=jnp.float32) / half)
    ang = pos.astype(jnp.float32)[..., None] * inv
    cos = jnp.cos(ang)[:, :, None, :]
    sin = jnp.sin(ang)[:, :, None, :]
    x1 = x[..., :half].astype(jnp.float32)
    x2 = x[..., half:rot_dim].astype(jnp.float32)
    rot = jnp.concatenate([x1 * cos - x2 * sin, x2 * cos + x1 * sin], axis=-1)
    return jnp.concatenate([rot.astype(x.dtype), x[..., rot_dim:]], axis=-1)

def pool_mixer(u, w_pool, pool_scale):
    B, S, _ = u.shape
    ug = u.reshape(B, S, N_POOL_GROUPS, POOL_GROUP)
    cs = jnp.cumsum(ug.astype(jnp.float32), axis=1)
    t = jnp.arange(S)
    outs = []
    for g, w in enumerate(POOL_WINDOWS):
        c = cs[:, :, g]
        lagged = jnp.pad(c, ((0, 0), (w, 0), (0, 0)))[:, :S]
        cnt = jnp.minimum(t + 1, w).astype(jnp.float32)[None, :, None]
        outs.append((c - lagged) / cnt - ug[:, :, g].astype(jnp.float32))
    d = jnp.stack(outs, axis=2).astype(u.dtype)
    y = jnp.einsum('bsgc,gcd->bsgd', d, w_pool)
    return y.reshape(B, S, POOL_WIDTH) * pool_scale

def dsa_attention(q, k, v, iq, ik, iw, topk):
    B, S = q.shape[0], q.shape[1]
    n_blocks = S // Q_BLOCK
    key_chunk = jnp.arange(S) // CHUNK
    ik32 = ik.astype(jnp.float32)

    def block(i):
        start = i * Q_BLOCK
        qb = lax.dynamic_slice_in_dim(q, start, Q_BLOCK, axis=1)
        iqb = lax.dynamic_slice_in_dim(iq, start, Q_BLOCK, axis=1).astype(jnp.float32)
        iwb = lax.dynamic_slice_in_dim(iw, start, Q_BLOCK, axis=1).astype(jnp.float32)
        q_chunk = (start + jnp.arange(Q_BLOCK)) // CHUNK
        allowed = key_chunk[None, :] <= q_chunk[:, None]
        logits = jnp.einsum('bqhd,bsd->bqhs', iqb, ik32) * (IDX_DIM ** -0.5)
        score = jnp.einsum('bqh,bqhs->bqs', iwb, jax.nn.relu(logits))
        score = jnp.where(allowed[None], score, -jnp.inf)
        top_val, top_idx = lax.top_k(score, topk)
        valid = jnp.isfinite(top_val)
        kg = jax.vmap(lambda kk, idx: kk[idx])(k, top_idx)
        vg = jax.vmap(lambda vv, idx: vv[idx])(v, top_idx)
        s = jnp.einsum('bqhd,bqkhd->bqhk', qb.astype(jnp.float32), kg.astype(jnp.float32)) * (HEAD_DIM ** -0.5)
        s = jnp.where(valid[:, :, None, :], s, -jnp.inf)
        p = jax.nn.softmax(s, axis=-1)
        o = jnp.einsum('bqhk,bqkhd->bqhd', p, vg.astype(jnp.float32))
        return o.astype(q.dtype)

    out = lax.map(block, jnp.arange(n_blocks))
    return jnp.transpose(out, (1, 0, 2, 3, 4)).reshape(B, S, N_HEADS * HEAD_DIM)

def second_inputs(seed: int = 0) -> dict:
    key = jax.random.key(seed)
    ks = jax.random.split(key, 12)
    f32 = jnp.float32
    def gain(k):
        return 1.0 + 0.02 * jax.random.normal(k, (DEPTH, D_MODEL), f32)
    x = jax.random.normal(ks[0], (BATCH, SEQ, D_MODEL), f32)
    positions = jnp.broadcast_to(jnp.arange(SEQ, dtype=jnp.int32)[None, :], (BATCH, SEQ)).astype(jnp.int32)
    return {
        "x": x,
        "positions": positions,
        "g_pre_mix": gain(ks[1]),
        "w_in": jax.random.normal(ks[2], (DEPTH, D_MODEL, IN_WIDTH), f32) * D_MODEL ** -0.5,
        "w_pool": jax.random.normal(ks[3], (DEPTH, N_POOL_GROUPS, POOL_GROUP, POOL_GROUP), f32) * POOL_GROUP ** -0.5,
        "pool_scale": 1.0 + 0.02 * jax.random.normal(ks[4], (DEPTH, POOL_WIDTH), f32),
        "w_out": jax.random.normal(ks[5], (DEPTH, D_MODEL, D_MODEL), f32) * D_MODEL ** -0.5,
        "g_post_mix": gain(ks[6]),
        "g_pre_ffn": gain(ks[7]),
        "w_ff1": jax.random.normal(ks[8], (DEPTH, D_MODEL, D_FF_2), f32) * D_MODEL ** -0.5,
        "w_ff2": jax.random.normal(ks[9], (DEPTH, D_FF_2, D_MODEL), f32) * D_FF_2 ** -0.5,
        "g_post_ffn": gain(ks[10]),
    }

def second_block(x, positions, g_pre_mix, w_in, w_pool, pool_scale, w_out, g_post_mix,
              g_pre_ffn, w_ff1, w_ff2, g_post_ffn):
    B, S, _ = x.shape
    topk = min(TOPK_MAX, S // 4)
    for l in range(DEPTH):
        h = rms_norm_2(x, g_pre_mix[l])
        proj = h @ w_in[l]
        u_pool, q, k, v, iq, ik, iw = jnp.split(proj, SPLIT_POINTS, axis=-1)
        q = rope_partial(q.reshape(B, S, N_HEADS, HEAD_DIM), positions, ROPE_DIM)
        k = rope_partial(k.reshape(B, S, N_HEADS, HEAD_DIM), positions, ROPE_DIM)
        v = v.reshape(B, S, N_HEADS, HEAD_DIM)
        iq = rope_partial(iq.reshape(B, S, IDX_HEADS, IDX_DIM), positions, IDX_ROPE_DIM)
        ik = rope_partial(ik[:, :, None, :], positions, IDX_ROPE_DIM)[:, :, 0, :]
        iw = iw * (IDX_HEADS ** -0.5)
        a_out = pool_mixer(u_pool, w_pool[l], pool_scale[l])
        b_out = dsa_attention(q, k, v, iq, ik, iw, topk)
        mix = jnp.concatenate([a_out, b_out], axis=-1) @ w_out[l]
        x = x + rms_norm_2(mix, g_post_mix[l])
        h = rms_norm_2(x, g_pre_ffn[l])
        f = jnp.square(jax.nn.relu(h @ w_ff1[l])) @ w_ff2[l]
        x = x + rms_norm_2(f, g_post_ffn[l])
    return x


def setup_inputs(seed=0):
    out = dict(first_inputs(seed))
    for name, value in second_inputs(seed + 1).items():
        if name != "x":
            out[name + "_2"] = value
    return out


def reference(
    x, w_in, dn_conv_w, dn_a_log, dn_dt_bias, dn_norm_w, w_out, ffn_w_in, ffn_conv_w,
    ffn_conv_b, ffn_w_out, norm_pre_mix, norm_post_mix, norm_pre_ffn, norm_post_ffn,
    positions_2, g_pre_mix_2, w_in_2, w_pool_2, pool_scale_2, w_out_2, g_post_mix_2,
    g_pre_ffn_2, w_ff1_2, w_ff2_2, g_post_ffn_2,
):
    x = first_block(
        x, w_in, dn_conv_w, dn_a_log, dn_dt_bias, dn_norm_w, w_out, ffn_w_in, ffn_conv_w,
        ffn_conv_b, ffn_w_out, norm_pre_mix, norm_post_mix, norm_pre_ffn, norm_post_ffn,
    )
    return second_block(
        x, positions_2, g_pre_mix_2, w_in_2, w_pool_2, pool_scale_2, w_out_2, g_post_mix_2,
        g_pre_ffn_2, w_ff1_2, w_ff2_2, g_post_ffn_2,
    )


_drawn_inputs = setup_inputs


def setup_inputs(seed=0):
    import zlib

    import numpy as np

    out = dict(_drawn_inputs(seed))
    spreads = {}
    factors = {'ffn_conv_b': 3.306,
     'g_pre_mix_2': 3.429,
     'pool_scale_2': 4.934,
     'g_post_mix_2': 4.716,
     'g_pre_ffn_2': 4.478,
     'g_post_ffn_2': 5.022}
    for name, (base, spread) in spreads.items():
        noise = np.random.default_rng([zlib.crc32(name.encode()), seed]).standard_normal(out[name].shape)
        drawn = base * np.exp(spread * noise) if base else spread * noise
        out[name] = __import__('jax').numpy.asarray(drawn.astype(out[name].dtype))
    for name, factor in factors.items():
        out[name] = (out[name] * factor).astype(out[name].dtype)
    return out
```

```python
from contextlib import ExitStack
import math

import numpy as np

import concourse.bass as bass
from concourse import mybir

F32 = mybir.dt.float32
F32R = mybir.dt.float32r
I32 = mybir.dt.int32
ALU = mybir.AluOpType
ACT = mybir.ActivationFunctionType
AX_X = mybir.AxisListType.X

P = 128
S = 512
D = 1024
KD = D // P
NT = S // P
LAYERS = 2
EPS = 1e-6
NEG = -1e30
REMOVED = -3e38

H1 = 8
HD = 64
HN = 4
CH = 64
NCH = S // CH
FF1 = 2816
NJ = FF1 // P
DCONV, FCONV = 4, 3

TOPK = 128
FF2 = 4096
NH2 = FF2 // P
HCH = 16
FCHUNKS = NH2 // HCH

U_IN = (28, 24)
U_OUT = (8, 8)
U1 = 28 + 8 + 2 * NJ + 3 * KD
U2 = 24 + 8 + NH2 + 2 * KD * FCHUNKS
UNITS = (U1, U2)
G_IN = (28, 25)
GROUPS = (28 + 8 + 2 * NJ + KD, 25 + 8 + NH2 + KD * FCHUNKS)
N_H1, N_ATT1, N_DN1, N_HF1, N_HID1 = 0, 8, 12, 16, 24
N_H2, N_PD2, N_PY2, N_ATT2, N_HF2, N_HID2 = 0, 8, 12, 16, 20, 28
PIECES = (24 + NJ, 28 + NH2)
N_HF = (N_HF1, N_HF2)
N_MIX = (16, 20)

PRE = 23


def ev_pre(t, k):
    return 1 + (t // 2) * (2 * PRE + 12) + 2 * k + t % 2


def ev_scan(c, j):
    return 1 + 2 * PRE + (c // 4) * (2 * PRE + 12) + 3 * (c % 4) + j


EVENTS = 1 + 2 * (2 * PRE + 12)
SLOTS = 2 * 4 * NT + 3


def mixer_order():
    steps = [("small", 0, 0)]
    for pair in range(2):
        steps += [("pre", pair, k) for k in range(PRE)]
        steps += [("scan", c, 0) for c in range(4 * pair, 4 * pair + 4)]
    order, n = [], 0
    for i, step in enumerate(steps):
        while n < SLOTS and n * len(steps) <= i * SLOTS:
            order.append(("att", n, 0))
            n += 1
        order.append(step)
    order += [("att", m, 0) for m in range(n, SLOTS)]
    return order


ORDER = mixer_order()

TOP_PLAN = ((8, 1, 3), (9, 1, 4), (10, 1, 4), (11, 1, 5), (12, 2, 4), (13, 2, 4), (14, 2, 4), (15, 2, 4),
            (16, 3, 4), (17, 3, 3), (18, 3, 3), (19, 3, 3), (20, 3, 3))
TOP_AT, _done = {}, {1: 0, 2: 0, 3: 0}
for _u, _i, _n in TOP_PLAN:
    TOP_AT[_u] = [(_i, _done[_i] + _r) for _r in range(_n)]
    _done[_i] += _n
assert set(_done.values()) == {TOPK // 8}

TWO_PI = (6.28125, 0.0019350051879882812, 2 * math.pi - 6.28125 - 0.0019350051879882812)
PI_BELOW = 3.1415925

CONST = [("cos1", S), ("sin1", S), ("count", S), ("turn1", P), ("turn2", P), ("ident", P), ("ones", P),
         ("upto", P), ("chunk", P), ("even", P), ("odd", P), ("causal", P), ("level", 6 * P),
         ("zeros", P), ("icnt", 16), ("invf", 1), ("eps", 1), ("one", 1), ("qscale", 1), ("halfpi", 1)]
CAT, _o = {}, 0
for _n, _w in CONST:
    CAT[_n] = (_o, _w)
    _o += _w
CONST_W = _o

PAR1 = [("pre", 8), ("post", 8), ("preff", 8), ("postff", 8), ("dconv", 12 * DCONV), ("dnorm", 1),
        ("alog", 4), ("dt", 4), ("fconv", 2 * NJ * FCONV), ("fbias", 2 * NJ), ("gates", KD * 8)]
PAR2 = [("pre", 8), ("post", 8), ("preff", 8), ("postff", 8), ("pscale", 4), ("gates", KD * 8)]


def offsets(table):
    at, o = {}, 0
    for n, w in table:
        at[n] = (o, w)
        o += w
    return at, o


PA1, PAR1_W = offsets(PAR1)
PA2, PAR2_W = offsets(PAR2)
PAR_W = max(PAR1_W, PAR2_W)


def constants():
    c = np.zeros((P, CONST_W), np.float32)

    def put(name, v):
        o, w = CAT[name]
        c[:, o:o + w] = v

    p = np.arange(P)
    inv = (1.0 / (np.float32(10000.0) ** (np.arange(0, HD, 2, dtype=np.float32) / np.float32(HD)))).astype(np.float32)
    ang = inv[(p % 64) % 32][:, None] * np.arange(S, dtype=np.float32)[None]
    put("cos1", np.cos(ang))
    put("sin1", np.sin(ang))
    dist = p[:, None] - (np.arange(S)[None] - (S - P))
    count = ((dist >= 0) & (dist <= 128)).astype(np.float64) + ((dist >= 0) & (dist % 4 == 0)) + ((dist >= 0) & (dist % 16 == 0))
    put("count", np.where(count > 0, np.log(np.maximum(count, 1)), NEG))
    for name, half, rot in (("turn1", 32, 64), ("turn2", 8, 16)):
        m = np.zeros((P, P), np.float32)
        for q in range(P):
            d = q % 64
            if d < half:
                m[q + half, q] = -1.0
            elif d < rot:
                m[q - half, q] = 1.0
        put(name, m)
    put("ident", np.eye(P))
    put("ones", 1.0)
    j, i = p[:, None], p[None]
    same = j // CH == i // CH
    put("upto", same & (j <= i))
    put("chunk", same)
    put("even", np.broadcast_to(j // CH == 0, (P, P)))
    put("odd", np.broadcast_to(j // CH == 1, (P, P)))
    put("causal", np.where(same & (j <= i), 0.0, NEG))
    put("level", np.concatenate([(i // (2 * b) == j // (2 * b)) & (i // b % 2 == 1) & (j // b % 2 == 0)
                                 for b in (1, 2, 4, 8, 16, 32)], axis=1))
    put("icnt", 1.0 / np.arange(1, 17, dtype=np.float32))
    f = (np.float32(500000.0) ** (-np.arange(8, dtype=np.float32) / np.float32(8))).astype(np.float32)
    put("invf", np.where(p % 64 < 16, f[p % 8], 0.0)[:, None])
    put("eps", EPS)
    put("one", 1.0)
    put("qscale", -0.5 * math.log(128.0))
    put("halfpi", math.pi / 2)
    return c


class Signal:

    def __init__(self, ctx, nc, name, per, credit=0):
        self.sem = ctx.enter_context(nc.semaphore(name))
        self.per, self.credit = per, credit

    def at(self, w, k):
        return self.credit + (LAYERS * self.per[0] if w.b else 0) + w.L * self.per[w.b] + k


class Where:

    def __init__(self, b, L):
        self.b, self.L = b, L


def build(nc, d):
    ctx = ExitStack()
    with ctx:
        def sb(name, shape, dt, c=ctx):
            return c.enter_context(nc.sbuf_tensor(name, shape, dt))

        def signal(name, first, second, credit=0):
            return Signal(ctx, nc, name, (first, second), credit)

        x = sb("x", [P, KD, S], F32)
        hH = sb("hH", [P, KD, S], F32R)
        hL = sb("hL", [P, KD, S], F32R)
        raw = sb("raw", [P, 2, KD * P], F32)
        wH = sb("wH", [P, 2, KD * P], F32R)
        wL = sb("wL", [P, 2, KD * P], F32R)
        sq = sb("sq", [P, 2, S], F32)
        piece = sb("piece", [P, 2, S], F32)
        rstd = sb("rstd", [P, 2, S], F32)
        const = sb("const", [P, CONST_W], F32)
        par = sb("par", [P, PAR_W], F32)
        gwH = sb("gwH", [P, KD * 8], F32R)
        gwL = sb("gwL", [P, KD * 8], F32R)

        with ExitStack() as share:
            mT1 = sb("mT1", [P, KD, S], F32, share)
            hidH1 = sb("hidH1", [P, NJ, S], F32R, share)
            hidL1 = sb("hidL1", [P, NJ, S], F32R, share)
        with ExitStack() as share:
            qT1 = sb("qT1", [P, 4, S], F32, share)
            kT1 = sb("kT1", [P, 4, S], F32, share)
            v1 = sb("v1", [P, NT, S], F32, share)
            dq = sb("dq", [P, HN, S], F32, share)
            dk = sb("dk", [P, HN, S], F32, share)
            dv = sb("dv", [P, HN, S], F32, share)
            kdec = sb("kdec", [P, NT, HN, P], F32, share)
            qkT = sb("qkT", [P, NT, HN, P], F32, share)
            zT = sb("zT", [P, HN, S], F32, share)
            eb = [sb(f"eb{i}", [P, HN, P], F32, share) for i in range(2)]
            ab = [sb(f"ab{i}", [P, HN, P], F32, share) for i in range(2)]
            xb = [sb(f"xb{i}", [P, HN, P], F32, share) for i in range(2)]
            xtb = [sb(f"xtb{i}", [P, HN, P], F32, share) for i in range(2)]
            mb = [sb(f"mb{i}", [P, HN, P], F32, share) for i in range(2)]
            vn = sb("vn", [P, HN, P], F32, share)
            state = sb("state", [P, HN, P], F32, share)
            gv = sb("gv", [P, 324], F32, share)
            sc1 = sb("sc1", [P, 2, S], F32, share)
            pt1 = sb("pt1", [P, 2, S], F32, share)
            ao1 = sb("ao1", [P, 2, P], F32, share)
            st1 = sb("st1", [P, 17], F32, share)
        rope2 = sb("rope2", [P, 2, S], F32)
        with ExitStack() as share:
            mT2 = sb("mT2", [P, KD, S], F32, share)
            hidH2 = sb("hidH2", [P, HCH, S], F32R, share)
            hidL2 = sb("hidL2", [P, HCH, S], F32R, share)
            relu = sb("relu", [P, 2, S], F32, share)
        with ExitStack() as share:
            qT2 = sb("qT2", [P, 4, S], F32, share)
            kT2 = sb("kT2", [P, 4, S], F32, share)
            v2 = sb("v2", [P, NT, S], F32, share)
            iqT = sb("iqT", [P, 4, S], F32, share)
            ikT = sb("ikT", [P, S], F32, share)
            bias2 = sb("bias2", [P, 10 * P], F32, share)
            ir = sb("ir", [P, 2, S], F32, share)
            pu = sb("pu", [P, 2, S], F32, share)
            turn2 = sb("turn2_in", [P, 2, S], F32, share)
            pdH = sb("pdH", [P, 4, S], F32R, share)
            pdL = sb("pdL", [P, 4, S], F32R, share)
            iw = sb("iw", [P, NT, 8], F32, share)
            top8 = sb("top8", [P, 8], F32, share)
            sc2 = sb("sc2", [P, 2, S], F32, share)
            pt2 = sb("pt2", [P, 2, S], F32, share)
            ao2 = sb("ao2", [P, 2, P], F32, share)
            st2 = sb("st2", [P, 17], F32, share)
        with ExitStack() as share:
            posi = sb("posi", [P, S], I32, share)
            ang = sb("ang", [P, 4, S], F32, share)

        bank = [ctx.enter_context(nc.psum_tensor(f"bank{i}", [P, S], F32)) for i in range(8)]
        ACC = bank[0:2]
        STAT = bank[2]
        DB = bank[0:3]
        SC = bank[3:5]
        PT, OA, TRO = bank[5:8]

        def cst(name, a=0, b=None):
            o, n = CAT[name]
            return const[:, o + a:o + (n if b is None else b)]

        def prm(w, name, a, b):
            o = (PA2 if w.b else PA1)[name][0]
            return par[:, o + a:o + b]

        def prmd(w, name, i):
            return par[:, bass.ds(i + (PA2 if w.b else PA1)[name][0], 1)]

        loaded = [signal(f"loaded{s}", 16 * U1 // 2, 16 * U2 // 2) for s in range(2)]
        w_hi = signal("w_hi", U1, U2, 2)
        w_lo = signal("w_lo", U1, U2, 2)
        unit_done = signal("unit_done", U1, U2, 2)
        acc_free = [signal(f"acc_free{b}", GROUPS[0] // 2, (GROUPS[1] + 1 - b) // 2, 1) for b in range(2)]
        piece_ready = signal("piece_ready", *PIECES)
        piece_hi = signal("piece_hi", *PIECES)
        piece_lo = signal("piece_lo", *PIECES, 2)
        sq_ready = signal("sq_ready", 44, 32)
        sq_used = signal("sq_used", 44, 32, 2)
        stat_free = signal("stat_free", 16, 4, 1)
        rstd_ready = signal("rstd_ready", 16, 4)
        rstd_used = signal("rstd_used", 16, 4, 2)
        x_ready = signal("x_ready", 16, 16, 8)
        par_in = signal("par_in", 16, 16)
        gw_hi = signal("gw_hi", 1, 1)
        gw_lo = signal("gw_lo", 1, 1)
        gates_done = signal("gates_done", 1, 1)
        turned = signal("turned", 12, 17)
        turn_done = signal("turn_done", 12, 17, 2)
        sc_done = signal("sc_done", 32, 32)
        sc_read = signal("sc_read", 32, 32, 2)
        nmax = signal("nmax", 32, 32)
        prob = signal("prob", 32, 32)
        pt_done = signal("pt_done", 32, 32)
        pt_copied = signal("pt_copied", 32, 32)
        pv_done = signal("pv_done", 32, 32)
        oa_read = signal("oa_read", 32, 32)
        tro_done = signal("tro_done", 16, 16)
        conv_in = signal("conv_in", 12, 0)
        dn_act = signal("dn_act", 12, 0)
        l2_done = signal("l2_done", 8, 0)
        gate_a = signal("gate_a", 1, 0)
        gate_b = signal("gate_b", 1, 0)
        g_ready = signal("g_ready", 1, 0)
        kd_in = signal("kd_in", 1, 0)
        kd_out = signal("kd_out", 1, 0)
        state_zero = signal("state_zero", 1, 0)
        d_done = signal("d_done", EVENTS, 0)
        d_free = [signal(f"d_free{b}", len(range(b, EVENTS, 3)), 0) for b in range(3)]
        gr_exp = signal("gr_exp", 4, 0)
        e_in = signal("e_in", 4, 0)
        e_ready = signal("e_ready", 4, 0)
        qdec_ready = signal("qdec_ready", 4, 0)
        xt_ready = signal("xt_ready", 4, 0)
        lt_ready = signal("lt_ready", 20, 0)
        glu_in = signal("glu_in", 2 * NJ, 0)
        gelu_done = signal("gelu_done", NJ, 0)
        ix_done = signal("ix_done", 0, 32)
        ix_relu = signal("ix_relu", 0, 32)
        ix_used = signal("ix_used", 0, 32, 2)
        const_in = ctx.enter_context(nc.semaphore("const_in"))
        x_in = ctx.enter_context(nc.semaphore("x_in"))
        pos_in = ctx.enter_context(nc.semaphore("pos_in"))
        rope_sin_in = ctx.enter_context(nc.semaphore("rope_sin_in"))
        rope_ready = ctx.enter_context(nc.semaphore("rope_ready"))
        stored = ctx.enter_context(nc.semaphore("stored"))

        def heads(ap):
            return ap.rearrange("p (h c) -> p h c", c=P)

        def per_head(ap, n=P):
            return ap.unsqueeze(2).broadcast_to([P, HN, n])

        def over_heads(ap, h=HN):
            return ap.unsqueeze(1).broadcast_to([P, h, ap.shape[-1]])

        def gcol(a, b=None):
            return gv[:, a:a + 16 if b is None else b]

        BA, XA, AX, E1, EBV, SP_, BETA, G_, SM, KDI, KD_, EG, GLB, BG, EA = (
            0, 32, 48, 64, 80, 96, 112, 128, 144, 208, 224, 240, 256, 288, 304)

        def tile4(a, t):
            return gv[:, a + 4 * t:a + 4 * t + 4]

        ATT = ((qT1, kT1, v1, sc1, pt1, ao1, st1, 0, N_ATT1), (qT2, kT2, v2, sc2, pt2, ao2, st2, 4, N_ATT2))
        MX, NMX, SUM, RS = 0, 4, 8, 12

        def bias_of(b, i):
            if b == 0:
                return cst("count", S - P * (i + 1), S)
            o = P * (i * (i + 1) // 2)
            return bias2[:, o:o + P * (i + 1)]

        def att_step(n):
            return n // 8, n // 2 % 4, n % 2

        def xconv(c):
            return xb[c % 2][:, :, :].rearrange("p h c -> p (h c)")

        def turn_src(b, j):
            if b == 0:
                return mb[j % 2][:, :, :].rearrange("p h c -> p (h c)")
            return turn2[:, j % 2, :]

        def turn_dst(b, j):
            if b == 0:
                return (qT1, kT1)[j // 4][:, j % 4, :]
            if j == 0:
                return ikT[:, :]
            return (iqT, qT2, kT2)[(j - 1) // 4][:, (j - 1) % 4, :]

        N_ROT = (8, 13)
        MT = (mT1, mT2)

        block = ctx.enter_context(nc.Block())

        @block.sync
        def _(sp):
            sp.dma_start(const[:, :], d["const"]).then_inc(const_in, 16)
            sp.dma_start(x[:, :, :], d["x"]).then_inc(x_in, 16)

            def load(w, src, i2, s):
                sp.wait_ge(w_hi.sem, w_hi.at(w, 2 * i2 + s - 1))
                sp.wait_ge(w_lo.sem, w_lo.at(w, 2 * i2 + s - 1))
                sp.dma_start(raw[:, s, :], src).then_inc(loaded[s].sem, 16)

            for b in range(2):
                with sp.Fori(0, LAYERS) as L:
                    w = Where(b, L)
                    with sp.Fori(0, UNITS[b] // 2) as i:
                        for s in range(2):
                            load(w, d[f"w{b}"][L * UNITS[b] + i * 2 + s], i, s)
            load(Where(1, LAYERS), d["w1"][0], 0, 0)
            sp.wait_ge(x_ready.sem, x_ready.at(Where(1, LAYERS), 0))
            sp.dma_start(d["out"], x[:, :, :]).then_inc(stored, 16)
            sp.wait_ge(stored, 16)
            sp.wait_ge(loaded[0].sem, loaded[0].at(Where(1, LAYERS), 16))

        @block.gpsimd
        def _(pool):
            for ring in (w_lo, piece_lo):
                pool.nop().then_inc(ring.sem, ring.credit)

            def w_low(w, i2, s):
                pool.wait_ge(w_hi.sem, w_hi.at(w, 2 * i2 + s + 1))
                pool.wait_ge(unit_done.sem, unit_done.at(w, 2 * i2 + s - 1))
                pool.tensor_tensor(wL[:, s, :], raw[:, s, :], wH[:, s, :].bitcast(F32),
                                   ALU.subtract).then_inc(w_lo.sem, 1)

            def next_low(w, i2, s):
                w_low(w, i2 + s, 1 - s)

            def piece_low(w, n, s, dst, hi):
                pool.wait_ge(piece_hi.sem, piece_hi.at(w, n + 1))
                pool.tensor_tensor(dst, piece[:, s, :], hi.bitcast(F32), ALU.subtract).then_inc(piece_lo.sem, 1)

            def layer_params(w):
                pool.wait_ge(x_ready.sem, x_ready.at(w, 0))
                width = PAR2_W if w.b else PAR1_W
                pool.dma_start(par[:, 0:width], d[f"par{w.b}"][w.L]).then_inc(par_in.sem, 16)
                pool.wait_ge(gw_hi.sem, gw_hi.at(w, 1))
                pool.tensor_tensor(gwL[:, :], prm(w, "gates", 0, KD * 8), gwH[:, :].bitcast(F32),
                                   ALU.subtract).then_inc(gw_lo.sem, 1)

            def level(w, t, l):
                pool.tensor_tensor(eb[t % 2][:, :, :], ab[t % 2][:, :, :],
                                   over_heads(cst("level", l * P, l * P + P)), ALU.mult).then_inc(lt_ready.sem, 1)

            def norm_pieces(w, n0):
                for k in range(KD):
                    piece_low(w, n0 + k, (n0 + k) % 2, hL[:, k, :], hH[:, k, :])

            w_low(Where(0, 0), 0, 0)
            with pool.Fori(0, LAYERS) as L:
                w = Where(0, L)
                layer_params(w)
                norm_pieces(w, N_H1)
                for u in range(28):
                    next_low(w, u // 2, u % 2)
                for kind, a, k in ORDER:
                    if kind == "att" and a % 8 == 2 and a >= 10:
                        f = (a - 10) // 8
                        piece_low(w, N_ATT1 + f, f % 2, hL[:, f, :], hH[:, f, :])
                    if kind == "pre" and k == 4:
                        for t in (2 * a, 2 * a + 1):
                            pool.wait_ge(xt_ready.sem, xt_ready.at(w, t + 1))
                            level(w, t, 1)
                    if kind == "pre" and k in (5, 8, 11, 14):
                        l = (k - 5) // 3 + 1
                        for t in (2 * a, 2 * a + 1):
                            pool.wait_ge(d_done.sem, d_done.at(w, ev_pre(t, k) + 1))
                            level(w, t, l + 1)
                for h in range(HN):
                    piece_low(w, N_DN1 + h, h % 2, hL[:, 4 + h, :], hH[:, 4 + h, :])
                with pool.Fori(0, 4) as i:
                    for s in range(2):
                        next_low(w, 14 + i, s)
                norm_pieces(w, N_HF1)
                with pool.Fori(0, NJ // 2) as i:
                    for q in range(2):
                        for s in range(2):
                            next_low(w, 18 + i * 2 + q, s)
                        piece_low(w, N_HID1 + i * 2 + q, q, hidL1[:, bass.ds(i * 2 + q, 1), :],
                                  hidH1[:, bass.ds(i * 2 + q, 1), :])
                with pool.Fori(0, 12) as i:
                    for s in range(2):
                        next_low(w, 40 + i, s)

            w = Where(1, 0)
            pool.wait_ge(x_ready.sem, x_ready.at(w, 0))
            pool.dma_start(posi[:, :], d["pos"].partition_broadcast(P)).then_inc(pos_in, 16)
            with pool.Fori(0, LAYERS) as L:
                w = Where(1, L)
                layer_params(w)
                norm_pieces(w, N_H2)
                for u in range(17):
                    next_low(w, u // 2, u % 2)
                for g in range(4):
                    next_low(w, (17 + g) // 2, (17 + g) % 2)
                    piece_low(w, N_PD2 + g, g % 2, pdL[:, g, :], pdH[:, g, :])
                for u in range(21, 24):
                    next_low(w, u // 2, u % 2)
                for g in range(4):
                    piece_low(w, N_PY2 + g, g % 2, hL[:, g, :], hH[:, g, :])
                for f in range(4):
                    piece_low(w, N_ATT2 + f, f % 2, hL[:, 4 + f, :], hH[:, 4 + f, :])
                with pool.Fori(0, 4) as i:
                    for s in range(2):
                        next_low(w, 12 + i, s)
                norm_pieces(w, N_HF2)
                for c in range(FCHUNKS):
                    with pool.Fori(0, HCH // 2) as i:
                        for s in range(2):
                            next_low(w, 16 + 16 * c + i, s)
                            piece_low(w, N_HID2 + HCH * c + i * 2 + s, s, hidL2[:, bass.ds(i * 2 + s, 1), :],
                                      hidH2[:, bass.ds(i * 2 + s, 1), :])
                    with pool.Fori(0, KD) as i:
                        for s in range(2):
                            next_low(w, 24 + 16 * c + i, s)

        @block.scalar
        def _(act):
            for ring in (w_hi, unit_done, *acc_free, sq_used, stat_free, rstd_used, sc_read, turn_done, ix_used):
                act.nop().then_inc(ring.sem, ring.credit)
            act.wait_ge(const_in, 16)

            def w_high(w, i2, s):
                act.wait_ge(loaded[s].sem, loaded[s].at(w, 16 * (i2 + 1)))
                act.wait_ge(unit_done.sem, unit_done.at(w, 2 * i2 + s - 1))
                act.activation(wH[:, s, :], raw[:, s, :], ACT.Copy).then_inc(w_hi.sem, 1)

            def next_high(w, i2, s):
                w_high(w, i2 + s, 1 - s)

            def unit_wait(w, i2, s):
                act.wait_ge(unit_done.sem, unit_done.at(w, 2 * i2 + s + 1))

            def piece_high(w, n, s, dst):
                act.wait_ge(piece_ready.sem, piece_ready.at(w, n + 1))
                act.activation(dst, piece[:, s, :], ACT.Copy).then_inc(piece_hi.sem, 1)

            def square(w, r, s, src):
                act.wait_ge(sq_used.sem, sq_used.at(w, r - 1))
                act.activation(sq[:, s, :], src, ACT.Square).then_inc(sq_ready.sem, 1)

            def inverse_root(w, r_end, v, scale, bias):
                act.wait_ge(sq_used.sem, sq_used.at(w, r_end))
                act.wait_ge(rstd_used.sem, rstd_used.at(w, v - 1))
                act.activation(rstd[:, v % 2, :], STAT[:, :], ACT.Ln, bias=cst("eps"),
                               scale=scale).then_inc(stat_free.sem, 1)
                act.drain()
                act.activation(rstd[:, v % 2, :], rstd[:, v % 2, :], ACT.Exp, bias=bias,
                               scale=-0.5).then_inc(rstd_ready.sem, 1)

            def norm(w, r0, v, n0, x0):
                for k in range(KD):
                    act.wait_ge(x_ready.sem, x_ready.at(w, x0 + k + 1))
                    square(w, r0 + k, k % 2, x[:, k, :])
                inverse_root(w, r0 + KD, v, 1.0 / D, 0.0)
                for k in range(KD):
                    piece_high(w, n0 + k, (n0 + k) % 2, hH[:, k, :])

            def narrow_gates(w):
                act.wait_ge(par_in.sem, par_in.at(w, 16))
                act.activation(gwH[:, :], prm(w, "gates", 0, KD * 8), ACT.Copy).then_inc(gw_hi.sem, 1)

            def turn_input(w, j, i2, s, bank_i, a2, scale):
                unit_wait(w, i2, s)
                act.wait_ge(turn_done.sem, turn_done.at(w, j - 1))
                act.activation(turn_src(w.b, j), ACC[bank_i][:, :], ACT.Copy,
                               scale=scale).then_inc(acc_free[bank_i].sem, 1)

            def attention(w, n):
                q, k, v, sc, pt, ao, st, _, _ = ATT[w.b]
                if n < 32:
                    act.wait_ge(nmax.sem, nmax.at(w, n + 1))
                    wd = P * (att_step(n)[1] + 1)
                    act.activation(sc[:, n % 2, 0:wd], sc[:, n % 2, 0:wd], ACT.Exp,
                                   bias=st[:, NMX + n % 4:NMX + n % 4 + 1],
                                   accum_out=st[:, SUM + n % 4:SUM + n % 4 + 1]).then_inc(prob.sem, 1)
                m = n - 1
                if 0 <= m < 32:
                    act.wait_ge(pt_done.sem, pt_done.at(w, m + 1))
                    if m >= 2:
                        act.wait_ge(pv_done.sem, pv_done.at(w, m - 1))
                    wd = P * (att_step(m)[1] + 1)
                    act.activation(pt[:, m % 2, 0:wd], PT[:, 0:wd], ACT.Copy).then_inc(pt_copied.sem, 1)
                if n % 8 == 2 and n >= 10:
                    f = (n - 10) // 8
                    piece_high(w, ATT[w.b][8] + f, f % 2, hH[:, ATT[w.b][7] + f, :])

            def out_unit(w, i, s, j2, r, a2, bank_i):
                next_high(w, j2, s)
                unit_wait(w, j2, s)
                square(w, r, s, ACC[bank_i][:, :])
                act.activation(MT[w.b][:, bass.ds(i, 1), :], ACC[bank_i][:, :], ACT.Copy)
                act.drain().then_inc(acc_free[bank_i].sem, 1)

            w_high(Where(0, 0), 0, 0)
            act.wait_ge(x_in, 16)
            act.nop().then_inc(x_ready.sem, 8)
            with act.Fori(0, LAYERS) as L:
                w = Where(0, L)
                narrow_gates(w)
                norm(w, 0, 0, N_H1, -KD)
                for u in range(28):
                    next_high(w, u // 2, u % 2)
                    if 13 <= u < 25:
                        c = u - 13
                        act.wait_ge(acc_free[(u - 1) % 2].sem, acc_free[(u - 1) % 2].at(w, (u - 1) // 2 + 1))
                        act.activation((dq, dk, dv)[c // 4][:, c % 4, :], xconv(c), ACT.Silu).then_inc(dn_act.sem, 1)
                    if u < 12:
                        turn_input(w, u, u // 2, u % 2, u % 2, u // 2, HD ** -0.5 if u < 4 else 1.0)
                    elif u < 24:
                        c = u - 12
                        unit_wait(w, u // 2, u % 2)
                        act.activation(xconv(c), ACC[u % 2][:, :], ACT.Copy,
                                       scale=prm(w, "dconv", 4 * c + 3, 4 * c + 4)).then_inc(conv_in.sem, 1)
                    else:
                        unit_wait(w, u // 2, u % 2)
                        act.activation(zT[:, u - 24, :], ACC[u % 2][:, :], ACT.Silu).then_inc(acc_free[u % 2].sem, 1)
                act.wait_ge(gate_a.sem, gate_a.at(w, 1))
                act.activation(gcol(E1, E1 + 16), gcol(AX, AX + 16), ACT.Exp, scale=-1.0)
                act.activation(gv[:, EBV:EBV + 16].rearrange("p (t h) -> p t h", h=4),
                               gv[:, BA:BA + 32].rearrange("p (t c) -> p t c", c=8)[:, :, 0:4], ACT.Exp, scale=-1.0)
                act.activation(gcol(EA, EA + 4), prm(w, "alog", 0, 4), ACT.Exp)
                act.drain()
                act.activation(gcol(SP_, SP_ + 16), gcol(E1, E1 + 16), ACT.Ln, bias=cst("one"))
                act.drain().then_inc(gate_b.sem, 1)
                for c in range(8):
                    src = (dq, dk)[c // 4][:, c % 4, :]
                    square(w, 8 + c, c % 2, src)
                    inverse_root(w, 8 + c + 1, 1 + c, 1.0, cst("qscale") if c < 4 else 0.0)
                for kind, a, k in ORDER:
                    if kind == "att":
                        attention(w, a)
                    elif kind == "small":
                        act.wait_ge(kd_in.sem, kd_in.at(w, 1))
                        act.activation(gcol(KD_, KD_ + 16), gcol(KDI, KDI + 16), ACT.Exp)
                        act.activation(gcol(EG, EG + 16), gcol(SM, SM + 16), ACT.Exp)
                        act.activation(gcol(GLB, GLB + 32), gcol(SM + 32, SM + 64), ACT.Exp)
                        act.drain().then_inc(kd_out.sem, 1)
                    elif kind == "pre":
                        for t in (2 * a, 2 * a + 1):
                            e = ev_pre(t, k)
                            free = d_free[e % 3]
                            if k in (0, 4, 5, 8, 11, 14, 17, 21, 22):
                                act.wait_ge(d_done.sem, d_done.at(w, e + 1))
                            if k == 0:
                                act.activation(xtb[t % 2][:, :, :], heads(DB[e % 3][:, :]), ACT.Exp).then_inc(gr_exp.sem, 1)
                                act.wait_ge(e_in.sem, e_in.at(w, t + 1))
                                act.activation(eb[t % 2][:, :, :], eb[t % 2][:, :, :], ACT.Exp).then_inc(e_ready.sem, 1)
                            elif k == 4:
                                act.activation(xb[t % 2][:, :, :], heads(DB[e % 3][:, :]), ACT.Copy).then_inc(free.sem, 1)
                            elif k in (5, 8, 11, 14, 17):
                                act.activation(mb[t % 2][:, :, :], heads(DB[e % 3][:, :]), ACT.Copy).then_inc(free.sem, 1)
                            elif k == 21:
                                act.activation(dv[:, :, t * P:t * P + P], heads(DB[e % 3][:, :]), ACT.Copy).then_inc(free.sem, 1)
                            elif k == 22:
                                act.activation(dk[:, :, t * P:t * P + P], heads(DB[e % 3][:, :]), ACT.Copy).then_inc(free.sem, 1)
                    elif kind == "scan":
                        e = ev_scan(a, 1)
                        act.wait_ge(d_done.sem, d_done.at(w, e + 1))
                        act.activation(dq[:, :, a * CH:a * CH + CH],
                                       DB[e % 3][:, 0:HN * CH].rearrange("p (h c) -> p h c", c=CH),
                                       ACT.Copy).then_inc(d_free[e % 3].sem, 1)
                act.drain()
                for h in range(HN):
                    square(w, 16 + h, h % 2, dq[:, h, :])
                    inverse_root(w, 16 + h + 1, 9 + h, 1.0 / P, 0.0)
                    piece_high(w, N_DN1 + h, h % 2, hH[:, 4 + h, :])
                with act.Fori(0, 4) as i:
                    for s in range(2):
                        out_unit(w, i * 2 + s, s, i + 14, i * 2 + 20 + s, i + 14, s)
                inverse_root(w, 28, 13, 1.0 / D, 0.0)
                norm(w, 28, 14, N_HF1, 0)
                with act.Fori(0, NJ // 2) as i:
                    for q in range(2):
                        i2 = i * 2 + q + 18
                        for s in range(2):
                            next_high(w, i2, s)
                            unit_wait(w, i2, s)
                            act.activation(mT1[:, 2 * q + s, :], ACC[s][:, :], ACT.Identity,
                                           bias=prmd(w, "fbias", i * 4 + 2 * q + s),
                                           scale=prmd(w, "fconv", i * 12 + 6 * q + 3 * s + 2)).then_inc(glu_in.sem, 1)
                        act.wait_ge(acc_free[0].sem, acc_free[0].at(w, i2 + 1))
                        act.activation(mT1[:, 2 * q, :], mT1[:, 2 * q, :], ACT.Gelu_apprx_tanh).then_inc(gelu_done.sem, 1)
                        piece_high(w, N_HID1 + i * 2 + q, q, hidH1[:, bass.ds(i * 2 + q, 1), :])
                with act.Fori(0, 4) as i:
                    for m in range(2):
                        for u in range(3):
                            y = 3 * m + u
                            next_high(w, i * 3 + 40 + y // 2, y % 2)
                        unit_wait(w, i * 3 + 40 + y // 2, y % 2)
                        square(w, i * 2 + 36 + m, m, ACC[m][:, :])
                        act.activation(mT1[:, bass.ds(i * 2 + m, 1), :], ACC[m][:, :], ACT.Copy)
                        act.drain().then_inc(acc_free[m].sem, 1)
                inverse_root(w, 44, 15, 1.0 / D, 0.0)

            act.wait_ge(rope_sin_in, 1)
            act.activation(rope2[:, 1, :], ang[:, 2, :], ACT.Sin)
            act.activation(rope2[:, 0, :], ang[:, 3, :], ACT.Sin, bias=cst("halfpi"), scale=-1.0)
            act.drain().then_inc(rope_ready, 1)
            with act.Fori(0, LAYERS) as L:
                w = Where(1, L)
                narrow_gates(w)
                norm(w, 0, 0, N_H2, -KD)
                for u in range(24):
                    if u < 24:
                        next_high(w, u // 2, u % 2)
                    if u < 17:
                        turn_input(w, u, u // 2, u % 2, u % 2, u // 2, HD ** -0.5 if 5 <= u < 9 else 1.0)
                    elif u < 21:
                        g = u - 17
                        unit_wait(w, u // 2, u % 2)
                        if g >= 2:
                            act.wait_ge(piece_ready.sem, piece_ready.at(w, N_PD2 + g - 1))
                        act.activation(pu[:, g % 2, :], ACC[u % 2][:, :], ACT.Copy).then_inc(acc_free[u % 2].sem, 1)
                        piece_high(w, N_PD2 + g, g % 2, pdH[:, g, :])
                    if 5 <= u < 13:
                        for y in range(4 * (u - 5), 4 * (u - 5) + 4):
                            wd = P * (y // 8 + 1)
                            act.wait_ge(ix_done.sem, ix_done.at(w, y + 1))
                            act.wait_ge(ix_used.sem, ix_used.at(w, y - 1))
                            act.activation(ir[:, y % 2, 0:wd], (PT, OA)[y % 2][:, 0:wd], ACT.Relu,
                                           scale=HD ** -0.5).then_inc(ix_relu.sem, 1)
                for g in range(4):
                    piece_high(w, N_PY2 + g, g % 2, hH[:, g, :])
                for n in range(SLOTS):
                    attention(w, n)
                with act.Fori(0, 4) as i:
                    for s in range(2):
                        out_unit(w, i * 2 + s, s, i + 12, i * 2 + 8 + s, i + 12, (25 + s) % 2)
                inverse_root(w, 16, 1, 1.0 / D, 0.0)
                norm(w, 16, 2, N_HF2, 0)
                for c in range(FCHUNKS):
                    with act.Fori(0, HCH // 2) as i:
                        for s in range(2):
                            bk = (33 + s) % 2
                            next_high(w, i + 16 + 16 * c, s)
                            unit_wait(w, i + 16 + 16 * c, s)
                            act.activation(relu[:, s, :], ACC[bk][:, :], ACT.Relu).then_inc(acc_free[bk].sem, 1)
                            piece_high(w, N_HID2 + HCH * c + i * 2 + s, s, hidH2[:, bass.ds(i * 2 + s, 1), :])
                    with act.Fori(0, KD // 2) as i:
                        for m in range(2):
                            bk = (49 + m) % 2
                            for s in range(2):
                                next_high(w, i * 2 + 24 + 16 * c + m, s)
                            unit_wait(w, i * 2 + 24 + 16 * c + m, 1)
                            if c == 0:
                                act.activation(mT2[:, bass.ds(i * 2 + m, 1), :], ACC[bk][:, :],
                                               ACT.Copy).then_inc(acc_free[bk].sem, 1)
                            else:
                                act.wait_ge(acc_free[bk].sem, acc_free[bk].at(w, i + 12 * c + 24 + m + 1))
                                square(w, i * 2 + 24 + m, m, mT2[:, bass.ds(i * 2 + m, 1), :])
                inverse_root(w, 32, 3, 1.0 / D, 0.0)

        @block.vector
        def _(dve):
            dve.wait_ge(const_in, 16)

            def new_piece(w, n):
                dve.wait_ge(piece_lo.sem, piece_lo.at(w, n - 1))

            def release_rstd():
                dve.drain().then_inc(rstd_used.sem, 1)

            def norm(w, v, n0, name):
                dve.wait_ge(rstd_ready.sem, rstd_ready.at(w, v + 1))
                for k in range(KD):
                    new_piece(w, n0 + k)
                    dve.scalar_tensor_tensor(piece[:, k % 2, :], x[:, k, :], prm(w, name, k, k + 1),
                                             rstd[:, v % 2, :], ALU.mult, ALU.mult).then_inc(piece_ready.sem, 1)
                release_rstd()

            def residual(w, v, name):
                m = MT[w.b]
                dve.wait_ge(rstd_ready.sem, rstd_ready.at(w, v + 1))

                def scaled(k):
                    dve.scalar_tensor_tensor(m[:, k, :], m[:, k, :], prm(w, name, k, k + 1),
                                             rstd[:, v % 2, :], ALU.mult, ALU.mult)

                scaled(0)
                dve.drain()
                for k in range(KD):
                    dve.tensor_tensor(x[:, k, :], x[:, k, :], m[:, k, :], ALU.add).then_inc(x_ready.sem, 1)
                    if k + 1 < KD:
                        scaled(k + 1)
                        dve.drain()
                release_rstd()

            def turn_finish(w, j):
                t1, t2 = ATT[w.b][3][:, 0, :], ATT[w.b][3][:, 1, :]
                cos, sin = (rope2[:, 0, :], rope2[:, 1, :]) if w.b else (cst("cos1"), cst("sin1"))
                dve.wait_ge(turned.sem, turned.at(w, j + 1))
                if j < N_ROT[w.b]:
                    dve.tensor_tensor(t1, SC[j % 2][:, :], sin, ALU.mult)
                    dve.tensor_tensor(t2, turn_src(w.b, j), cos, ALU.mult)
                    dve.drain()
                    dve.tensor_tensor(turn_dst(w.b, j), t1, t2, ALU.add).then_inc(turn_done.sem, 1)
                    dve.drain()
                else:
                    f = j - N_ROT[w.b]
                    dve.tensor_copy(ATT[w.b][2][:, :, f * P:f * P + P], heads(SC[j % 2][:, :])).then_inc(turn_done.sem, 1)

            def attention(w, n):
                q, k, v, sc, pt, ao, st, _, n0 = ATT[w.b]
                if n < 32:
                    wd = P * (att_step(n)[1] + 1)
                    c = n % 4
                    dve.wait_ge(sc_done.sem, sc_done.at(w, n + 1))
                    if n >= 2:
                        dve.wait_ge(pt_done.sem, pt_done.at(w, n - 1))
                    dve.memset(st[:, 16:17], 0.0)
                    dve.tensor_tensor_reduce(sc[:, n % 2, 0:wd], SC[n % 2][:, 0:wd], bias_of(w.b, att_step(n)[1]),
                                             1.0, NEG, ALU.add, ALU.max,
                                             st[:, MX + c:MX + c + 1]).then_inc(sc_read.sem, 1)
                    dve.drain()
                    dve.tensor_scalar(st[:, NMX + c:NMX + c + 1], st[:, MX + c:MX + c + 1], -1.0, None,
                                      ALU.mult).then_inc(nmax.sem, 1)
                m = n - 2
                if 0 <= m < 32:
                    c, p = m % 4, m // 2
                    dve.wait_ge(pv_done.sem, pv_done.at(w, m + 1))
                    dve.reciprocal(st[:, RS + c:RS + c + 1], st[:, SUM + c:SUM + c + 1])
                    dve.drain()
                    if p >= 2:
                        dve.wait_ge(tro_done.sem, tro_done.at(w, p - 1))
                    dve.tensor_scalar(ao[:, p % 2, m % 2 * HD:m % 2 * HD + HD], OA[:, 0:HD],
                                      st[:, RS + c:RS + c + 1], None, ALU.mult).then_inc(oa_read.sem, 1)
                if n % 8 == 2 and n >= 10:
                    f = (n - 10) // 8
                    dve.wait_ge(tro_done.sem, tro_done.at(w, 4 * f + 4))
                    new_piece(w, n0 + f)
                    dve.tensor_copy(piece[:, f % 2, :], TRO[:, :]).then_inc(piece_ready.sem, 1)

            def convolve(w, c):
                u = c + 12
                dve.wait_ge(conv_in.sem, conv_in.at(w, c + 1))
                for lag in (1, 2, 3):
                    last = dve.scalar_tensor_tensor(xconv(c)[:, lag:S], ACC[u % 2][:, 0:S - lag],
                                                    prm(w, "dconv", 4 * c + 3 - lag, 4 * c + 4 - lag),
                                                    xconv(c)[:, lag:S], ALU.mult, ALU.add)
                    if lag < 3:
                        dve.drain()
                last.then_inc(acc_free[u % 2].sem, 1)

            def delta_gates(w):
                ba = gv[:, BA:BA + 32].rearrange("p (t c) -> p t c", c=8)

                def by_head(ap):
                    return ap.rearrange("p (t h) -> p t h", h=4)

                dve.wait_ge(gates_done.sem, gates_done.at(w, 1))
                dve.tensor_copy(gv[:, BA:BA + 32], TRO[:, 0:32])
                dve.drain()
                dve.tensor_tensor(by_head(gcol(XA, XA + 16)), ba[:, :, 4:8],
                                  over_heads(prm(w, "dt", 0, 4)), ALU.add)
                dve.drain()
                dve.tensor_scalar(gcol(AX, AX + 16), gcol(XA, XA + 16), -1.0, None, ALU.mult)
                dve.drain()
                dve.tensor_tensor(gcol(AX, AX + 16), gcol(AX, AX + 16), gcol(XA, XA + 16), ALU.max)
                dve.drain().then_inc(gate_a.sem, 1)
                dve.tensor_scalar(gcol(XA, XA + 16), gcol(XA, XA + 16), 0.0, None, ALU.max)
                dve.wait_ge(gate_b.sem, gate_b.at(w, 1))
                dve.tensor_scalar(gcol(EBV, EBV + 16), gcol(EBV, EBV + 16), 1.0, None, ALU.add)
                dve.drain()
                dve.reciprocal(gcol(BETA, BETA + 16), gcol(EBV, EBV + 16))
                dve.tensor_tensor(gcol(G_, G_ + 16), gcol(SP_, SP_ + 16), gcol(XA, XA + 16), ALU.add)
                dve.drain()
                dve.tensor_tensor(by_head(gcol(G_, G_ + 16)), by_head(gcol(G_, G_ + 16)),
                                  over_heads(gcol(EA, EA + 4)), ALU.mult)
                dve.drain()
                dve.tensor_scalar(gcol(G_, G_ + 16), gcol(G_, G_ + 16), -1.0, None, ALU.mult)
                dve.drain().then_inc(g_ready.sem, 1)

            def delta_small(w):
                dve.wait_ge(d_done.sem, d_done.at(w, 1))
                dve.tensor_copy(gcol(SM, SM + 64), DB[0][:, 0:64]).then_inc(d_free[0].sem, 1)
                dve.drain()
                dve.tensor_tensor(gcol(KDI, KDI + 16), gcol(SM + 16, SM + 32), gcol(SM, SM + 16), ALU.subtract)
                dve.drain().then_inc(kd_in.sem, 1)
                dve.wait_ge(kd_out.sem, kd_out.at(w, 1))
                dve.tensor_tensor(gcol(BG, BG + 16), gcol(BETA, BETA + 16), gcol(EG, EG + 16), ALU.mult)
                dve.drain()

            def delta_pre(w, t, k):
                e = ev_pre(t, k)
                psum, free = heads(DB[e % 3][:, :]), d_free[e % 3].sem
                E, A, X, XT = (r[t % 2][:, :, :] for r in (eb, ab, xb, xtb))
                if k in (4, 5, 8, 11, 14, 17, 21, 22):
                    return
                if k > 4 or k == 2:
                    dve.drain()
                dve.wait_ge(d_done.sem, d_done.at(w, e + 1))
                if k == 0:
                    dve.wait_ge(gr_exp.sem, gr_exp.at(w, t + 1))
                    dve.tensor_tensor(E, psum, over_heads(cst("causal")), ALU.add).then_inc(free, 1)
                    dve.drain()
                    dve.tensor_tensor(E, E, per_head(tile4(SM, t)), ALU.subtract).then_inc(e_in.sem, 1)
                elif k == 1:
                    dve.wait_ge(e_ready.sem, e_ready.at(w, t + 1))
                    dve.tensor_tensor(A, psum, E, ALU.mult).then_inc(free, 1)
                elif k == 2:
                    dve.tensor_tensor(A, psum, A, ALU.mult).then_inc(free, 1)
                elif k == 3:
                    dve.tensor_tensor(qkT[:, t, :, :], psum, E, ALU.mult).then_inc(free, 1)
                    dve.tensor_tensor(dq[:, :, t * P:t * P + P], dq[:, :, t * P:t * P + P], XT,
                                      ALU.mult).then_inc(qdec_ready.sem, 1)
                    dve.drain()
                    dve.tensor_tensor(E, A, over_heads(cst("level", 0, P)), ALU.mult)
                    dve.drain()
                    dve.tensor_tensor(XT, over_heads(cst("ident")), E, ALU.subtract).then_inc(xt_ready.sem, 1)
                elif k in (6, 9, 12, 15):
                    dve.tensor_tensor(X, X, psum, ALU.subtract).then_inc(free, 1)
                elif k in (7, 10, 13, 16, 18):
                    dve.tensor_tensor(XT, XT, psum, ALU.subtract).then_inc(free, 1)
                elif k == 19:
                    dve.tensor_tensor(kdec[:, t, :, :], psum, per_head(tile4(KD_, t)), ALU.mult)
                    dve.tensor_tensor(A, psum, per_head(tile4(BG, t)), ALU.mult)
                    dve.drain().then_inc(free, 1)
                elif k == 20:
                    dve.tensor_tensor(E, psum, per_head(tile4(BETA, t)), ALU.mult).then_inc(free, 1)

            def delta_scan(w, c):
                t, p0 = c // 2, c % 2 * CH
                e = ev_scan(c, 0)
                dve.wait_ge(d_done.sem, d_done.at(w, e + 1))
                dve.tensor_tensor(vn[p0:p0 + CH, :, :], dv[p0:p0 + CH, :, t * P:t * P + P],
                                  DB[e % 3][p0:p0 + CH, :].rearrange("p (h c) -> p h c", c=P),
                                  ALU.subtract).then_inc(d_free[e % 3].sem, 1)
                e = ev_scan(c, 2)
                dve.wait_ge(d_done.sem, d_done.at(w, e + 1))
                for h in range(HN):
                    a = GLB + 16 * (c % 2) + 4 * t + h
                    dve.scalar_tensor_tensor(state[:, h, :], state[:, h, :], gv[:, a:a + 1],
                                             DB[e % 3][:, h * P:h * P + P], ALU.mult, ALU.add)
                dve.drain().then_inc(d_free[e % 3].sem, 1)

            def delta_out(w, h):
                v = 9 + h
                dve.wait_ge(rstd_ready.sem, rstd_ready.at(w, v + 1))
                new_piece(w, N_DN1 + h)
                dve.scalar_tensor_tensor(piece[:, h % 2, :], dq[:, h, :], prm(w, "dnorm", 0, 1),
                                         rstd[:, v % 2, :], ALU.mult, ALU.mult)
                dve.drain().then_inc(rstd_used.sem, 1)
                dve.tensor_tensor(piece[:, h % 2, :], piece[:, h % 2, :], zT[:, h, :],
                                  ALU.mult).then_inc(piece_ready.sem, 1)

            with dve.Fori(0, LAYERS) as L:
                w = Where(0, L)
                norm(w, 0, N_H1, "pre")
                dve.memset(state[:, :, :], 0.0).then_inc(state_zero.sem, 1)
                for u in range(24):
                    if u < 12:
                        turn_finish(w, u)
                    else:
                        convolve(w, u - 12)
                delta_gates(w)
                for c in range(8):
                    tile = (dq, dk)[c // 4][:, c % 4, :]
                    dve.wait_ge(rstd_ready.sem, rstd_ready.at(w, c + 2))
                    dve.tensor_tensor(tile, tile, rstd[:, (c + 1) % 2, :], ALU.mult).then_inc(l2_done.sem, 1)
                    release_rstd()
                for kind, a, k in ORDER:
                    if kind == "att":
                        attention(w, a)
                    elif kind == "small":
                        delta_small(w)
                    elif kind == "pre":
                        delta_pre(w, 2 * a, k)
                        delta_pre(w, 2 * a + 1, k)
                    else:
                        delta_scan(w, a)
                for h in range(HN):
                    delta_out(w, h)
                residual(w, 13, "post")
                norm(w, 14, N_HF1, "preff")
                with dve.Fori(0, NJ // 2) as i:
                    for q in range(2):
                        for s in range(2):
                            buf = mT1[:, 2 * q + s, :]
                            dve.wait_ge(glu_in.sem, glu_in.at(w, i * 4 + 2 * q + s + 1))
                            for lag in (1, 2):
                                last = dve.scalar_tensor_tensor(
                                    buf[:, lag:S], ACC[s][:, 0:S - lag],
                                    prmd(w, "fconv", i * 12 + 6 * q + 3 * s + 2 - lag), buf[:, lag:S],
                                    ALU.mult, ALU.add)
                                if lag == 1:
                                    dve.drain()
                            last.then_inc(acc_free[s].sem, 1)
                        dve.drain()
                        dve.wait_ge(gelu_done.sem, gelu_done.at(w, i * 2 + q + 1))
                        new_piece(w, i * 2 + N_HID1 + q)
                        dve.tensor_tensor(piece[:, q, :], mT1[:, 2 * q, :], mT1[:, 2 * q + 1, :],
                                          ALU.mult).then_inc(piece_ready.sem, 1)
                residual(w, 15, "postff")

            R, N, T, A = (ang[:, i, :] for i in (2, 1, 0, 3))
            dve.wait_ge(pos_in, 16)
            dve.tensor_copy(T, posi[:, :])
            dve.drain()
            dve.tensor_scalar(T, T, cst("invf"), None, ALU.mult)
            dve.drain()
            dve.tensor_scalar(N, T, 1.0 / (2 * math.pi), None, ALU.mult)
            dve.drain()
            dve.tensor_scalar(N, N, 12582912.0, None, ALU.add)
            dve.drain()
            dve.tensor_scalar(N, N, -12582912.0, None, ALU.add)
            dve.drain()
            for part in TWO_PI:
                dve.scalar_tensor_tensor(T, N, -part, T, ALU.mult, ALU.add)
                dve.drain()
            dve.tensor_scalar(R, T, PI_BELOW, -PI_BELOW, ALU.min, ALU.max)
            dve.drain()
            dve.tensor_scalar(A, R, -1.0, None, ALU.mult)
            dve.drain()
            dve.tensor_tensor(A, A, R, ALU.max)
            dve.drain().then_inc(rope_sin_in, 1)
            dve.wait_ge(rope_ready, 1)

            def index_score(w, y):
                i, h = y // 8, y % 8
                score, r = bias_of(1, i), ir[:, y % 2, 0:P * (i + 1)]
                dve.wait_ge(ix_relu.sem, ix_relu.at(w, y + 1))
                if h == 0:
                    dve.tensor_scalar(score, r, iw[:, i, 0:1], None, ALU.mult).then_inc(ix_used.sem, 1)
                else:
                    dve.scalar_tensor_tensor(score, r, iw[:, i, h:h + 1], score, ALU.mult,
                                             ALU.add).then_inc(ix_used.sem, 1)
                dve.drain()
                if h == 7:
                    dve.memset(score[0:64, P * i + 64:P * i + P], REMOVED)
                    dve.drain()
                    if i == 0:
                        dve.tensor_scalar(score, score, 0.1 * REMOVED, NEG, ALU.is_le, ALU.mult)
                        dve.drain()

            def top_round(i, r):
                score = bias_of(1, i)
                dve.max(top8[:, :], score)
                dve.drain()
                dve.match_replace(score, top8[:, :], score, REMOVED)
                dve.drain()
                if r == TOPK // 8 - 1:
                    dve.tensor_scalar(score, score, 0.1 * REMOVED, NEG, ALU.is_gt, ALU.mult)
                    dve.drain()
                    dve.memset(score[0:64, P * i + 64:P * i + P], NEG)
                    dve.drain()

            def pool_window(w, g):
                win = 2 << g
                u = pu[:, g % 2, :]
                dve.wait_ge(acc_free[(17 + g) % 2].sem, acc_free[(17 + g) % 2].at(w, (17 + g) // 2 + 1))
                src = u
                for step in range(g + 1):
                    lag, dst = 1 << step, sc2[:, step % 2, :]
                    dve.tensor_tensor(dst[:, lag:S], src[:, lag:S], src[:, 0:S - lag], ALU.add)
                    dve.tensor_copy(dst[:, 0:lag], src[:, 0:lag])
                    dve.drain()
                    src = dst
                other = sc2[:, (g + 1) % 2, 0:win]
                dve.tensor_tensor(other, src[:, 0:win], cst("icnt", 0, win), ALU.mult)
                new_piece(w, N_PD2 + g)
                dve.scalar_tensor_tensor(piece[:, g % 2, :], src, 1.0 / win, u, ALU.mult, ALU.subtract)
                dve.drain()
                dve.tensor_tensor(piece[:, g % 2, 0:win], other, u[:, 0:win], ALU.subtract)
                dve.drain().then_inc(piece_ready.sem, 1)

            with dve.Fori(0, LAYERS) as L:
                w = Where(1, L)
                norm(w, 0, N_H2, "pre")
                for u in range(21):
                    if u < 17:
                        turn_finish(w, u)
                    else:
                        pool_window(w, u - 17)
                    if u == 1:
                        dve.wait_ge(gates_done.sem, gates_done.at(w, 1))
                        dve.tensor_scalar(iw[:, :, :], TRO[:, 0:32].rearrange("p (t h) -> p t h", h=8),
                                          8 ** -0.5, None, ALU.mult)
                        dve.drain()
                    if 5 <= u < 13:
                        for y in range(4 * (u - 5), 4 * (u - 5) + 4):
                            index_score(w, y)
                    for i, r in TOP_AT.get(u, ()):
                        top_round(i, r)
                for g in range(4):
                    u, a = (21, 21, 22, 23)[g], 21 + g
                    dve.wait_ge(unit_done.sem, unit_done.at(w, u + 1))
                    new_piece(w, N_PY2 + g)
                    dve.tensor_scalar(piece[:, g % 2, :], ACC[a % 2][:, :], prm(w, "pscale", g, g + 1), None,
                                      ALU.mult).then_inc(acc_free[a % 2].sem, 1)
                    dve.drain().then_inc(piece_ready.sem, 1)
                for n in range(SLOTS):
                    attention(w, n)
                residual(w, 1, "post")
                norm(w, 2, N_HF2, "preff")
                for c in range(FCHUNKS):
                    with dve.Fori(0, HCH // 2) as i:
                        for s in range(2):
                            bk = (33 + s) % 2
                            dve.wait_ge(acc_free[bk].sem, acc_free[bk].at(w, i + 12 * c + 16 + s + 1))
                            new_piece(w, i * 2 + N_HID2 + HCH * c + s)
                            dve.tensor_tensor(piece[:, s, :], relu[:, s, :], relu[:, s, :],
                                              ALU.mult).then_inc(piece_ready.sem, 1)
                    if c == FCHUNKS - 1:
                        with dve.Fori(0, KD // 2) as i:
                            for m in range(2):
                                bk = (49 + m) % 2
                                dve.wait_ge(unit_done.sem, unit_done.at(w, i * 4 + 48 + 32 * c + 2 * m + 2))
                                dve.tensor_tensor(mT2[:, bass.ds(i * 2 + m, 1), :], mT2[:, bass.ds(i * 2 + m, 1), :],
                                                  ACC[bk][:, :].unsqueeze(1), ALU.add).then_inc(acc_free[bk].sem, 1)
                residual(w, 3, "postff")

        @block.tensor
        def _(pe):
            pe.wait_ge(const_in, 16)
            ident = cst("ident")

            def unit(w, i2, s, bk, a2, tiles, rhs_hi, rhs_lo, first=True, last=True, pieces=None, w0=0, done=True):
                pe.wait_ge(w_lo.sem, w_lo.at(w, 2 * i2 + s + 1))
                if first:
                    pe.wait_ge(acc_free[bk].sem, acc_free[bk].at(w, a2))
                for k in range(tiles):
                    if pieces is not None:
                        pe.wait_ge(piece_lo.sem, piece_lo.at(w, pieces + k + 1))
                    c = (w0 + k) * P
                    for j, (wt, rhs) in enumerate(((wH, rhs_hi(k)), (wL, rhs_hi(k)), (wH, rhs_lo(k)))):
                        mm = pe.matmul(ACC[bk][:, :], wt[:, s, c:c + P], rhs, start=first and k == 0 and j == 0,
                                       stop=last and k == tiles - 1 and j == 2)
                if done:
                    mm.then_inc(unit_done.sem, 1)

            def h_hi(k):
                return hH[:, k, :]

            def h_lo(k):
                return hL[:, k, :]

            def sums(w, r0, v, n):
                pe.wait_ge(stat_free.sem, stat_free.at(w, v))
                for k in range(n):
                    pe.wait_ge(sq_ready.sem, sq_ready.at(w, r0 + k + 1))
                    pe.matmul(STAT[:, :], cst("ones"), sq[:, (r0 + k) % 2, :], start=k == 0,
                              stop=k == n - 1).then_inc(sq_used.sem, 1)

            def open_sum(w, v):
                pe.wait_ge(stat_free.sem, stat_free.at(w, v))
                pe.matmul(STAT[:, :], const[0:32, CAT["zeros"][0]:CAT["zeros"][0] + P], const[0:32, 0:S],
                          start=True, stop=True)

            def add_sum(w, r, s):
                pe.wait_ge(sq_ready.sem, sq_ready.at(w, r + 1))
                pe.matmul(STAT[:, :], cst("ones"), sq[:, s, :], start=False, stop=False,
                          skip_group_check=True).then_inc(sq_used.sem, 1)

            def turn(w, j):
                src = turn_src(w.b, j)
                pe.wait_ge(acc_free[j % 2].sem, acc_free[j % 2].at(w, j // 2 + 1))
                if j < N_ROT[w.b]:
                    pe.matmul(SC[j % 2][:, :], cst("turn2" if w.b else "turn1"), src, start=True,
                              stop=True).then_inc(turned.sem, 1)
                else:
                    for t in range(NT):
                        tr = pe.transpose(SC[j % 2][:, t * P:t * P + P], src[:, t * P:t * P + P], ident)
                    tr.then_inc(turned.sem, 1)

            def narrow(w):
                pe.wait_ge(gw_lo.sem, gw_lo.at(w, 1))
                for t in range(NT):
                    for k in range(KD):
                        for j, (a, g) in enumerate(((hH, gwH), (hL, gwH), (hH, gwL))):
                            mm = pe.matmul(TRO[:, t * 8:t * 8 + 8], a[:, k, t * P:t * P + P],
                                           g[:, k * 8:k * 8 + 8], start=k == 0 and j == 0,
                                           stop=k == KD - 1 and j == 2)
                mm.then_inc(gates_done.sem, 1)

            def attention(w, n):
                q, k, v, sc, pt, ao, st, _, n0 = ATT[w.b]
                if n < 32:
                    f, i, h = att_step(n)
                    if n == 0:
                        pe.wait_ge(turn_done.sem, turn_done.at(w, (12, 17)[w.b]))
                    pe.wait_ge(sc_read.sem, sc_read.at(w, n - 1))
                    pe.matmul(SC[n % 2][:, 0:P * (i + 1)], q[h * HD:h * HD + HD, f, i * P:i * P + P],
                              k[h * HD:h * HD + HD, f, 0:P * (i + 1)], start=True, stop=True).then_inc(sc_done.sem, 1)
                m = n - 1
                if 0 <= m < 32:
                    f, i, h = att_step(m)
                    pe.wait_ge(prob.sem, prob.at(w, m + 1))
                    if m:
                        pe.wait_ge(pt_copied.sem, pt_copied.at(w, m))
                    for j in range(i + 1):
                        tr = pe.transpose(PT[:, j * P:j * P + P], sc[:, m % 2, j * P:j * P + P], ident)
                    tr.then_inc(pt_done.sem, 1)
                m = n - 2
                if 0 <= m < 32:
                    f, i, h = att_step(m)
                    pe.wait_ge(pt_copied.sem, pt_copied.at(w, m + 1))
                    if m:
                        pe.wait_ge(oa_read.sem, oa_read.at(w, m))
                    for j in range(i + 1):
                        mm = pe.matmul(OA[:, 0:HD], pt[:, m % 2, j * P:j * P + P],
                                       v[:, j, (2 * f + h) * HD:(2 * f + h) * HD + HD], start=j == 0, stop=j == i)
                    mm.then_inc(pv_done.sem, 1)
                if n >= 4 and n % 2 == 0:
                    p = (n - 4) // 2
                    pe.wait_ge(oa_read.sem, oa_read.at(w, 2 * p + 2))
                    if p % 4 == 0 and p >= 4:
                        pe.wait_ge(piece_ready.sem, piece_ready.at(w, n0 + p // 4))
                    pe.transpose(TRO[:, p % 4 * P:p % 4 * P + P], ao[:, p % 2, :], ident).then_inc(tro_done.sem, 1)

            def start(w, e, *operands):
                latest = {}
                for x_ in (e - 3, *operands):
                    latest[x_ % 3] = max(latest.get(x_ % 3, x_), x_)
                for b_, x_ in latest.items():
                    if x_ >= 0:
                        pe.wait_ge(d_free[b_].sem, d_free[b_].at(w, x_ // 3 + 1))
                return DB[e % 3]

            def delta_small(w):
                pe.wait_ge(g_ready.sem, g_ready.at(w, 1))
                for b in range(2):
                    pe.wait_ge(acc_free[b].sem, acc_free[b].at(w, 14))
                pe.wait_ge(stat_free.sem, stat_free.at(w, 9))
                out = start(w, 0)
                for i, name in enumerate(("upto", "chunk", "even", "odd")):
                    mm = pe.matmul(out[:, 16 * i:16 * i + 16], cst(name), gcol(G_, G_ + 16), start=True, stop=True)
                mm.then_inc(d_done.sem, 1)

            def delta_pre(w, t, k):
                operands = {5: (4,), 6: (5,), 7: (5,), 18: (17, 16), 21: (20, 18), 22: (19,)}.get(k, ())
                if k in (8, 11, 14, 17):
                    operands = (k - 2,)
                elif k in (9, 12, 15, 10, 13, 16):
                    operands = ((k - 1, k - 2) if k % 3 == 0 else (k - 2, k - 3))
                e = ev_pre(t, k)
                out = start(w, e, *(ev_pre(t, o) for o in operands))
                tc = slice(t * P, t * P + P)
                LT, A, X, XT, M = (r[t % 2] for r in (eb, ab, xb, xtb, mb))
                two = {}
                if k == 0:
                    two = {h: (gv[:, G_ + 4 * t + h:G_ + 4 * t + h + 1].broadcast_to([P, P]), cst("upto")) for h in range(HN)}
                elif k == 1:
                    two = {h: (gv[:, BETA + 4 * t + h:BETA + 4 * t + h + 1].broadcast_to([P, P]), ident) for h in range(HN)}
                elif k == 2:
                    pe.wait_ge(l2_done.sem, l2_done.at(w, 8))
                    two = {h: (dk[:, h, tc], dk[:, h, tc]) for h in range(HN)}
                elif k == 3:
                    two = {h: (dk[:, h, tc], dq[:, h, tc]) for h in range(HN)}
                elif k == 4:
                    pe.wait_ge(xt_ready.sem, xt_ready.at(w, t + 1))
                elif k in (5, 8, 11, 14, 17):
                    l = (k - 5) // 3 + 1
                    pe.wait_ge(lt_ready.sem, lt_ready.at(w, 10 * (t // 2) + 2 * (l - 1) + t % 2 + 1))
                    two = {h: (LT[:, h, :], X[:, h, :]) for h in range(HN)}
                elif k in (6, 9, 12, 15):
                    two = {h: (XT[:, h, :], M[:, h, :]) for h in range(HN)}
                elif k in (7, 10, 13, 16, 18):
                    two = {h: (M[:, h, :], XT[:, h, :]) for h in range(HN)}
                elif k == 20:
                    pe.wait_ge(dn_act.sem, dn_act.at(w, 12))
                elif k == 21:
                    two = {h: (XT[:, h, :], LT[:, h, :]) for h in range(HN)}
                elif k == 22:
                    two = {h: (A[:, h, :], XT[:, h, :]) for h in range(HN)}
                for h in range(HN):
                    o = out[:, h * P:h * P + P]
                    if h in two:
                        mm = pe.matmul(o, two[h][0], two[h][1], start=True, stop=True)
                    elif k == 4:
                        mm = pe.transpose(o, XT[:, h, :], ident)
                    else:
                        mm = pe.transpose(o, (dk if k == 19 else dv)[:, h, tc], ident)
                mm.then_inc(d_done.sem, 1)

            def delta_scan(w, c):
                t, p0 = c // 2, c % 2 * CH
                cc = slice(c * CH, c * CH + CH)
                e = ev_scan(c, 0)
                last_state = (ev_scan(c - 1, 2),) if c else ()
                out = start(w, e, ev_pre(t, 21), ev_pre(t, 22), *last_state)
                if c == 0:
                    pe.wait_ge(state_zero.sem, state_zero.at(w, 1))
                for h in range(HN):
                    mm = pe.matmul(out[p0:p0 + CH, h * P:h * P + P], dk[:, h, cc], state[:, h, :], start=True, stop=True)
                mm.then_inc(d_done.sem, 1)
                out = start(w, e + 1, e)
                pe.wait_ge(qdec_ready.sem, qdec_ready.at(w, t + 1))
                for h in range(HN):
                    o = out[:, h * CH:h * CH + CH]
                    pe.matmul(o, state[:, h, :], dq[:, h, cc], start=True, stop=False)
                    mm = pe.matmul(o, vn[p0:p0 + CH, h, :], qkT[p0:p0 + CH, t, h, p0:p0 + CH], start=False, stop=True)
                mm.then_inc(d_done.sem, 1)
                out = start(w, e + 2)
                for h in range(HN):
                    mm = pe.matmul(out[:, h * P:h * P + P], kdec[p0:p0 + CH, t, h, :], vn[p0:p0 + CH, h, :],
                                   start=True, stop=True)
                mm.then_inc(d_done.sem, 1)

            with pe.Fori(0, LAYERS) as L:
                w = Where(0, L)
                sums(w, 0, 0, KD)
                for u in range(28):
                    unit(w, u // 2, u % 2, u % 2, u // 2, KD, h_hi, h_lo, pieces=N_H1 if u == 0 else None)
                    if 1 <= u <= 12:
                        turn(w, u - 1)
                    if u == 13:
                        narrow(w)
                for c in range(8):
                    sums(w, 8 + c, 1 + c, 1)
                for kind, a, k in ORDER:
                    if kind == "att":
                        attention(w, a)
                    elif kind == "small":
                        delta_small(w)
                    elif kind == "pre":
                        delta_pre(w, 2 * a, k)
                        delta_pre(w, 2 * a + 1, k)
                    else:
                        delta_scan(w, a)
                start(w, EVENTS, EVENTS - 2, EVENTS - 1)
                for h in range(HN):
                    sums(w, 16 + h, 9 + h, 1)
                open_sum(w, 13)
                with pe.Fori(0, KD // 2) as i:
                    for s in range(2):
                        unit(w, i + 14, s, s, i + 14, KD, h_hi, h_lo, pieces=(N_ATT1, None)[s])
                    for s in range(2):
                        add_sum(w, i * 2 + 20 + s, s)
                sums(w, 28, 14, KD)
                with pe.Fori(0, NJ) as i:
                    for s in range(2):
                        unit(w, i + 18, s, s, i + 18, KD, h_hi, h_lo, pieces=(N_HF1, None)[s])
                open_sum(w, 15)
                with pe.Fori(0, KD // 2) as i:
                    for m in range(2):
                        for u in range(3):
                            y = 3 * m + u
                            unit(w, i * 3 + 40 + y // 2, y % 2, m, i + 40, min(8, NJ - 8 * u),
                                 lambda k, u=u: hidH1[:, 8 * u + k, :], lambda k, u=u: hidL1[:, 8 * u + k, :],
                                 first=u == 0, last=u == 2, pieces=N_HID1 + 8 * u if m == 0 else None)
                    for m in range(2):
                        add_sum(w, i * 2 + 36 + m, m)

            with pe.Fori(0, LAYERS) as L:
                w = Where(1, L)
                sums(w, 0, 0, KD)
                for u in range(21):
                    unit(w, u // 2, u % 2, u % 2, u // 2, KD, h_hi, h_lo, pieces=N_H2 if u == 0 else None)
                    if 1 <= u <= 17:
                        turn(w, u - 1)
                    if u == 0:
                        narrow(w)
                    if 5 <= u < 13:
                        for y in range(4 * (u - 5), 4 * (u - 5) + 4):
                            i, h = y // 8, y % 8
                            if y == 0:
                                pe.wait_ge(turn_done.sem, turn_done.at(w, 5))
                            if y >= 2:
                                pe.wait_ge(ix_relu.sem, ix_relu.at(w, y - 1))
                            p0 = h % 2 * HD
                            pe.matmul((PT, OA)[y % 2][:, 0:P * (i + 1)], iqT[p0:p0 + HD, h // 2, i * P:i * P + P],
                                      ikT[p0:p0 + HD, 0:P * (i + 1)], start=True, stop=True).then_inc(ix_done.sem, 1)
                for g in range(4):
                    u, a = (21, 21, 22, 23)[g], 21 + g
                    unit(w, u // 2, u % 2, a % 2, a // 2, 1, lambda k, g=g: pdH[:, g, :], lambda k, g=g: pdL[:, g, :],
                         pieces=N_PD2 + g, w0=1 if g == 1 else 0, done=g > 0)
                for n in range(SLOTS):
                    attention(w, n)
                open_sum(w, 1)
                with pe.Fori(0, KD // 2) as i:
                    for s in range(2):
                        unit(w, i + 12, s, (25 + s) % 2, i + 12 + s, KD, h_hi, h_lo, pieces=(N_PY2, None)[s])
                    for s in range(2):
                        add_sum(w, i * 2 + 8 + s, s)
                sums(w, 16, 2, KD)
                for c in range(FCHUNKS):
                    with pe.Fori(0, HCH // 2) as i:
                        for s in range(2):
                            unit(w, i + 16 + 16 * c, s, (33 + s) % 2, i + 12 * c + 16 + s, KD, h_hi, h_lo,
                                 pieces=(N_HF2, None)[s])
                    if c == FCHUNKS - 1:
                        open_sum(w, 3)
                    with pe.Fori(0, KD // 2) as i:
                        for m in range(2):
                            for s in range(2):
                                unit(w, i * 2 + 24 + 16 * c + m, s, (49 + m) % 2, i + 12 * c + 24 + m, KD,
                                     lambda k, s=s: hidH2[:, 8 * s + k, :], lambda k, s=s: hidL2[:, 8 * s + k, :],
                                     first=s == 0, last=s == 1,
                                     pieces=N_HID2 + HCH * c + 8 * s if m == 0 else None)
                        if c == FCHUNKS - 1:
                            for m in range(2):
                                add_sum(w, i * 2 + 24 + m, m)


def tiles(a):
    return a.reshape(a.shape[0] // P, P, a.shape[1]).transpose(1, 0, 2)


def unit_of(a):
    u = tiles(a).reshape(P, -1)
    return np.pad(u, ((0, 0), (0, KD * P - u.shape[1])))


def columns(a, order):
    return [unit_of(a[:, c * P:c * P + P]) for c in order]


def channel_cols(a):
    return a.reshape(-1, P).T


def kernel(**inputs):
    import concourse.bacc as bacc
    from concourse.bass_utils import run_bass_kernel_spmd

    z = {k: np.ascontiguousarray(v) for k, v in inputs.items()}
    interleave = [c for j in range(NJ) for c in (j, NJ + j)]
    w0, w1, par0, par1 = [], [], [], []
    for l in range(LAYERS):
        win = z["w_in"][l]
        w0 += columns(win, range(28)) + columns(z["w_out"][l], range(KD)) + columns(z["ffn_w_in"][l], interleave)
        down = z["ffn_w_out"][l]
        for m in range(KD):
            w0 += [unit_of(down[r * P:min(r + 8, NJ) * P, m * P:m * P + P]) for r in (0, 8, 16)]
        fconv = z["ffn_conv_w"][l].reshape(FCONV, 2 * NJ, P)[:, interleave]
        par0.append(np.concatenate([
            channel_cols(z["norm_pre_mix"][l]), channel_cols(z["norm_post_mix"][l]),
            channel_cols(z["norm_pre_ffn"][l]), channel_cols(z["norm_post_ffn"][l]),
            z["dn_conv_w"][l].reshape(DCONV, 12, P).transpose(2, 1, 0).reshape(P, -1),
            z["dn_norm_w"][l][:, None],
            np.broadcast_to(z["dn_a_log"][l], (P, 4)), np.broadcast_to(z["dn_dt_bias"][l], (P, 4)),
            fconv.transpose(2, 1, 0).reshape(P, -1),
            z["ffn_conv_b"][l].reshape(2 * NJ, P)[interleave].T,
            tiles(win[:, 28 * P:]).reshape(P, -1)], axis=1))
        win = z["w_in_2"][l]
        ik = win[:, 20 * P:20 * P + 64]
        w1 += [unit_of(np.concatenate([ik, ik], axis=1))]
        w1 += columns(win, [*range(16, 20), *range(4, 8), *range(8, 12), *range(12, 16), *range(4)])
        wp = z["w_pool_2"][l]
        w1 += [unit_of(np.concatenate([wp[0], wp[1]])), unit_of(wp[2]), unit_of(wp[3])]
        w1 += columns(z["w_out_2"][l], range(KD))
        for c in range(FCHUNKS):
            w1 += columns(z["w_ff1_2"][l], range(HCH * c, HCH * c + HCH))
            down = z["w_ff2_2"][l][HCH * P * c:HCH * P * (c + 1)]
            for m in range(KD):
                w1 += [unit_of(down[r * D:r * D + D, m * P:m * P + P]) for r in range(2)]
        par1.append(np.concatenate([
            channel_cols(z["g_pre_mix_2"][l]), channel_cols(z["g_post_mix_2"][l]),
            channel_cols(z["g_pre_ffn_2"][l]), channel_cols(z["g_post_ffn_2"][l]),
            channel_cols(z["pool_scale_2"][l]), tiles(win[:, 20 * P + 64:]).reshape(P, -1)], axis=1))
    arrays = {
        "x_dram": np.ascontiguousarray(tiles(z["x"][0].T)),
        "w0_dram": np.stack(w0), "w1_dram": np.stack(w1),
        "par0_dram": np.stack(par0), "par1_dram": np.stack(par1),
        "pos_dram": z["positions_2"][0], "const_dram": constants(),
    }
    nc = bacc.Bacc("TRN2", target_bir_lowering=False, num_devices=1)
    d = {n[:-5]: nc.dram_tensor(n, a.shape, mybir.dt.from_np(a.dtype), kind="ExternalInput").ap()
         for n, a in arrays.items()}
    d["out"] = nc.dram_tensor("out_dram", (P, KD, S), F32, kind="ExternalOutput").ap()
    build(nc, d)
    r = run_bass_kernel_spmd(nc, [arrays], core_ids=[0])
    out = r.results[0]["out_dram"]
    return np.ascontiguousarray(out.transpose(1, 0, 2).reshape(D, S).T).reshape(1, S, D)
```

```python
from contextlib import ExitStack
import math

import numpy as np

import concourse.bass as bass
from concourse import mybir

F32 = mybir.dt.float32
F32R = mybir.dt.float32r
I32 = mybir.dt.int32
ALU = mybir.AluOpType
ACT = mybir.ActivationFunctionType
AX_X = mybir.AxisListType.X

P = 128
S = 512
D = 1024
KD = D // P
NT = S // P
LAYERS = 2
EPS = 1e-6
NEG = -1e30
REMOVED = -3e38

H1 = 8
HD = 64
HN = 4
CH = 64
NCH = S // CH
FF1 = 2816
NJ = FF1 // P
DCONV, FCONV = 4, 3

TOPK = 128
FF2 = 4096
NH2 = FF2 // P
HCH = 16
FCHUNKS = NH2 // HCH

U_IN = (28, 24)
U_OUT = (8, 8)
U1 = 28 + 8 + 2 * NJ + 3 * KD
U2 = 24 + 8 + NH2 + 2 * KD * FCHUNKS
UNITS = (U1, U2)
G_IN = (28, 25)
GROUPS = (28 + 8 + 2 * NJ + KD, 25 + 8 + NH2 + KD * FCHUNKS)
N_H1, N_ATT1, N_DN1, N_HF1, N_HID1 = 0, 8, 12, 16, 24
N_H2, N_PD2, N_PY2, N_ATT2, N_HF2, N_HID2 = 0, 8, 12, 16, 20, 28
PIECES = (24 + NJ, 28 + NH2)
N_HF = (N_HF1, N_HF2)
N_MIX = (16, 20)

PRE = 23


def ev_pre(t, k):
    return 1 + (t // 2) * (2 * PRE + 12) + 2 * k + t % 2


def ev_scan(c, j):
    return 1 + 2 * PRE + (c // 4) * (2 * PRE + 12) + 3 * (c % 4) + j


EVENTS = 1 + 2 * (2 * PRE + 12)
SLOTS = 2 * 4 * NT + 3


def mixer_order():
    steps = [("small", 0, 0)]
    for pair in range(2):
        steps += [("pre", pair, k) for k in range(PRE)]
        steps += [("scan", c, 0) for c in range(4 * pair, 4 * pair + 4)]
    order, n = [], 0
    for i, step in enumerate(steps):
        while n < SLOTS and n * len(steps) <= i * SLOTS:
            order.append(("att", n, 0))
            n += 1
        order.append(step)
    order += [("att", m, 0) for m in range(n, SLOTS)]
    return order


ORDER = mixer_order()

IX_AT, _y = {}, 0
for _u, _n in ((6, 3), (7, 6), (8, 6), (9, 6), (10, 6), (11, 5)):
    IX_AT[_u] = tuple(range(_y, _y + _n))
    _y += _n
assert _y == 32

BEHIND = 3
_steps = [[(i, r - (BEHIND if i == 3 else 0)) for i in (1, 2, 3)] for r in range(TOPK // 8 + BEHIND)]
_steps = [[(i, r) for i, r in step if 0 <= r < TOPK // 8] for step in _steps]
TOP_AT = {}
for _u, _n in ((9, 1), (10, 2), (11, 1), (12, 2), (13, 2), (14, 2), (15, 2), (16, 2), (17, 1), (18, 1), (19, 1),
               (21, 2)):
    TOP_AT[_u], _steps = _steps[:_n], _steps[_n:]
assert not _steps

TWO_PI = (6.28125, 0.0019350051879882812, 2 * math.pi - 6.28125 - 0.0019350051879882812)
PI_BELOW = 3.1415925

CONST = [("cos1", S), ("sin1", S), ("count", S), ("turn1", P), ("turn2", P), ("ident", P), ("ones", P),
         ("upto", P), ("chunk", P), ("even", P), ("odd", P), ("causal", P), ("level", 6 * P),
         ("zeros", P), ("icnt", 16), ("invf", 1), ("eps", 1), ("one", 1), ("qscale", 1), ("halfpi", 1)]
CAT, _o = {}, 0
for _n, _w in CONST:
    CAT[_n] = (_o, _w)
    _o += _w
CONST_W = _o

PAR1 = [("pre", 8), ("post", 8), ("preff", 8), ("postff", 8), ("dconv", 12 * DCONV), ("dnorm", 1),
        ("alog", 4), ("dt", 4), ("fconv", 2 * NJ * FCONV), ("fbias", 2 * NJ), ("gates", KD * 8)]
PAR2 = [("pre", 8), ("post", 8), ("preff", 8), ("postff", 8), ("pscale", 4), ("gates", KD * 8)]


def offsets(table):
    at, o = {}, 0
    for n, w in table:
        at[n] = (o, w)
        o += w
    return at, o


PA1, PAR1_W = offsets(PAR1)
PA2, PAR2_W = offsets(PAR2)
PAR_W = max(PAR1_W, PAR2_W)


def constants():
    c = np.zeros((P, CONST_W), np.float32)

    def put(name, v):
        o, w = CAT[name]
        c[:, o:o + w] = v

    p = np.arange(P)
    inv = (1.0 / (np.float32(10000.0) ** (np.arange(0, HD, 2, dtype=np.float32) / np.float32(HD)))).astype(np.float32)
    ang = inv[(p % 64) % 32][:, None] * np.arange(S, dtype=np.float32)[None]
    put("cos1", np.cos(ang))
    put("sin1", np.sin(ang))
    dist = p[:, None] - (np.arange(S)[None] - (S - P))
    count = ((dist >= 0) & (dist <= 128)).astype(np.float64) + ((dist >= 0) & (dist % 4 == 0)) + ((dist >= 0) & (dist % 16 == 0))
    put("count", np.where(count > 0, np.log(np.maximum(count, 1)), NEG))
    for name, half, rot in (("turn1", 32, 64), ("turn2", 8, 16)):
        m = np.zeros((P, P), np.float32)
        for q in range(P):
            d = q % 64
            if d < half:
                m[q + half, q] = -1.0
            elif d < rot:
                m[q - half, q] = 1.0
        put(name, m)
    put("ident", np.eye(P))
    put("ones", 1.0)
    j, i = p[:, None], p[None]
    same = j // CH == i // CH
    put("upto", same & (j <= i))
    put("chunk", same)
    put("even", np.broadcast_to(j // CH == 0, (P, P)))
    put("odd", np.broadcast_to(j // CH == 1, (P, P)))
    put("causal", np.where(same & (j <= i), 0.0, NEG))
    put("level", np.concatenate([(i // (2 * b) == j // (2 * b)) & (i // b % 2 == 1) & (j // b % 2 == 0)
                                 for b in (1, 2, 4, 8, 16, 32)], axis=1))
    put("icnt", 1.0 / np.arange(1, 17, dtype=np.float32))
    f = (np.float32(500000.0) ** (-np.arange(8, dtype=np.float32) / np.float32(8))).astype(np.float32)
    put("invf", np.where(p % 64 < 16, f[p % 8], 0.0)[:, None])
    put("eps", EPS)
    put("one", 1.0)
    put("qscale", -0.5 * math.log(128.0))
    put("halfpi", math.pi / 2)
    return c


class Signal:

    def __init__(self, ctx, nc, name, per, credit=0):
        self.sem = ctx.enter_context(nc.semaphore(name))
        self.per, self.credit = per, credit

    def at(self, w, k):
        return self.credit + (LAYERS * self.per[0] if w.b else 0) + w.L * self.per[w.b] + k


class Where:

    def __init__(self, b, L):
        self.b, self.L = b, L


def build(nc, d):
    ctx = ExitStack()
    with ctx:
        def sb(name, shape, dt, c=ctx):
            return c.enter_context(nc.sbuf_tensor(name, shape, dt))

        def signal(name, first, second, credit=0):
            return Signal(ctx, nc, name, (first, second), credit)

        x = sb("x", [P, KD, S], F32)
        hH = sb("hH", [P, KD, S], F32R)
        hL = sb("hL", [P, KD, S], F32R)
        raw = sb("raw", [P, 2, KD * P], F32)
        wH = sb("wH", [P, 2, KD * P], F32R)
        wL = sb("wL", [P, 2, KD * P], F32R)
        sq = sb("sq", [P, 2, S], F32)
        piece = sb("piece", [P, 2, S], F32)
        rstd = sb("rstd", [P, 2, S], F32)
        const = sb("const", [P, CONST_W], F32)
        par = sb("par", [P, PAR_W], F32)
        par_next = sb("par_next", [P, PAR_W], F32)
        gwH = sb("gwH", [P, KD * 8], F32R)
        gwL = sb("gwL", [P, KD * 8], F32R)

        with ExitStack() as share:
            mT1 = sb("mT1", [P, KD, S], F32, share)
            hidH1 = sb("hidH1", [P, NJ, S], F32R, share)
            hidL1 = sb("hidL1", [P, NJ, S], F32R, share)
            sq_sum1 = sb("sq_sum1", [P, S], F32, share)
        with ExitStack() as share:
            qT1 = sb("qT1", [P, 4, S], F32, share)
            kT1 = sb("kT1", [P, 4, S], F32, share)
            v1 = sb("v1", [P, NT, S], F32, share)
            dq = sb("dq", [P, HN, S], F32, share)
            dk = sb("dk", [P, HN, S], F32, share)
            dv = sb("dv", [P, HN, S], F32, share)
            kdec = sb("kdec", [P, NT, HN, P], F32, share)
            qkT = sb("qkT", [P, NT, HN, P], F32, share)
            zT = sb("zT", [P, HN, S], F32, share)
            eb = [sb(f"eb{i}", [P, HN, P], F32, share) for i in range(2)]
            ab = [sb(f"ab{i}", [P, HN, P], F32, share) for i in range(2)]
            xb = [sb(f"xb{i}", [P, HN, P], F32, share) for i in range(2)]
            xtb = [sb(f"xtb{i}", [P, HN, P], F32, share) for i in range(2)]
            mb = [sb(f"mb{i}", [P, HN, P], F32, share) for i in range(2)]
            vn = sb("vn", [P, HN, P], F32, share)
            state = sb("state", [P, HN, P], F32, share)
            gv = sb("gv", [P, 324], F32, share)
            sc1 = sb("sc1", [P, 2, S], F32, share)
            pt1 = sb("pt1", [P, 2, S], F32, share)
            ao1 = sb("ao1", [P, 2, P], F32, share)
            st1 = sb("st1", [P, 17], F32, share)
        rope2 = sb("rope2", [P, 2, S], F32)
        with ExitStack() as share:
            mT2 = sb("mT2", [P, KD, S], F32, share)
            hidH2 = sb("hidH2", [P, HCH, S], F32R, share)
            hidL2 = sb("hidL2", [P, HCH, S], F32R, share)
            relu = sb("relu", [P, 2, S], F32, share)
            sq_sum2 = sb("sq_sum2", [P, S], F32, share)
        with ExitStack() as share:
            qT2 = sb("qT2", [P, 4, S], F32, share)
            kT2 = sb("kT2", [P, 4, S], F32, share)
            v2 = sb("v2", [P, NT, S], F32, share)
            iqT = sb("iqT", [P, 4, S], F32, share)
            ikT = sb("ikT", [P, S], F32, share)
            bias2 = sb("bias2", [P, 10 * P], F32, share)
            ir = sb("ir", [P, 2, S], F32, share)
            pu = sb("pu", [P, 2, S], F32, share)
            turn2 = sb("turn2_in", [P, 2, S], F32, share)
            pdH = sb("pdH", [P, 4, S], F32R, share)
            pdL = sb("pdL", [P, 4, S], F32R, share)
            iw = sb("iw", [P, NT, 8], F32, share)
            top8 = sb("top8", [P, 3, 8], F32, share)
            sc2 = sb("sc2", [P, 2, S], F32, share)
            pt2 = sb("pt2", [P, 2, S], F32, share)
            ao2 = sb("ao2", [P, 2, P], F32, share)
            st2 = sb("st2", [P, 17], F32, share)
        with ExitStack() as share:
            posi = sb("posi", [P, S], I32, share)
            ang = sb("ang", [P, 4, S], F32, share)

        bank = [ctx.enter_context(nc.psum_tensor(f"bank{i}", [P, S], F32)) for i in range(8)]
        ACC = bank[0:2]
        STAT = bank[2]
        DB = bank[0:3]
        SC = bank[3:5]
        PT, OA, TRO = bank[5:8]

        def cst(name, a=0, b=None):
            o, n = CAT[name]
            return const[:, o + a:o + (n if b is None else b)]

        def prm(w, name, a, b):
            o = (PA2 if w.b else PA1)[name][0]
            return par[:, o + a:o + b]

        def prmd(w, name, i):
            return par[:, bass.ds(i + (PA2 if w.b else PA1)[name][0], 1)]

        loaded = [signal(f"loaded{s}", 16 * U1 // 2, 16 * U2 // 2) for s in range(2)]
        w_hi = signal("w_hi", U1, U2, 2)
        w_lo = signal("w_lo", U1, U2, 2)
        unit_done = signal("unit_done", U1, U2, 2)
        acc_free = [signal(f"acc_free{b}", GROUPS[0] // 2, (GROUPS[1] + 1 - b) // 2, 1) for b in range(2)]
        piece_ready = signal("piece_ready", *PIECES)
        piece_hi = signal("piece_hi", *PIECES)
        piece_lo = signal("piece_lo", *PIECES, 2)
        sq_ready = signal("sq_ready", 44, 32)
        sq_used = signal("sq_used", 44, 32, 2)
        sq_summed = signal("sq_summed", 2, 2)
        out_summed = signal("out_summed", 2, 2)
        stat_free = signal("stat_free", 4, 4, 1)
        rstd_ready = signal("rstd_ready", 4, 4)
        rstd_used = signal("rstd_used", 4, 4, 2)
        x_ready = signal("x_ready", 16, 16, 8)
        par_loaded = signal("par_loaded", 16, 16)
        par_in = signal("par_in", 1, 1)
        gw_hi = signal("gw_hi", 1, 1)
        gw_lo = signal("gw_lo", 1, 1)
        gates_done = signal("gates_done", 1, 1)
        turned = signal("turned", 12, 17)
        turn_done = signal("turn_done", 12, 17, 2)
        sc_done = signal("sc_done", 32, 32)
        sc_read = signal("sc_read", 32, 32, 2)
        nmax = signal("nmax", 32, 32)
        prob = signal("prob", 32, 32)
        pt_done = signal("pt_done", 32, 32)
        pt_copied = signal("pt_copied", 32, 32)
        pv_done = signal("pv_done", 32, 32)
        oa_read = signal("oa_read", 32, 32)
        tro_done = signal("tro_done", 16, 16)
        conv_in = signal("conv_in", 12, 0)
        dn_act = signal("dn_act", 12, 0)
        l2_copied = signal("l2_copied", 8, 0)
        l2_rstd = signal("l2_rstd", 2, 0)
        l2_done = signal("l2_done", 2, 0)
        dn_rstd = signal("dn_rstd", 4, 0)
        gate_a = signal("gate_a", 1, 0)
        gate_b = signal("gate_b", 1, 0)
        g_ready = signal("g_ready", 1, 0)
        kd_in = signal("kd_in", 1, 0)
        kd_out = signal("kd_out", 1, 0)
        state_zero = signal("state_zero", 1, 0)
        d_done = signal("d_done", EVENTS, 0)
        d_free = [signal(f"d_free{b}", len(range(b, EVENTS, 3)), 0) for b in range(3)]
        gr_exp = signal("gr_exp", 4, 0)
        e_in = signal("e_in", 4, 0)
        e_ready = signal("e_ready", 4, 0)
        qdec_ready = signal("qdec_ready", 4, 0)
        xt_ready = signal("xt_ready", 4, 0)
        lt_ready = signal("lt_ready", 20, 0)
        glu_in = signal("glu_in", 2 * NJ, 0)
        gelu_done = signal("gelu_done", NJ, 0)
        ix_done = signal("ix_done", 0, 32)
        ix_relu = signal("ix_relu", 0, 32)
        ix_used = signal("ix_used", 0, 32, 2)
        cos_done = signal("cos_done", 0, 13)
        const_in = ctx.enter_context(nc.semaphore("const_in"))
        x_in = ctx.enter_context(nc.semaphore("x_in"))
        pos_in = ctx.enter_context(nc.semaphore("pos_in"))
        rope_sin_in = ctx.enter_context(nc.semaphore("rope_sin_in"))
        rope_ready = ctx.enter_context(nc.semaphore("rope_ready"))
        stored = ctx.enter_context(nc.semaphore("stored"))

        def heads(ap):
            return ap.rearrange("p (h c) -> p h c", c=P)

        def per_head(ap, n=P):
            return ap.unsqueeze(2).broadcast_to([P, HN, n])

        def over_heads(ap, h=HN):
            return ap.unsqueeze(1).broadcast_to([P, h, ap.shape[-1]])

        def gcol(a, b=None):
            return gv[:, a:a + 16 if b is None else b]

        BA, XA, AX, E1, EBV, SP_, BETA, G_, SM, KDI, KD_, EG, GLB, BG, EA = (
            0, 32, 48, 64, 80, 96, 112, 128, 144, 208, 224, 240, 256, 288, 304)

        def tile4(a, t):
            return gv[:, a + 4 * t:a + 4 * t + 4]

        ATT = ((qT1, kT1, v1, sc1, pt1, ao1, st1, 0, N_ATT1), (qT2, kT2, v2, sc2, pt2, ao2, st2, 4, N_ATT2))
        MX, NMX, SUM, RS = 0, 4, 8, 12

        def bias_of(b, i):
            if b == 0:
                return cst("count", S - P * (i + 1), S)
            o = P * (i * (i + 1) // 2)
            return bias2[:, o:o + P * (i + 1)]

        def att_step(n):
            return n // 8, n // 2 % 4, n % 2

        def xconv(c):
            return xb[c % 2][:, :, :].rearrange("p h c -> p (h c)")

        def turn_src(b, j):
            if b == 0:
                return mb[j % 2][:, :, :].rearrange("p h c -> p (h c)")
            return turn2[:, j % 2, :]

        def turn_dst(b, j):
            if b == 0:
                return (qT1, kT1)[j // 4][:, j % 4, :]
            if j == 0:
                return ikT[:, :]
            return (iqT, qT2, kT2)[(j - 1) // 4][:, (j - 1) % 4, :]

        def l2_stat(i):
            return (kdec, qkT)[i][:, :, :, :]

        def head_stat(h):
            return kdec[:, h, :, :].rearrange("p h c -> p (h c)")

        DSUM = bank[3:7]

        N_ROT = (8, 13)
        MT = (mT1, mT2)
        SQ_SUM = (sq_sum1, sq_sum2)

        block = ctx.enter_context(nc.Block())

        @block.sync
        def _(sp):
            sp.dma_start(const[:, :], d["const"]).then_inc(const_in, 16)
            sp.dma_start(x[:, :, :], d["x"]).then_inc(x_in, 16)

            def load(w, src, i2, s):
                sp.wait_ge(w_hi.sem, w_hi.at(w, 2 * i2 + s - 1))
                sp.wait_ge(w_lo.sem, w_lo.at(w, 2 * i2 + s - 1))
                sp.dma_start(raw[:, s, :], src).then_inc(loaded[s].sem, 16)

            for b in range(2):
                with sp.Fori(0, LAYERS) as L:
                    w = Where(b, L)
                    with sp.Fori(0, UNITS[b] // 2) as i:
                        for s in range(2):
                            load(w, d[f"w{b}"][L * UNITS[b] + i * 2 + s], i, s)
            for s in range(2):
                load(Where(1, LAYERS), d["w1"][s], 0, s)
            sp.wait_ge(x_ready.sem, x_ready.at(Where(1, LAYERS), 0))
            sp.dma_start(d["out"], x[:, :, :]).then_inc(stored, 16)
            sp.wait_ge(stored, 16)
            for s in range(2):
                sp.wait_ge(loaded[s].sem, loaded[s].at(Where(1, LAYERS), 16))
            sp.wait_ge(par_loaded.sem, par_loaded.at(Where(1, LAYERS), 16))

        @block.gpsimd
        def _(pool):
            for ring in (w_lo, piece_lo):
                pool.nop().then_inc(ring.sem, ring.credit)

            def w_low(w, i2, s):
                pool.wait_ge(w_hi.sem, w_hi.at(w, 2 * i2 + s + 1))
                pool.wait_ge(unit_done.sem, unit_done.at(w, 2 * i2 + s - 1))
                pool.tensor_tensor(wL[:, s, :], raw[:, s, :], wH[:, s, :].bitcast(F32),
                                   ALU.subtract).then_inc(w_lo.sem, 1)

            def next_low(w, i2, s):
                w_low(w, i2 + 1, s)

            def piece_low(w, n, s, dst, hi):
                pool.wait_ge(piece_hi.sem, piece_hi.at(w, n + 1))
                pool.tensor_tensor(dst, piece[:, s, :], hi.bitcast(F32), ALU.subtract).then_inc(piece_lo.sem, 1)

            def layer_params(w):
                pool.wait_ge(par_in.sem, par_in.at(w, 1))
                pool.dma_start(par_next[:, :], d["par"][w.L + (w.b * LAYERS + 1)]).then_inc(par_loaded.sem, 16)
                pool.wait_ge(gw_hi.sem, gw_hi.at(w, 1))
                pool.tensor_tensor(gwL[:, :], prm(w, "gates", 0, KD * 8), gwH[:, :].bitcast(F32),
                                   ALU.subtract).then_inc(gw_lo.sem, 1)

            def level(w, t, l):
                pool.tensor_tensor(eb[t % 2][:, :, :], ab[t % 2][:, :, :],
                                   over_heads(cst("level", l * P, l * P + P)), ALU.mult).then_inc(lt_ready.sem, 1)

            def norm_pieces(w, n0):
                for k in range(KD):
                    piece_low(w, n0 + k, (n0 + k) % 2, hL[:, k, :], hH[:, k, :])

            pool.dma_start(par_next[:, :], d["par"][0]).then_inc(par_loaded.sem, 16)
            for s in range(2):
                w_low(Where(0, 0), 0, s)
            with pool.Fori(0, LAYERS) as L:
                w = Where(0, L)
                layer_params(w)
                norm_pieces(w, N_H1)
                for u in range(28):
                    next_low(w, u // 2, u % 2)
                for kind, a, k in ORDER:
                    if kind == "att" and a % 8 == 2 and a >= 10:
                        f = (a - 10) // 8
                        piece_low(w, N_ATT1 + f, f % 2, hL[:, f, :], hH[:, f, :])
                    if kind == "pre" and k == 4:
                        for t in (2 * a, 2 * a + 1):
                            pool.wait_ge(xt_ready.sem, xt_ready.at(w, t + 1))
                            level(w, t, 1)
                    if kind == "pre" and k in (5, 8, 11, 14):
                        l = (k - 5) // 3 + 1
                        for t in (2 * a, 2 * a + 1):
                            pool.wait_ge(d_done.sem, d_done.at(w, ev_pre(t, k) + 1))
                            level(w, t, l + 1)
                for h in range(HN):
                    piece_low(w, N_DN1 + h, h % 2, hL[:, 4 + h, :], hH[:, 4 + h, :])
                with pool.Fori(0, 4) as i:
                    for s in range(2):
                        next_low(w, 14 + i, s)
                norm_pieces(w, N_HF1)
                with pool.Fori(0, NJ // 2) as i:
                    for q in range(2):
                        for s in range(2):
                            next_low(w, 18 + i * 2 + q, s)
                        piece_low(w, N_HID1 + i * 2 + q, q, hidL1[:, bass.ds(i * 2 + q, 1), :],
                                  hidH1[:, bass.ds(i * 2 + q, 1), :])
                with pool.Fori(0, 12) as i:
                    for s in range(2):
                        next_low(w, 40 + i, s)

            w = Where(1, 0)
            pool.wait_ge(x_ready.sem, x_ready.at(w, 0))
            pool.dma_start(posi[:, :], d["pos"].partition_broadcast(P)).then_inc(pos_in, 16)
            with pool.Fori(0, LAYERS) as L:
                w = Where(1, L)
                layer_params(w)
                norm_pieces(w, N_H2)
                for u in range(21):
                    next_low(w, u // 2, u % 2)
                    if u < N_ROT[1]:
                        pool.wait_ge(acc_free[u % 2].sem, acc_free[u % 2].at(w, u // 2 + 1))
                        pool.wait_ge(turn_done.sem, turn_done.at(w, u - 1))
                        pool.tensor_tensor(pt2[:, u % 2, :], turn_src(1, u), rope2[:, 0, :],
                                           ALU.mult).then_inc(cos_done.sem, 1)
                    if u > 17:
                        piece_low(w, N_PD2 + u - 18, u % 2, pdL[:, u - 18, :], pdH[:, u - 18, :])
                piece_low(w, N_PD2 + 3, 1, pdL[:, 3, :], pdH[:, 3, :])
                for g in range(4):
                    if g != 1:
                        u = (21, 21, 22, 23)[g]
                        next_low(w, u // 2, u % 2)
                    piece_low(w, N_PY2 + g, g % 2, hL[:, g, :], hH[:, g, :])
                for f in range(4):
                    piece_low(w, N_ATT2 + f, f % 2, hL[:, 4 + f, :], hH[:, 4 + f, :])
                with pool.Fori(0, 4) as i:
                    for s in range(2):
                        next_low(w, 12 + i, s)
                norm_pieces(w, N_HF2)
                for c in range(FCHUNKS):
                    with pool.Fori(0, HCH // 2) as i:
                        for s in range(2):
                            next_low(w, 16 + 16 * c + i, s)
                            piece_low(w, N_HID2 + HCH * c + i * 2 + s, s, hidL2[:, bass.ds(i * 2 + s, 1), :],
                                      hidH2[:, bass.ds(i * 2 + s, 1), :])
                    with pool.Fori(0, KD) as i:
                        for s in range(2):
                            next_low(w, 24 + 16 * c + i, s)

        @block.scalar
        def _(act):
            for ring in (w_hi, unit_done, *acc_free, sq_used, stat_free, rstd_used, sc_read, turn_done, ix_used):
                act.nop().then_inc(ring.sem, ring.credit)
            act.wait_ge(const_in, 16)

            def w_high(w, i2, s):
                act.wait_ge(loaded[s].sem, loaded[s].at(w, 16 * (i2 + 1)))
                act.wait_ge(unit_done.sem, unit_done.at(w, 2 * i2 + s - 1))
                act.activation(wH[:, s, :], raw[:, s, :], ACT.Copy).then_inc(w_hi.sem, 1)

            def next_high(w, i2, s):
                w_high(w, i2 + 1, s)

            def use_table(name):
                act.preload_act_table_set(name)

            def unit_wait(w, i2, s):
                act.wait_ge(unit_done.sem, unit_done.at(w, 2 * i2 + s + 1))

            def piece_high(w, n, s, dst):
                act.wait_ge(piece_ready.sem, piece_ready.at(w, n + 1))
                act.activation(dst, piece[:, s, :], ACT.Copy).then_inc(piece_hi.sem, 1)

            def square(w, r, s, src):
                act.wait_ge(sq_used.sem, sq_used.at(w, r - 1))
                act.activation(sq[:, s, :], src, ACT.Square).then_inc(sq_ready.sem, 1)

            def inverse_root(w, summed, v):
                act.wait_ge(*summed)
                act.wait_ge(rstd_used.sem, rstd_used.at(w, v - 1))
                act.activation(rstd[:, v % 2, :], STAT[:, :], ACT.Ln, bias=cst("eps"),
                               scale=1.0 / D).then_inc(stat_free.sem, 1)
                act.drain()
                act.activation(rstd[:, v % 2, :], rstd[:, v % 2, :], ACT.Exp,
                               scale=-0.5).then_inc(rstd_ready.sem, 1)

            def output_root(w, k, v):
                inverse_root(w, (out_summed.sem, out_summed.at(w, k + 1)), v)

            def norm(w, r0, v, n0, x0):
                for k in range(KD):
                    act.wait_ge(x_ready.sem, x_ready.at(w, x0 + k + 1))
                    square(w, r0 + k, k % 2, x[:, k, :])
                if v == 0:
                    act.wait_ge(par_loaded.sem, par_loaded.at(w, 16))
                    act.activation(par[:, :], par_next[:, :], ACT.Copy).then_inc(par_in.sem, 1)
                inverse_root(w, (sq_used.sem, sq_used.at(w, r0 + KD)), v)
                if v == 0:
                    narrow_gates(w)
                for k in range(KD):
                    piece_high(w, n0 + k, (n0 + k) % 2, hH[:, k, :])

            def narrow_gates(w):
                act.wait_ge(par_in.sem, par_in.at(w, 1))
                act.activation(gwH[:, :], prm(w, "gates", 0, KD * 8), ACT.Copy).then_inc(gw_hi.sem, 1)

            def turn_input(w, j, i2, s, bank_i, a2, scale):
                unit_wait(w, i2, s)
                act.wait_ge(turn_done.sem, turn_done.at(w, j - 1))
                act.activation(turn_src(w.b, j), ACC[bank_i][:, :], ACT.Copy,
                               scale=scale).then_inc(acc_free[bank_i].sem, 1)

            def attention(w, n):
                q, k, v, sc, pt, ao, st, _, _ = ATT[w.b]
                if n < 32:
                    act.wait_ge(nmax.sem, nmax.at(w, n + 1))
                    wd = P * (att_step(n)[1] + 1)
                    act.activation(sc[:, n % 2, 0:wd], sc[:, n % 2, 0:wd], ACT.Exp,
                                   bias=st[:, NMX + n % 4:NMX + n % 4 + 1],
                                   accum_out=st[:, SUM + n % 4:SUM + n % 4 + 1]).then_inc(prob.sem, 1)
                m = n - 1
                if 0 <= m < 32:
                    act.wait_ge(pt_done.sem, pt_done.at(w, m + 1))
                    if m >= 2:
                        act.wait_ge(pv_done.sem, pv_done.at(w, m - 1))
                    wd = P * (att_step(m)[1] + 1)
                    act.activation(pt[:, m % 2, 0:wd], PT[:, 0:wd], ACT.Copy).then_inc(pt_copied.sem, 1)
                if n % 8 == 2 and n >= 10:
                    f = (n - 10) // 8
                    piece_high(w, ATT[w.b][8] + f, f % 2, hH[:, ATT[w.b][7] + f, :])

            def out_unit(w, i, s, j2, r, a2, bank_i):
                unit_wait(w, j2, s)
                square(w, r, s, ACC[bank_i][:, :])
                act.activation(MT[w.b][:, bass.ds(i, 1), :], ACC[bank_i][:, :], ACT.Copy)
                act.drain().then_inc(acc_free[bank_i].sem, 1)
                next_high(w, j2, s)

            def gate_functions(w):
                act.wait_ge(gate_a.sem, gate_a.at(w, 1))
                act.activation(gcol(E1, E1 + 16), gcol(AX, AX + 16), ACT.Exp, scale=-1.0)
                act.activation(gv[:, EBV:EBV + 16].rearrange("p (t h) -> p t h", h=4),
                               gv[:, BA:BA + 32].rearrange("p (t c) -> p t c", c=8)[:, :, 0:4], ACT.Exp, scale=-1.0)
                act.activation(gcol(EA, EA + 4), prm(w, "alog", 0, 4), ACT.Exp)
                act.drain()
                act.activation(gcol(SP_, SP_ + 16), gcol(E1, E1 + 16), ACT.Ln, bias=cst("one"))
                act.drain().then_inc(gate_b.sem, 1)

            use_table("natural_log")
            for s in range(2):
                w_high(Where(0, 0), 0, s)
            act.wait_ge(x_in, 16)
            act.nop().then_inc(x_ready.sem, 8)
            with act.Fori(0, LAYERS) as L:
                w = Where(0, L)
                norm(w, 0, 0, N_H1, -KD)
                for u in range(28):
                    if u == 12:
                        use_table("silu_and_others")
                    if u < 12:
                        turn_input(w, u, u // 2, u % 2, u % 2, u // 2, HD ** -0.5 if u < 4 else 1.0)
                    elif u < 24:
                        c = u - 12
                        if c >= 2:
                            act.wait_ge(dn_act.sem, dn_act.at(w, c - 1))
                        unit_wait(w, u // 2, u % 2)
                        act.activation(xconv(c), ACC[u % 2][:, :], ACT.Copy,
                                       scale=prm(w, "dconv", 4 * c + 3, 4 * c + 4)).then_inc(conv_in.sem, 1)
                    else:
                        unit_wait(w, u // 2, u % 2)
                        act.activation(zT[:, u - 24, :], ACC[u % 2][:, :], ACT.Copy).then_inc(acc_free[u % 2].sem, 1)
                    next_high(w, u // 2, u % 2)
                    if 13 <= u < 25:
                        c = u - 13
                        act.wait_ge(acc_free[(u - 1) % 2].sem, acc_free[(u - 1) % 2].at(w, (u - 1) // 2 + 1))
                        act.activation((dq, dk, dv)[c // 4][:, c % 4, :], xconv(c), ACT.Silu).then_inc(dn_act.sem, 1)
                        if c < 8:
                            act.wait_ge(dn_act.sem, dn_act.at(w, c + 1))
                            square(w, 8 + c, c % 2, (dq, dk)[c // 4][:, c % 4, :])
                    if u == 5:
                        gate_functions(w)
                    if u in (24, 25):
                        if u == 24:
                            use_table("natural_log")
                        act.wait_ge(l2_copied.sem, l2_copied.at(w, 4 * (u - 23)))
                        act.activation(l2_stat(u - 24), l2_stat(u - 24), ACT.Ln, bias=cst("eps"))
                    if u in (26, 27):
                        if u == 26:
                            act.drain()
                            use_table("exp_and_others")
                        act.activation(l2_stat(u - 26), l2_stat(u - 26), ACT.Exp,
                                       bias=cst("qscale") if u == 26 else 0.0, scale=-0.5).then_inc(l2_rstd.sem, 1)
                for kind, a, k in ORDER:
                    if kind == "att":
                        attention(w, a)
                    elif kind == "small":
                        act.wait_ge(kd_in.sem, kd_in.at(w, 1))
                        act.activation(gcol(KD_, KD_ + 16), gcol(KDI, KDI + 16), ACT.Exp)
                        act.activation(gcol(EG, EG + 16), gcol(SM, SM + 16), ACT.Exp)
                        act.activation(gcol(GLB, GLB + 32), gcol(SM + 32, SM + 64), ACT.Exp)
                        act.drain().then_inc(kd_out.sem, 1)
                    elif kind == "pre":
                        for t in (2 * a, 2 * a + 1):
                            e = ev_pre(t, k)
                            free = d_free[e % 3]
                            if k in (0, 4, 5, 8, 11, 14, 17, 21, 22):
                                act.wait_ge(d_done.sem, d_done.at(w, e + 1))
                            if k == 0:
                                act.activation(xtb[t % 2][:, :, :], heads(DB[e % 3][:, :]), ACT.Exp).then_inc(gr_exp.sem, 1)
                                act.wait_ge(e_in.sem, e_in.at(w, t + 1))
                                act.activation(eb[t % 2][:, :, :], eb[t % 2][:, :, :], ACT.Exp).then_inc(e_ready.sem, 1)
                            elif k == 4:
                                act.activation(xb[t % 2][:, :, :], heads(DB[e % 3][:, :]), ACT.Copy).then_inc(free.sem, 1)
                            elif k in (5, 8, 11, 14, 17):
                                act.activation(mb[t % 2][:, :, :], heads(DB[e % 3][:, :]), ACT.Copy).then_inc(free.sem, 1)
                            elif k == 21:
                                act.activation(dv[:, :, t * P:t * P + P], heads(DB[e % 3][:, :]), ACT.Copy).then_inc(free.sem, 1)
                            elif k == 22:
                                act.activation(dk[:, :, t * P:t * P + P], heads(DB[e % 3][:, :]), ACT.Copy).then_inc(free.sem, 1)
                    elif kind == "scan":
                        e = ev_scan(a, 1)
                        act.wait_ge(d_done.sem, d_done.at(w, e + 1))
                        act.activation(dq[:, :, a * CH:a * CH + CH],
                                       DB[e % 3][:, 0:HN * CH].rearrange("p (h c) -> p h c", c=CH),
                                       ACT.Copy).then_inc(d_free[e % 3].sem, 1)
                act.drain()
                for h in range(HN):
                    square(w, 16 + h, h % 2, dq[:, h, :])
                use_table("silu_and_others")
                act.activation(zT[:, :, :], zT[:, :, :], ACT.Silu)
                use_table("natural_log")
                for h in range(HN):
                    act.wait_ge(sq_used.sem, sq_used.at(w, 16 + h + 1))
                    act.activation(head_stat(h), DSUM[h][:, :], ACT.Ln, bias=cst("eps"), scale=1.0 / P)
                act.drain()
                use_table("exp_and_others")
                for h in range(HN):
                    act.activation(head_stat(h), head_stat(h), ACT.Exp, scale=-0.5).then_inc(dn_rstd.sem, 1)
                for h in range(HN):
                    piece_high(w, N_DN1 + h, h % 2, hH[:, 4 + h, :])
                use_table("natural_log")
                with act.Fori(0, 4) as i:
                    for s in range(2):
                        out_unit(w, i * 2 + s, s, i + 14, i * 2 + 20 + s, i + 14, s)
                output_root(w, 0, 1)
                use_table("natural_log")
                norm(w, 28, 2, N_HF1, 0)
                use_table("gelu_apprx_tanh_and_others")
                with act.Fori(0, NJ // 2) as i:
                    for q in range(2):
                        i2 = i * 2 + q + 18
                        for s in range(2):
                            unit_wait(w, i2, s)
                            act.activation(mT1[:, 2 * q + s, :], ACC[s][:, :], ACT.Identity,
                                           bias=prmd(w, "fbias", i * 4 + 2 * q + s),
                                           scale=prmd(w, "fconv", i * 12 + 6 * q + 3 * s + 2)).then_inc(glu_in.sem, 1)
                            next_high(w, i2, s)
                            if s == 0:
                                act.wait_ge(acc_free[0].sem, acc_free[0].at(w, i2 + 1))
                                act.activation(mT1[:, 2 * q, :], mT1[:, 2 * q, :],
                                               ACT.Gelu_apprx_tanh).then_inc(gelu_done.sem, 1)
                        piece_high(w, N_HID1 + i * 2 + q, q, hidH1[:, bass.ds(i * 2 + q, 1), :])
                use_table("natural_log")
                with act.Fori(0, 4) as i:
                    for m in range(2):
                        for u in range(2):
                            y = 3 * m + u
                            next_high(w, i * 3 + 40 + y // 2, y % 2)
                        y = 3 * m + 2
                        unit_wait(w, i * 3 + 40 + y // 2, y % 2)
                        square(w, i * 2 + 36 + m, m, ACC[m][:, :])
                        act.activation(mT1[:, bass.ds(i * 2 + m, 1), :], ACC[m][:, :], ACT.Copy)
                        act.drain().then_inc(acc_free[m].sem, 1)
                        next_high(w, i * 3 + 40 + y // 2, y % 2)
                output_root(w, 1, 3)
                use_table("natural_log")

            act.wait_ge(rope_sin_in, 1)
            act.activation(rope2[:, 1, :], ang[:, 2, :], ACT.Sin)
            act.activation(rope2[:, 0, :], ang[:, 3, :], ACT.Sin, bias=cst("halfpi"), scale=-1.0)
            act.drain().then_inc(rope_ready, 1)
            use_table("natural_log")
            with act.Fori(0, LAYERS) as L:
                w = Where(1, L)
                norm(w, 0, 0, N_H2, -KD)
                for u in range(21):
                    for y in IX_AT.get(u, ()):
                        wd = P * (y // 8 + 1)
                        act.wait_ge(ix_done.sem, ix_done.at(w, y + 1))
                        act.wait_ge(ix_used.sem, ix_used.at(w, y - 1))
                        act.activation(ir[:, y % 2, 0:wd], (PT, OA)[y % 2][:, 0:wd], ACT.Relu,
                                       scale=HD ** -0.5).then_inc(ix_relu.sem, 1)
                    if u < 17:
                        turn_input(w, u, u // 2, u % 2, u % 2, u // 2, HD ** -0.5 if 5 <= u < 9 else 1.0)
                    elif u < 21:
                        g = u - 17
                        unit_wait(w, u // 2, u % 2)
                        if g >= 2:
                            act.wait_ge(piece_ready.sem, piece_ready.at(w, N_PD2 + g - 1))
                        act.activation(pu[:, g % 2, :], ACC[u % 2][:, :], ACT.Copy).then_inc(acc_free[u % 2].sem, 1)
                    next_high(w, u // 2, u % 2)
                    if u > 17:
                        piece_high(w, N_PD2 + u - 18, u % 2, pdH[:, u - 18, :])
                piece_high(w, N_PD2 + 3, 1, pdH[:, 3, :])
                for g in range(4):
                    if g != 1:
                        u = (21, 21, 22, 23)[g]
                        next_high(w, u // 2, u % 2)
                    piece_high(w, N_PY2 + g, g % 2, hH[:, g, :])
                use_table("exp_and_others")
                for n in range(SLOTS):
                    attention(w, n)
                use_table("natural_log")
                with act.Fori(0, 4) as i:
                    for s in range(2):
                        out_unit(w, i * 2 + s, s, i + 12, i * 2 + 8 + s, i + 12, (25 + s) % 2)
                output_root(w, 0, 1)
                use_table("natural_log")
                norm(w, 16, 2, N_HF2, 0)
                for c in range(FCHUNKS):
                    with act.Fori(0, HCH // 2) as i:
                        for s in range(2):
                            bk = (33 + s) % 2
                            unit_wait(w, i + 16 + 16 * c, s)
                            act.activation(relu[:, s, :], ACC[bk][:, :], ACT.Relu).then_inc(acc_free[bk].sem, 1)
                            next_high(w, i + 16 + 16 * c, s)
                            piece_high(w, N_HID2 + HCH * c + i * 2 + s, s, hidH2[:, bass.ds(i * 2 + s, 1), :])
                    with act.Fori(0, KD // 2) as i:
                        for m in range(2):
                            bk = (49 + m) % 2
                            next_high(w, i * 2 + 24 + 16 * c + m, 0)
                            unit_wait(w, i * 2 + 24 + 16 * c + m, 1)
                            if c == 0:
                                act.activation(mT2[:, bass.ds(i * 2 + m, 1), :], ACC[bk][:, :],
                                               ACT.Copy).then_inc(acc_free[bk].sem, 1)
                            else:
                                act.wait_ge(acc_free[bk].sem, acc_free[bk].at(w, i + 12 * c + 24 + m + 1))
                                square(w, i * 2 + 24 + m, m, mT2[:, bass.ds(i * 2 + m, 1), :])
                            next_high(w, i * 2 + 24 + 16 * c + m, 1)
                output_root(w, 1, 3)
                use_table("natural_log")

        @block.vector
        def _(dve):
            dve.wait_ge(const_in, 16)

            def new_piece(w, n):
                dve.wait_ge(piece_lo.sem, piece_lo.at(w, n - 1))

            def release_rstd():
                dve.drain().then_inc(rstd_used.sem, 1)

            def norm(w, v, n0, name):
                if v == 0:
                    dve.wait_ge(par_in.sem, par_in.at(w, 1))
                dve.wait_ge(rstd_ready.sem, rstd_ready.at(w, v + 1))
                for k in range(KD):
                    new_piece(w, n0 + k)
                    dve.scalar_tensor_tensor(piece[:, k % 2, :], x[:, k, :], prm(w, name, k, k + 1),
                                             rstd[:, v % 2, :], ALU.mult, ALU.mult).then_inc(piece_ready.sem, 1)
                release_rstd()

            def sum_output(w, k, r0, of_bank=None):
                dve.memset(SQ_SUM[w.b][:, :], 0.0)
                dve.drain()
                with dve.Fori(0, KD // 2) as i:
                    for m in range(2):
                        if of_bank:
                            of_bank(i, m)
                        dve.wait_ge(sq_ready.sem, sq_ready.at(w, i * 2 + r0 + m + 1))
                        dve.tensor_tensor(SQ_SUM[w.b][:, :], SQ_SUM[w.b][:, :], sq[:, m, :], ALU.add).then_inc(sq_used.sem, 1)
                        dve.drain()
                dve.drain().then_inc(sq_summed.sem, 1)

            def residual(w, v, name):
                m = MT[w.b]
                dve.wait_ge(rstd_ready.sem, rstd_ready.at(w, v + 1))

                def scaled(k):
                    dve.scalar_tensor_tensor(m[:, k, :], m[:, k, :], prm(w, name, k, k + 1),
                                             rstd[:, v % 2, :], ALU.mult, ALU.mult)

                scaled(0)
                dve.drain()
                for k in range(KD):
                    dve.tensor_tensor(x[:, k, :], x[:, k, :], m[:, k, :], ALU.add).then_inc(x_ready.sem, 1)
                    if k + 1 < KD:
                        scaled(k + 1)
                        dve.drain()
                release_rstd()

            def turn_finish(w, j):
                t1, t2 = ATT[w.b][3][:, 0, :], ATT[w.b][3][:, 1, :]
                cos, sin = (rope2[:, 0, :], rope2[:, 1, :]) if w.b else (cst("cos1"), cst("sin1"))
                dve.wait_ge(turned.sem, turned.at(w, j + 1))
                if j < N_ROT[w.b]:
                    if w.b:
                        t2 = pt2[:, j % 2, :]
                        dve.wait_ge(cos_done.sem, cos_done.at(w, j + 1))
                    dve.tensor_tensor(t1, SC[j % 2][:, :], sin, ALU.mult)
                    if w.b == 0:
                        dve.tensor_tensor(t2, turn_src(w.b, j), cos, ALU.mult)
                    dve.drain()
                    dve.tensor_tensor(turn_dst(w.b, j), t1, t2, ALU.add).then_inc(turn_done.sem, 1)
                    dve.drain()
                else:
                    f = j - N_ROT[w.b]
                    dve.tensor_copy(ATT[w.b][2][:, :, f * P:f * P + P], heads(SC[j % 2][:, :])).then_inc(turn_done.sem, 1)

            def attention(w, n):
                q, k, v, sc, pt, ao, st, _, n0 = ATT[w.b]
                if n < 32:
                    wd = P * (att_step(n)[1] + 1)
                    c = n % 4
                    dve.wait_ge(sc_done.sem, sc_done.at(w, n + 1))
                    if n >= 2:
                        dve.wait_ge(pt_done.sem, pt_done.at(w, n - 1))
                    dve.memset(st[:, 16:17], 0.0)
                    dve.tensor_tensor_reduce(sc[:, n % 2, 0:wd], SC[n % 2][:, 0:wd], bias_of(w.b, att_step(n)[1]),
                                             1.0, NEG, ALU.add, ALU.max,
                                             st[:, MX + c:MX + c + 1]).then_inc(sc_read.sem, 1)
                    dve.drain()
                    dve.tensor_scalar(st[:, NMX + c:NMX + c + 1], st[:, MX + c:MX + c + 1], -1.0, None,
                                      ALU.mult).then_inc(nmax.sem, 1)
                m = n - 2
                if 0 <= m < 32:
                    c, p = m % 4, m // 2
                    dve.wait_ge(pv_done.sem, pv_done.at(w, m + 1))
                    dve.reciprocal(st[:, RS + c:RS + c + 1], st[:, SUM + c:SUM + c + 1])
                    dve.drain()
                    if p >= 2:
                        dve.wait_ge(tro_done.sem, tro_done.at(w, p - 1))
                    dve.tensor_scalar(ao[:, p % 2, m % 2 * HD:m % 2 * HD + HD], OA[:, 0:HD],
                                      st[:, RS + c:RS + c + 1], None, ALU.mult).then_inc(oa_read.sem, 1)
                if n % 8 == 2 and n >= 10:
                    f = (n - 10) // 8
                    dve.wait_ge(tro_done.sem, tro_done.at(w, 4 * f + 4))
                    new_piece(w, n0 + f)
                    dve.tensor_copy(piece[:, f % 2, :], TRO[:, :]).then_inc(piece_ready.sem, 1)

            def convolve(w, c):
                u = c + 12
                dve.wait_ge(conv_in.sem, conv_in.at(w, c + 1))
                for lag in (1, 2, 3):
                    last = dve.scalar_tensor_tensor(xconv(c)[:, lag:S], ACC[u % 2][:, 0:S - lag],
                                                    prm(w, "dconv", 4 * c + 3 - lag, 4 * c + 4 - lag),
                                                    xconv(c)[:, lag:S], ALU.mult, ALU.add)
                    if lag < 3:
                        dve.drain()
                last.then_inc(acc_free[u % 2].sem, 1)

            def by_head(ap):
                return ap.rearrange("p (t h) -> p t h", h=4)

            def delta_gates(w):
                ba = gv[:, BA:BA + 32].rearrange("p (t c) -> p t c", c=8)

                dve.wait_ge(gates_done.sem, gates_done.at(w, 1))
                dve.tensor_copy(gv[:, BA:BA + 32], TRO[:, 0:32])
                dve.drain()
                dve.tensor_tensor(by_head(gcol(XA, XA + 16)), ba[:, :, 4:8],
                                  over_heads(prm(w, "dt", 0, 4)), ALU.add)
                dve.drain()
                dve.tensor_scalar(gcol(AX, AX + 16), gcol(XA, XA + 16), -1.0, None, ALU.mult)
                dve.drain()
                dve.tensor_tensor(gcol(AX, AX + 16), gcol(AX, AX + 16), gcol(XA, XA + 16), ALU.max)
                dve.drain().then_inc(gate_a.sem, 1)
                dve.tensor_scalar(gcol(XA, XA + 16), gcol(XA, XA + 16), 0.0, None, ALU.max)

            def delta_gates_end(w):
                dve.wait_ge(gate_b.sem, gate_b.at(w, 1))
                dve.tensor_scalar(gcol(EBV, EBV + 16), gcol(EBV, EBV + 16), 1.0, None, ALU.add)
                dve.drain()
                dve.reciprocal(gcol(BETA, BETA + 16), gcol(EBV, EBV + 16))
                dve.tensor_tensor(gcol(G_, G_ + 16), gcol(SP_, SP_ + 16), gcol(XA, XA + 16), ALU.add)
                dve.drain()
                dve.tensor_tensor(by_head(gcol(G_, G_ + 16)), by_head(gcol(G_, G_ + 16)),
                                  over_heads(gcol(EA, EA + 4)), ALU.mult)
                dve.drain()
                dve.tensor_scalar(gcol(G_, G_ + 16), gcol(G_, G_ + 16), -1.0, None, ALU.mult)
                dve.drain().then_inc(g_ready.sem, 1)

            def delta_small(w):
                dve.wait_ge(d_done.sem, d_done.at(w, 1))
                dve.tensor_copy(gcol(SM, SM + 64), DB[0][:, 0:64]).then_inc(d_free[0].sem, 1)
                dve.drain()
                dve.tensor_tensor(gcol(KDI, KDI + 16), gcol(SM + 16, SM + 32), gcol(SM, SM + 16), ALU.subtract)
                dve.drain().then_inc(kd_in.sem, 1)
                dve.wait_ge(kd_out.sem, kd_out.at(w, 1))
                dve.tensor_tensor(gcol(BG, BG + 16), gcol(BETA, BETA + 16), gcol(EG, EG + 16), ALU.mult)
                dve.drain()

            def delta_pre(w, t, k):
                e = ev_pre(t, k)
                psum, free = heads(DB[e % 3][:, :]), d_free[e % 3].sem
                E, A, X, XT = (r[t % 2][:, :, :] for r in (eb, ab, xb, xtb))
                if k in (4, 5, 8, 11, 14, 17, 21, 22):
                    return
                if k > 4 or k == 2:
                    dve.drain()
                dve.wait_ge(d_done.sem, d_done.at(w, e + 1))
                if k == 0:
                    dve.wait_ge(gr_exp.sem, gr_exp.at(w, t + 1))
                    dve.tensor_tensor(E, psum, over_heads(cst("causal")), ALU.add).then_inc(free, 1)
                    dve.drain()
                    dve.tensor_tensor(E, E, per_head(tile4(SM, t)), ALU.subtract).then_inc(e_in.sem, 1)
                elif k == 1:
                    dve.wait_ge(e_ready.sem, e_ready.at(w, t + 1))
                    dve.tensor_tensor(A, psum, E, ALU.mult).then_inc(free, 1)
                elif k == 2:
                    dve.tensor_tensor(A, psum, A, ALU.mult).then_inc(free, 1)
                elif k == 3:
                    dve.tensor_tensor(qkT[:, t, :, :], psum, E, ALU.mult).then_inc(free, 1)
                    dve.tensor_tensor(dq[:, :, t * P:t * P + P], dq[:, :, t * P:t * P + P], XT,
                                      ALU.mult).then_inc(qdec_ready.sem, 1)
                    dve.drain()
                    dve.tensor_tensor(E, A, over_heads(cst("level", 0, P)), ALU.mult)
                    dve.drain()
                    dve.tensor_tensor(XT, over_heads(cst("ident")), E, ALU.subtract).then_inc(xt_ready.sem, 1)
                elif k in (6, 9, 12, 15):
                    dve.tensor_tensor(X, X, psum, ALU.subtract).then_inc(free, 1)
                elif k in (7, 10, 13, 16, 18):
                    dve.tensor_tensor(XT, XT, psum, ALU.subtract).then_inc(free, 1)
                elif k == 19:
                    dve.tensor_tensor(kdec[:, t, :, :], psum, per_head(tile4(KD_, t)), ALU.mult)
                    dve.tensor_tensor(A, psum, per_head(tile4(BG, t)), ALU.mult)
                    dve.drain().then_inc(free, 1)
                elif k == 20:
                    dve.tensor_tensor(E, psum, per_head(tile4(BETA, t)), ALU.mult).then_inc(free, 1)

            def delta_scan(w, c):
                t, p0 = c // 2, c % 2 * CH
                e = ev_scan(c, 0)
                dve.wait_ge(d_done.sem, d_done.at(w, e + 1))
                dve.tensor_tensor(vn[p0:p0 + CH, :, :], dv[p0:p0 + CH, :, t * P:t * P + P],
                                  DB[e % 3][p0:p0 + CH, :].rearrange("p (h c) -> p h c", c=P),
                                  ALU.subtract).then_inc(d_free[e % 3].sem, 1)
                e = ev_scan(c, 2)
                dve.wait_ge(d_done.sem, d_done.at(w, e + 1))
                for h in range(HN):
                    a = GLB + 16 * (c % 2) + 4 * t + h
                    dve.scalar_tensor_tensor(state[:, h, :], state[:, h, :], gv[:, a:a + 1],
                                             DB[e % 3][:, h * P:h * P + P], ALU.mult, ALU.add)
                dve.drain().then_inc(d_free[e % 3].sem, 1)

            def delta_out(w, h):
                dve.wait_ge(dn_rstd.sem, dn_rstd.at(w, h + 1))
                new_piece(w, N_DN1 + h)
                dve.scalar_tensor_tensor(piece[:, h % 2, :], dq[:, h, :], prm(w, "dnorm", 0, 1),
                                         head_stat(h), ALU.mult, ALU.mult)
                dve.drain()
                dve.tensor_tensor(piece[:, h % 2, :], piece[:, h % 2, :], zT[:, h, :],
                                  ALU.mult).then_inc(piece_ready.sem, 1)

            with dve.Fori(0, LAYERS) as L:
                w = Where(0, L)
                norm(w, 0, N_H1, "pre")
                dve.memset(state[:, :, :], 0.0).then_inc(state_zero.sem, 1)
                for u in range(24):
                    if u < 12:
                        turn_finish(w, u)
                    if 15 <= u < 23:
                        c = u - 15
                        dve.wait_ge(sq_used.sem, sq_used.at(w, 8 + c + 1))
                        dve.tensor_copy(l2_stat(c // 4)[:, c % 4, :, :], heads(STAT[:, :])).then_inc(l2_copied.sem, 1)
                    if u >= 12:
                        convolve(w, u - 12)
                    if u == 4:
                        delta_gates(w)
                    if u == 6:
                        delta_gates_end(w)
                for i in range(2):
                    tile = (dq, dk)[i][:, :, :]
                    dve.wait_ge(l2_rstd.sem, l2_rstd.at(w, i + 1))
                    dve.tensor_tensor(tile, tile, l2_stat(i).rearrange("p t h c -> p t (h c)"),
                                      ALU.mult).then_inc(l2_done.sem, 1)
                dve.drain()
                for kind, a, k in ORDER:
                    if kind == "att":
                        attention(w, a)
                    elif kind == "small":
                        delta_small(w)
                    elif kind == "pre":
                        delta_pre(w, 2 * a, k)
                        delta_pre(w, 2 * a + 1, k)
                    else:
                        delta_scan(w, a)
                for h in range(HN):
                    delta_out(w, h)
                sum_output(w, 0, 20)
                residual(w, 1, "post")
                norm(w, 2, N_HF1, "preff")
                with dve.Fori(0, NJ // 2) as i:
                    for q in range(2):
                        for s in range(2):
                            buf = mT1[:, 2 * q + s, :]
                            dve.wait_ge(glu_in.sem, glu_in.at(w, i * 4 + 2 * q + s + 1))
                            for lag in (1, 2):
                                last = dve.scalar_tensor_tensor(
                                    buf[:, lag:S], ACC[s][:, 0:S - lag],
                                    prmd(w, "fconv", i * 12 + 6 * q + 3 * s + 2 - lag), buf[:, lag:S],
                                    ALU.mult, ALU.add)
                                if lag == 1:
                                    dve.drain()
                            last.then_inc(acc_free[s].sem, 1)
                        dve.drain()
                        dve.wait_ge(gelu_done.sem, gelu_done.at(w, i * 2 + q + 1))
                        new_piece(w, i * 2 + N_HID1 + q)
                        dve.tensor_tensor(piece[:, q, :], mT1[:, 2 * q, :], mT1[:, 2 * q + 1, :],
                                          ALU.mult).then_inc(piece_ready.sem, 1)
                sum_output(w, 1, 36)
                residual(w, 3, "postff")

            R, N, T, A = (ang[:, i, :] for i in (2, 1, 0, 3))
            dve.wait_ge(pos_in, 16)
            dve.tensor_copy(T, posi[:, :])
            dve.drain()
            dve.tensor_scalar(T, T, cst("invf"), None, ALU.mult)
            dve.drain()
            dve.tensor_scalar(N, T, 1.0 / (2 * math.pi), None, ALU.mult)
            dve.drain()
            dve.tensor_scalar(N, N, 12582912.0, None, ALU.add)
            dve.drain()
            dve.tensor_scalar(N, N, -12582912.0, None, ALU.add)
            dve.drain()
            for part in TWO_PI:
                dve.scalar_tensor_tensor(T, N, -part, T, ALU.mult, ALU.add)
                dve.drain()
            dve.tensor_scalar(R, T, PI_BELOW, -PI_BELOW, ALU.min, ALU.max)
            dve.drain()
            dve.tensor_scalar(A, R, -1.0, None, ALU.mult)
            dve.drain()
            dve.tensor_tensor(A, A, R, ALU.max)
            dve.drain().then_inc(rope_sin_in, 1)
            dve.wait_ge(rope_ready, 1)

            def index_score(w, y):
                i, h = y // 8, y % 8
                score, r = bias_of(1, i), ir[:, y % 2, 0:P * (i + 1)]
                dve.wait_ge(ix_relu.sem, ix_relu.at(w, y + 1))
                if h == 0:
                    dve.tensor_scalar(score, r, iw[:, i, 0:1], None, ALU.mult).then_inc(ix_used.sem, 1)
                else:
                    dve.scalar_tensor_tensor(score, r, iw[:, i, h:h + 1], score, ALU.mult,
                                             ALU.add).then_inc(ix_used.sem, 1)
                dve.drain()
                if h == 7:
                    dve.memset(score[0:64, P * i + 64:P * i + P], REMOVED)
                    dve.drain()
                    if i == 0:
                        dve.tensor_scalar(score, score, 0.1 * REMOVED, NEG, ALU.is_le, ALU.mult)
                        dve.drain()

            def top_round(rounds):
                for i, r in rounds:
                    dve.max(top8[:, i - 1, :], bias_of(1, i))
                dve.drain()
                for i, r in rounds:
                    dve.match_replace(bias_of(1, i), top8[:, i - 1, :], bias_of(1, i), REMOVED)
                dve.drain()
                for i in [i for i, r in rounds if r == TOPK // 8 - 1]:
                    score = bias_of(1, i)
                    dve.tensor_scalar(score, score, 0.1 * REMOVED, NEG, ALU.is_gt, ALU.mult)
                    dve.drain()
                    dve.memset(score[0:64, P * i + 64:P * i + P], NEG)
                    dve.drain()

            def gate_scale(w):
                dve.wait_ge(gates_done.sem, gates_done.at(w, 1))
                dve.tensor_scalar(iw[:, :, :], TRO[:, 0:32].rearrange("p (t h) -> p t h", h=8),
                                  8 ** -0.5, None, ALU.mult)
                dve.drain()

            def pool_window(w, g):
                win = 2 << g
                u = pu[:, g % 2, :]
                dve.wait_ge(acc_free[(17 + g) % 2].sem, acc_free[(17 + g) % 2].at(w, (17 + g) // 2 + 1))
                src = u
                for step in range(g + 1):
                    lag, dst = 1 << step, sc2[:, step % 2, :]
                    dve.tensor_tensor(dst[:, lag:S], src[:, lag:S], src[:, 0:S - lag], ALU.add)
                    dve.tensor_copy(dst[:, 0:lag], src[:, 0:lag])
                    dve.drain()
                    src = dst
                other = sc2[:, (g + 1) % 2, 0:win]
                dve.tensor_tensor(other, src[:, 0:win], cst("icnt", 0, win), ALU.mult)
                new_piece(w, N_PD2 + g)
                dve.scalar_tensor_tensor(piece[:, g % 2, :], src, 1.0 / win, u, ALU.mult, ALU.subtract)
                dve.drain()
                dve.tensor_tensor(piece[:, g % 2, 0:win], other, u[:, 0:win], ALU.subtract)
                dve.drain().then_inc(piece_ready.sem, 1)

            with dve.Fori(0, LAYERS) as L:
                w = Where(1, L)
                norm(w, 0, N_H2, "pre")
                for u in range(21):
                    if u == 2:
                        gate_scale(w)
                    for n, y in enumerate(IX_AT.get(u + 1, ())):
                        index_score(w, y)
                    if u < 17:
                        turn_finish(w, u)
                    else:
                        pool_window(w, u - 17)
                    for rounds in TOP_AT.get(u, ()):
                        top_round(rounds)
                for g in range(4):
                    u, a = (21, 21, 22, 23)[g], 21 + g
                    dve.wait_ge(unit_done.sem, unit_done.at(w, u + 1))
                    new_piece(w, N_PY2 + g)
                    dve.tensor_scalar(piece[:, g % 2, :], ACC[a % 2][:, :], prm(w, "pscale", g, g + 1), None,
                                      ALU.mult).then_inc(acc_free[a % 2].sem, 1)
                    dve.drain().then_inc(piece_ready.sem, 1)
                for rounds in TOP_AT[21]:
                    top_round(rounds)
                for n in range(SLOTS):
                    attention(w, n)
                sum_output(w, 0, 8)
                residual(w, 1, "post")
                norm(w, 2, N_HF2, "preff")
                for c in range(FCHUNKS):
                    with dve.Fori(0, HCH // 2) as i:
                        for s in range(2):
                            bk = (33 + s) % 2
                            dve.wait_ge(acc_free[bk].sem, acc_free[bk].at(w, i + 12 * c + 16 + s + 1))
                            new_piece(w, i * 2 + N_HID2 + HCH * c + s)
                            dve.tensor_tensor(piece[:, s, :], relu[:, s, :], relu[:, s, :],
                                              ALU.mult).then_inc(piece_ready.sem, 1)

                def add_chunk(i, m):
                    bk = (49 + m) % 2
                    dve.wait_ge(unit_done.sem, unit_done.at(w, i * 4 + 48 + 32 * (FCHUNKS - 1) + 2 * m + 2))
                    dve.tensor_tensor(mT2[:, bass.ds(i * 2 + m, 1), :], mT2[:, bass.ds(i * 2 + m, 1), :],
                                      ACC[bk][:, :].unsqueeze(1), ALU.add).then_inc(acc_free[bk].sem, 1)

                sum_output(w, 1, 24, add_chunk)
                residual(w, 3, "postff")

        @block.tensor
        def _(pe):
            pe.wait_ge(const_in, 16)
            ident = cst("ident")

            def unit(w, i2, s, bk, a2, tiles, rhs_hi, rhs_lo, first=True, last=True, pieces=None, w0=0, done=True,
                     between=()):
                pe.wait_ge(w_lo.sem, w_lo.at(w, 2 * i2 + s + 1))
                if first:
                    pe.wait_ge(acc_free[bk].sem, acc_free[bk].at(w, a2))
                for k in range(tiles):
                    if pieces is not None:
                        pe.wait_ge(piece_lo.sem, piece_lo.at(w, pieces + k + 1))
                    c = (w0 + k) * P
                    for j, (wt, rhs) in enumerate(((wH, rhs_hi(k)), (wL, rhs_hi(k)), (wH, rhs_lo(k)))):
                        mm = pe.matmul(ACC[bk][:, :], wt[:, s, c:c + P], rhs, start=first and k == 0 and j == 0,
                                       stop=last and k == tiles - 1 and j == 2)
                    for n, small in enumerate(between):
                        if k == n + tiles - 1 - len(between):
                            small()
                if done:
                    mm.then_inc(unit_done.sem, 1)

            def h_hi(k):
                return hH[:, k, :]

            def h_lo(k):
                return hL[:, k, :]

            def sums(w, r0, v, n):
                pe.wait_ge(stat_free.sem, stat_free.at(w, v))
                for k in range(n):
                    pe.wait_ge(sq_ready.sem, sq_ready.at(w, r0 + k + 1))
                    pe.matmul(STAT[:, :], cst("ones"), sq[:, (r0 + k) % 2, :], start=k == 0,
                              stop=k == n - 1).then_inc(sq_used.sem, 1)

            def output_sum(w, k, v):
                pe.wait_ge(stat_free.sem, stat_free.at(w, v))
                pe.wait_ge(sq_summed.sem, sq_summed.at(w, k + 1))
                pe.matmul(STAT[:, :], cst("ones"), SQ_SUM[w.b][:, :], start=True, stop=True).then_inc(out_summed.sem, 1)

            def l2_sum(w, c):
                if c == 0:
                    pe.wait_ge(stat_free.sem, stat_free.at(w, 1))
                else:
                    pe.wait_ge(l2_copied.sem, l2_copied.at(w, c))
                pe.wait_ge(sq_ready.sem, sq_ready.at(w, 8 + c + 1))
                pe.matmul(STAT[:, :], cst("ones"), sq[:, c % 2, :], start=True, stop=True).then_inc(sq_used.sem, 1)

            def index_logits(w, y):
                i, h = y // 8, y % 8
                if y == 0:
                    pe.wait_ge(turn_done.sem, turn_done.at(w, 5))
                if y >= 2:
                    pe.wait_ge(ix_relu.sem, ix_relu.at(w, y - 1))
                p0 = h % 2 * HD
                pe.matmul((PT, OA)[y % 2][:, 0:P * (i + 1)], iqT[p0:p0 + HD, h // 2, i * P:i * P + P],
                          ikT[p0:p0 + HD, 0:P * (i + 1)], start=True, stop=True).then_inc(ix_done.sem, 1)

            def turn(w, j):
                src = turn_src(w.b, j)
                pe.wait_ge(acc_free[j % 2].sem, acc_free[j % 2].at(w, j // 2 + 1))
                if j < N_ROT[w.b]:
                    pe.matmul(SC[j % 2][:, :], cst("turn2" if w.b else "turn1"), src, start=True,
                              stop=True).then_inc(turned.sem, 1)
                else:
                    for t in range(NT):
                        tr = pe.transpose(SC[j % 2][:, t * P:t * P + P], src[:, t * P:t * P + P], ident)
                    tr.then_inc(turned.sem, 1)

            def narrow(w):
                pe.wait_ge(gw_lo.sem, gw_lo.at(w, 1))
                for t in range(NT):
                    for k in range(KD):
                        for j, (a, g) in enumerate(((hH, gwH), (hL, gwH), (hH, gwL))):
                            mm = pe.matmul(TRO[:, t * 8:t * 8 + 8], a[:, k, t * P:t * P + P],
                                           g[:, k * 8:k * 8 + 8], start=k == 0 and j == 0,
                                           stop=k == KD - 1 and j == 2)
                mm.then_inc(gates_done.sem, 1)

            def attention(w, n):
                q, k, v, sc, pt, ao, st, _, n0 = ATT[w.b]
                if n < 32:
                    f, i, h = att_step(n)
                    if n == 0:
                        pe.wait_ge(turn_done.sem, turn_done.at(w, (12, 17)[w.b]))
                    pe.wait_ge(sc_read.sem, sc_read.at(w, n - 1))
                    pe.matmul(SC[n % 2][:, 0:P * (i + 1)], q[h * HD:h * HD + HD, f, i * P:i * P + P],
                              k[h * HD:h * HD + HD, f, 0:P * (i + 1)], start=True, stop=True).then_inc(sc_done.sem, 1)
                m = n - 1
                if 0 <= m < 32:
                    f, i, h = att_step(m)
                    pe.wait_ge(prob.sem, prob.at(w, m + 1))
                    if m:
                        pe.wait_ge(pt_copied.sem, pt_copied.at(w, m))
                    for j in range(i + 1):
                        tr = pe.transpose(PT[:, j * P:j * P + P], sc[:, m % 2, j * P:j * P + P], ident)
                    tr.then_inc(pt_done.sem, 1)
                m = n - 2
                if 0 <= m < 32:
                    f, i, h = att_step(m)
                    pe.wait_ge(pt_copied.sem, pt_copied.at(w, m + 1))
                    if m:
                        pe.wait_ge(oa_read.sem, oa_read.at(w, m))
                    for j in range(i + 1):
                        mm = pe.matmul(OA[:, 0:HD], pt[:, m % 2, j * P:j * P + P],
                                       v[:, j, (2 * f + h) * HD:(2 * f + h) * HD + HD], start=j == 0, stop=j == i)
                    mm.then_inc(pv_done.sem, 1)
                if n >= 4 and n % 2 == 0:
                    p = (n - 4) // 2
                    pe.wait_ge(oa_read.sem, oa_read.at(w, 2 * p + 2))
                    if p % 4 == 0 and p >= 4:
                        pe.wait_ge(piece_ready.sem, piece_ready.at(w, n0 + p // 4))
                    pe.transpose(TRO[:, p % 4 * P:p % 4 * P + P], ao[:, p % 2, :], ident).then_inc(tro_done.sem, 1)

            def start(w, e, *operands):
                latest = {}
                for x_ in (e - 3, *operands):
                    latest[x_ % 3] = max(latest.get(x_ % 3, x_), x_)
                for b_, x_ in latest.items():
                    if x_ >= 0:
                        pe.wait_ge(d_free[b_].sem, d_free[b_].at(w, x_ // 3 + 1))
                return DB[e % 3]

            def delta_small(w):
                pe.wait_ge(g_ready.sem, g_ready.at(w, 1))
                for b in range(2):
                    pe.wait_ge(acc_free[b].sem, acc_free[b].at(w, 14))
                pe.wait_ge(l2_copied.sem, l2_copied.at(w, 8))
                out = start(w, 0)
                for i, name in enumerate(("upto", "chunk", "even", "odd")):
                    mm = pe.matmul(out[:, 16 * i:16 * i + 16], cst(name), gcol(G_, G_ + 16), start=True, stop=True)
                mm.then_inc(d_done.sem, 1)

            def delta_pre(w, t, k):
                operands = {5: (4,), 6: (5,), 7: (5,), 18: (17, 16), 21: (20, 18), 22: (19,)}.get(k, ())
                if k in (8, 11, 14, 17):
                    operands = (k - 2,)
                elif k in (9, 12, 15, 10, 13, 16):
                    operands = ((k - 1, k - 2) if k % 3 == 0 else (k - 2, k - 3))
                e = ev_pre(t, k)
                out = start(w, e, *(ev_pre(t, o) for o in operands))
                tc = slice(t * P, t * P + P)
                LT, A, X, XT, M = (r[t % 2] for r in (eb, ab, xb, xtb, mb))
                two = {}
                if k == 0:
                    two = {h: (gv[:, G_ + 4 * t + h:G_ + 4 * t + h + 1].broadcast_to([P, P]), cst("upto")) for h in range(HN)}
                elif k == 1:
                    two = {h: (gv[:, BETA + 4 * t + h:BETA + 4 * t + h + 1].broadcast_to([P, P]), ident) for h in range(HN)}
                elif k == 2:
                    pe.wait_ge(l2_done.sem, l2_done.at(w, 2))
                    two = {h: (dk[:, h, tc], dk[:, h, tc]) for h in range(HN)}
                elif k == 3:
                    two = {h: (dk[:, h, tc], dq[:, h, tc]) for h in range(HN)}
                elif k == 4:
                    pe.wait_ge(xt_ready.sem, xt_ready.at(w, t + 1))
                elif k in (5, 8, 11, 14, 17):
                    l = (k - 5) // 3 + 1
                    pe.wait_ge(lt_ready.sem, lt_ready.at(w, 10 * (t // 2) + 2 * (l - 1) + t % 2 + 1))
                    two = {h: (LT[:, h, :], X[:, h, :]) for h in range(HN)}
                elif k in (6, 9, 12, 15):
                    two = {h: (XT[:, h, :], M[:, h, :]) for h in range(HN)}
                elif k in (7, 10, 13, 16, 18):
                    two = {h: (M[:, h, :], XT[:, h, :]) for h in range(HN)}
                elif k == 20:
                    pe.wait_ge(dn_act.sem, dn_act.at(w, 12))
                elif k == 21:
                    two = {h: (XT[:, h, :], LT[:, h, :]) for h in range(HN)}
                elif k == 22:
                    two = {h: (A[:, h, :], XT[:, h, :]) for h in range(HN)}
                for h in range(HN):
                    o = out[:, h * P:h * P + P]
                    if h in two:
                        mm = pe.matmul(o, two[h][0], two[h][1], start=True, stop=True)
                    elif k == 4:
                        mm = pe.transpose(o, XT[:, h, :], ident)
                    else:
                        mm = pe.transpose(o, (dk if k == 19 else dv)[:, h, tc], ident)
                mm.then_inc(d_done.sem, 1)

            def delta_scan(w, c):
                t, p0 = c // 2, c % 2 * CH
                cc = slice(c * CH, c * CH + CH)
                e = ev_scan(c, 0)
                last_state = (ev_scan(c - 1, 2),) if c else ()
                out = start(w, e, ev_pre(t, 21), ev_pre(t, 22), *last_state)
                if c == 0:
                    pe.wait_ge(state_zero.sem, state_zero.at(w, 1))
                for h in range(HN):
                    mm = pe.matmul(out[p0:p0 + CH, h * P:h * P + P], dk[:, h, cc], state[:, h, :], start=True, stop=True)
                mm.then_inc(d_done.sem, 1)
                out = start(w, e + 1, e)
                pe.wait_ge(qdec_ready.sem, qdec_ready.at(w, t + 1))
                for h in range(HN):
                    o = out[:, h * CH:h * CH + CH]
                    pe.matmul(o, state[:, h, :], dq[:, h, cc], start=True, stop=False)
                    mm = pe.matmul(o, vn[p0:p0 + CH, h, :], qkT[p0:p0 + CH, t, h, p0:p0 + CH], start=False, stop=True)
                mm.then_inc(d_done.sem, 1)
                out = start(w, e + 2)
                for h in range(HN):
                    mm = pe.matmul(out[:, h * P:h * P + P], kdec[p0:p0 + CH, t, h, :], vn[p0:p0 + CH, h, :],
                                   start=True, stop=True)
                mm.then_inc(d_done.sem, 1)

            with pe.Fori(0, LAYERS) as L:
                w = Where(0, L)
                sums(w, 0, 0, KD)
                for u in range(28):
                    unit(w, u // 2, u % 2, u % 2, u // 2, KD, h_hi, h_lo, pieces=N_H1 if u == 0 else None)
                    if 1 <= u <= 12:
                        turn(w, u - 1)
                    if u == 3:
                        narrow(w)
                    if 14 <= u < 22:
                        l2_sum(w, u - 14)
                for kind, a, k in ORDER:
                    if kind == "att":
                        attention(w, a)
                    elif kind == "small":
                        delta_small(w)
                    elif kind == "pre":
                        delta_pre(w, 2 * a, k)
                        delta_pre(w, 2 * a + 1, k)
                    else:
                        delta_scan(w, a)
                start(w, EVENTS, EVENTS - 2, EVENTS - 1)
                for h in range(HN):
                    pe.wait_ge(sq_ready.sem, sq_ready.at(w, 16 + h + 1))
                    pe.matmul(DSUM[h][:, :], cst("ones"), sq[:, h % 2, :], start=True, stop=True).then_inc(sq_used.sem, 1)
                with pe.Fori(0, KD // 2) as i:
                    for s in range(2):
                        unit(w, i + 14, s, s, i + 14, KD, h_hi, h_lo, pieces=(N_ATT1, None)[s])
                output_sum(w, 0, 1)
                sums(w, 28, 2, KD)
                with pe.Fori(0, NJ) as i:
                    for s in range(2):
                        unit(w, i + 18, s, s, i + 18, KD, h_hi, h_lo, pieces=(N_HF1, None)[s])
                with pe.Fori(0, KD // 2) as i:
                    for m in range(2):
                        for u in range(3):
                            y = 3 * m + u
                            unit(w, i * 3 + 40 + y // 2, y % 2, m, i + 40, min(8, NJ - 8 * u),
                                 lambda k, u=u: hidH1[:, 8 * u + k, :], lambda k, u=u: hidL1[:, 8 * u + k, :],
                                 first=u == 0, last=u == 2, pieces=N_HID1 + 8 * u if m == 0 else None)
                output_sum(w, 1, 3)

            with pe.Fori(0, LAYERS) as L:
                w = Where(1, L)
                sums(w, 0, 0, KD)
                for u in range(21):
                    unit(w, u // 2, u % 2, u % 2, u // 2, KD, h_hi, h_lo, pieces=N_H2 if u == 0 else None,
                         between=[lambda y=y: index_logits(w, y) for y in IX_AT.get(u, ())])
                    if 1 <= u <= 17:
                        turn(w, u - 1)
                    if u == 0:
                        narrow(w)
                for g in range(4):
                    u, a = (21, 21, 22, 23)[g], 21 + g
                    unit(w, u // 2, u % 2, a % 2, a // 2, 1, lambda k, g=g: pdH[:, g, :], lambda k, g=g: pdL[:, g, :],
                         pieces=N_PD2 + g, w0=1 if g == 1 else 0, done=g > 0)
                for n in range(SLOTS):
                    attention(w, n)
                with pe.Fori(0, KD // 2) as i:
                    for s in range(2):
                        unit(w, i + 12, s, (25 + s) % 2, i + 12 + s, KD, h_hi, h_lo, pieces=(N_PY2, None)[s])
                output_sum(w, 0, 1)
                sums(w, 16, 2, KD)
                for c in range(FCHUNKS):
                    with pe.Fori(0, HCH // 2) as i:
                        for s in range(2):
                            unit(w, i + 16 + 16 * c, s, (33 + s) % 2, i + 12 * c + 16 + s, KD, h_hi, h_lo,
                                 pieces=(N_HF2, None)[s])
                    with pe.Fori(0, KD // 2) as i:
                        for m in range(2):
                            for s in range(2):
                                unit(w, i * 2 + 24 + 16 * c + m, s, (49 + m) % 2, i + 12 * c + 24 + m, KD,
                                     lambda k, s=s: hidH2[:, 8 * s + k, :], lambda k, s=s: hidL2[:, 8 * s + k, :],
                                     first=s == 0, last=s == 1,
                                     pieces=N_HID2 + HCH * c + 8 * s if m == 0 else None)
                output_sum(w, 1, 3)


def tiles(a):
    return a.reshape(a.shape[0] // P, P, a.shape[1]).transpose(1, 0, 2)


def unit_of(a):
    u = tiles(a).reshape(P, -1)
    return np.pad(u, ((0, 0), (0, KD * P - u.shape[1])))


def columns(a, order):
    return [unit_of(a[:, c * P:c * P + P]) for c in order]


def channel_cols(a):
    return a.reshape(-1, P).T


def kernel(**inputs):
    import concourse.bacc as bacc
    from concourse.bass_utils import run_bass_kernel_spmd

    z = {k: np.ascontiguousarray(v) for k, v in inputs.items()}
    interleave = [c for j in range(NJ) for c in (j, NJ + j)]
    w0, w1, par0, par1 = [], [], [], []
    for l in range(LAYERS):
        win = z["w_in"][l]
        w0 += columns(win, range(28)) + columns(z["w_out"][l], range(KD)) + columns(z["ffn_w_in"][l], interleave)
        down = z["ffn_w_out"][l]
        for m in range(KD):
            w0 += [unit_of(down[r * P:min(r + 8, NJ) * P, m * P:m * P + P]) for r in (0, 8, 16)]
        fconv = z["ffn_conv_w"][l].reshape(FCONV, 2 * NJ, P)[:, interleave]
        par0.append(np.concatenate([
            channel_cols(z["norm_pre_mix"][l]), channel_cols(z["norm_post_mix"][l]),
            channel_cols(z["norm_pre_ffn"][l]), channel_cols(z["norm_post_ffn"][l]),
            z["dn_conv_w"][l].reshape(DCONV, 12, P).transpose(2, 1, 0).reshape(P, -1),
            z["dn_norm_w"][l][:, None],
            np.broadcast_to(z["dn_a_log"][l], (P, 4)), np.broadcast_to(z["dn_dt_bias"][l], (P, 4)),
            fconv.transpose(2, 1, 0).reshape(P, -1),
            z["ffn_conv_b"][l].reshape(2 * NJ, P)[interleave].T,
            tiles(win[:, 28 * P:]).reshape(P, -1)], axis=1))
        win = z["w_in_2"][l]
        ik = win[:, 20 * P:20 * P + 64]
        w1 += [unit_of(np.concatenate([ik, ik], axis=1))]
        w1 += columns(win, [*range(16, 20), *range(4, 8), *range(8, 12), *range(12, 16), *range(4)])
        wp = z["w_pool_2"][l]
        w1 += [unit_of(np.concatenate([wp[0], wp[1]])), unit_of(wp[2]), unit_of(wp[3])]
        w1 += columns(z["w_out_2"][l], range(KD))
        for c in range(FCHUNKS):
            w1 += columns(z["w_ff1_2"][l], range(HCH * c, HCH * c + HCH))
            down = z["w_ff2_2"][l][HCH * P * c:HCH * P * (c + 1)]
            for m in range(KD):
                w1 += [unit_of(down[r * D:r * D + D, m * P:m * P + P]) for r in range(2)]
        par1.append(np.concatenate([
            channel_cols(z["g_pre_mix_2"][l]), channel_cols(z["g_post_mix_2"][l]),
            channel_cols(z["g_pre_ffn_2"][l]), channel_cols(z["g_post_ffn_2"][l]),
            channel_cols(z["pool_scale_2"][l]), tiles(win[:, 20 * P + 64:]).reshape(P, -1)], axis=1))
    arrays = {
        "x_dram": np.ascontiguousarray(tiles(z["x"][0].T)),
        "w0_dram": np.stack(w0), "w1_dram": np.stack(w1),
        "par_dram": np.stack([np.pad(p, ((0, 0), (0, PAR_W - p.shape[1]))) for p in (*par0, *par1, par1[-1])]),
        "pos_dram": z["positions_2"][0], "const_dram": constants(),
    }
    nc = bacc.Bacc("TRN2", target_bir_lowering=False, num_devices=1)
    d = {n[:-5]: nc.dram_tensor(n, a.shape, mybir.dt.from_np(a.dtype), kind="ExternalInput").ap()
         for n, a in arrays.items()}
    d["out"] = nc.dram_tensor("out_dram", (P, KD, S), F32, kind="ExternalOutput").ap()
    build(nc, d)
    r = run_bass_kernel_spmd(nc, [arrays], core_ids=[0])
    out = r.results[0]["out_dram"]
    return np.ascontiguousarray(out.transpose(1, 0, 2).reshape(D, S).T).reshape(1, S, D)
```

```python
from contextlib import ExitStack
import math

import numpy as np

import concourse.bass as bass
from concourse import mybir

F32 = mybir.dt.float32
F32R = mybir.dt.float32r
I32 = mybir.dt.int32
ALU = mybir.AluOpType
ACT = mybir.ActivationFunctionType
AX_X = mybir.AxisListType.X

P = 128
S = 512
D = 1024
KD = D // P
NT = S // P
LAYERS = 2
EPS = 1e-6
NEG = -1e30
REMOVED = -3e38

H1 = 8
HD = 64
HN = 4
CH = 64
NCH = S // CH
FF1 = 2816
NJ = FF1 // P
DCONV, FCONV = 4, 3

TOPK = 128
FF2 = 4096
NH2 = FF2 // P
HCH = 16
FCHUNKS = NH2 // HCH

U_IN = (28, 22)
POOL_U = 5
U1 = 28 + 8 + 2 * NJ + 3 * KD
U2 = 22 + 8 + NH2 + 2 * KD * FCHUNKS
UNITS = (U1, U2)
G_IN = (28, 25)
GROUPS = (28 + 8 + 2 * NJ + KD, 25 + 8 + NH2 + KD * FCHUNKS)
N_H1, N_ATT1, N_DN1, N_HF1, N_HID1 = 0, 8, 12, 16, 24
N_H2, N_PD2, N_PY2, N_ATT2, N_HF2, N_HID2 = 0, 8, 12, 16, 20, 28
PIECES = (24 + NJ, 28 + NH2)

SLOTS = 2 * 4 * NT + 3
PRE = 23
ATT_SPLIT = (12, 20)


def mixer_order():

    def spread(steps, n0, n1):
        out, n = [], n0
        for i, step in enumerate(steps):
            while n < n1 and (n - n0) * len(steps) <= i * (n1 - n0):
                out.append(("att", n, 0))
                n += 1
            out.append(step)
        return out + [("att", m, 0) for m in range(n, n1)]

    scans = [[("scan", c, j) for c in range(4 * pair, 4 * pair + 4) for j in range(3)] for pair in range(2)]
    second = []
    for k in range(PRE):
        second += [("pre", 1, k)] + scans[0][k - 1:k] * (1 <= k <= 12)
    first = [("small", 0, 0)] + [("pre", 0, k) for k in range(PRE)]
    return (spread(first, 0, ATT_SPLIT[0]) + spread(second, *ATT_SPLIT) + spread(scans[1], ATT_SPLIT[1], SLOTS))


ORDER = mixer_order()

EVENT_OF = {}
for _kind, _a, _k in ORDER:
    if _kind == "small":
        EVENT_OF["small"] = len(EVENT_OF)
    elif _kind == "pre":
        for _t in (2 * _a, 2 * _a + 1):
            EVENT_OF["pre", _t, _k] = len(EVENT_OF)
    elif _kind == "scan":
        EVENT_OF["scan", _a, _k] = len(EVENT_OF)
EVENTS = len(EVENT_OF)


def ev_pre(t, k):
    return EVENT_OF["pre", t, k]


def ev_scan(c, j):
    return EVENT_OF["scan", c, j]


IX_AT, _y = {}, 0
for _u, _n in ((6, 3), (7, 6), (8, 6), (9, 6), (10, 6), (11, 5)):
    IX_AT[_u] = tuple(range(_y, _y + _n))
    _y += _n
assert _y == 32

TOP_AT, _r = {}, 0
for _u, _n in ((9, 1), (10, 1), (11, 1), (12, 1), (13, 1), (14, 2), (15, 2), (16, 2), (17, 2), (18, 2), (19, 1)):
    TOP_AT[_u] = [[(1, r), (2, r)] for r in range(_r, _r + _n)]
    _r += _n
assert _r == TOPK // 8
TOP_AT[20] = [[(3, 0)]]
TOP_STEPS = {(r - 1) * 22 // 15 + 1: [(3, r)] for r in range(1, TOPK // 8)}

TWO_PI = (6.28125, 0.0019350051879882812, 2 * math.pi - 6.28125 - 0.0019350051879882812)
PI_BELOW = 3.1415925

CONST = [("ident", P), ("ones", P), ("invf", 1), ("eps", 1), ("one", 1), ("qscale", 1), ("halfpi", 1),
         ("cos1", S), ("sin1", S), ("count", S), ("turn1", P), ("turn2", P),
         ("upto", P), ("even", 1), ("odd", 1), ("causal", P), ("level", 6 * P), ("icnt", 16)]
CAT, _o = {}, 0
for _n, _w in CONST:
    CAT[_n] = (_o, _w)
    _o += _w
CONST_W = _o
CONST_FIRST = CAT["cos1"][0]

PAR1 = [("pre", 8), ("post", 8), ("preff", 8), ("postff", 8), ("dconv", 12 * DCONV), ("dnorm", 1),
        ("alog", 4), ("dt", 4), ("fconv", 2 * NJ * FCONV), ("fbias", 2 * NJ), ("gates", KD * 8)]
PAR2 = [("pre", 8), ("post", 8), ("preff", 8), ("postff", 8), ("pscale", 4), ("gates", KD * 8)]


def offsets(table):
    at, o = {}, 0
    for n, w in table:
        at[n] = (o, w)
        o += w
    return at, o


PA1, PAR1_W = offsets(PAR1)
PA2, PAR2_W = offsets(PAR2)
PAR_W = max(PAR1_W, PAR2_W)


def constants():
    c = np.zeros((P, CONST_W), np.float32)

    def put(name, v):
        o, w = CAT[name]
        c[:, o:o + w] = v

    p = np.arange(P)
    inv = (1.0 / (np.float32(10000.0) ** (np.arange(0, HD, 2, dtype=np.float32) / np.float32(HD)))).astype(np.float32)
    ang = inv[(p % 64) % 32][:, None] * np.arange(S, dtype=np.float32)[None]
    put("cos1", np.cos(ang))
    put("sin1", np.sin(ang))
    dist = p[:, None] - (np.arange(S)[None] - (S - P))
    count = ((dist >= 0) & (dist <= 128)).astype(np.float64) + ((dist >= 0) & (dist % 4 == 0)) + ((dist >= 0) & (dist % 16 == 0))
    put("count", np.where(count > 0, np.log(np.maximum(count, 1)), NEG))
    for name, half, rot in (("turn1", 32, 64), ("turn2", 8, 16)):
        m = np.zeros((P, P), np.float32)
        for q in range(P):
            d = q % 64
            if d < half:
                m[q + half, q] = -1.0
            elif d < rot:
                m[q - half, q] = 1.0
        put(name, m)
    put("ident", np.eye(P))
    put("ones", 1.0)
    j, i = p[:, None], p[None]
    same = j // CH == i // CH
    put("upto", same & (j <= i))
    put("even", j // CH == 0)
    put("odd", j // CH == 1)
    put("causal", np.where(same & (j <= i), 0.0, NEG))
    put("level", np.concatenate([(i // (2 * b) == j // (2 * b)) & (i // b % 2 == 1) & (j // b % 2 == 0)
                                 for b in (1, 2, 4, 8, 16, 32)], axis=1))
    put("icnt", 1.0 / np.arange(1, 17, dtype=np.float32))
    f = (np.float32(500000.0) ** (-np.arange(8, dtype=np.float32) / np.float32(8))).astype(np.float32)
    put("invf", np.where(p % 64 < 16, f[p % 8], 0.0)[:, None])
    put("eps", EPS)
    put("one", 1.0)
    put("qscale", -0.5 * math.log(128.0))
    put("halfpi", math.pi / 2)
    return c


class Signal:

    def __init__(self, ctx, nc, name, per, credit=0):
        self.sem = ctx.enter_context(nc.semaphore(name))
        self.per, self.credit = per, credit

    def at(self, w, k):
        return self.credit + (LAYERS * self.per[0] if w.b else 0) + w.L * self.per[w.b] + k


class Where:

    def __init__(self, b, L):
        self.b, self.L = b, L


def build(nc, d):
    ctx = ExitStack()
    with ctx:
        def sb(name, shape, dt, c=ctx):
            return c.enter_context(nc.sbuf_tensor(name, shape, dt))

        def signal(name, first, second, credit=0):
            return Signal(ctx, nc, name, (first, second), credit)

        x = sb("x", [P, KD, S], F32)
        hH = sb("hH", [P, KD, S], F32R)
        hL = sb("hL", [P, KD, S], F32R)
        raw = sb("raw", [P, 2, KD * P], F32)
        wH = sb("wH", [P, 2, KD * P], F32R)
        wL = sb("wL", [P, 2, KD * P], F32R)
        sq = sb("sq", [P, 2, S], F32)
        piece = sb("piece", [P, 2, S], F32)
        rstd = sb("rstd", [P, S], F32)
        root = sb("root", [P, 2, 4 * NT], F32)
        rope2 = sb("rope2", [P, 2, S], F32)
        const = sb("const", [P, CONST_W], F32)
        par = sb("par", [P, PAR_W], F32)
        par_next = sb("par_next", [P, PAR_W], F32)
        gwH = sb("gwH", [P, KD * 8], F32R)
        gwL = sb("gwL", [P, KD * 8], F32R)

        with ExitStack() as share:
            mT1 = sb("mT1", [P, KD, S], F32, share)
            hidH1 = sb("hidH1", [P, NJ, S], F32R, share)
            hidL1 = sb("hidL1", [P, NJ, S], F32R, share)
            sq_sum1 = sb("sq_sum1", [P, S], F32, share)
        with ExitStack() as share:
            qT1 = sb("qT1", [P, 4, S], F32, share)
            kT1 = sb("kT1", [P, 4, S], F32, share)
            v1 = sb("v1", [P, NT, S], F32, share)
            dq = sb("dq", [P, HN, S], F32, share)
            dk = sb("dk", [P, HN, S], F32, share)
            dv = sb("dv", [P, HN, S], F32, share)
            kdec = sb("kdec", [P, NT, HN, P], F32, share)
            qkT = sb("qkT", [P, NT, HN, P], F32, share)
            zT = sb("zT", [P, HN, S], F32, share)
            eb = [sb(f"eb{i}", [P, HN, P], F32, share) for i in range(2)]
            ab = [sb(f"ab{i}", [P, HN, P], F32, share) for i in range(2)]
            xb = [sb(f"xb{i}", [P, HN, P], F32, share) for i in range(2)]
            xtb = [sb(f"xtb{i}", [P, HN, P], F32, share) for i in range(2)]
            mb = [sb(f"mb{i}", [P, HN, P], F32, share) for i in range(2)]
            vn = sb("vn", [P, HN, P], F32, share)
            state = sb("state", [P, HN, P], F32, share)
            gv = sb("gv", [P, 324], F32, share)
            sc1 = sb("sc1", [P, 2, S], F32, share)
            pt1 = sb("pt1", [P, 2, S], F32, share)
            ao1 = sb("ao1", [P, 2, P], F32, share)
            st1 = sb("st1", [P, 17], F32, share)
        with ExitStack() as share:
            mT2 = sb("mT2", [P, KD, S], F32, share)
            hidH2 = sb("hidH2", [P, HCH, S], F32R, share)
            hidL2 = sb("hidL2", [P, HCH, S], F32R, share)
            relu = sb("relu", [P, 2, S], F32, share)
            sq_sum2 = sb("sq_sum2", [P, S], F32, share)
        with ExitStack() as share:
            qT2 = sb("qT2", [P, 4, S], F32, share)
            kT2 = sb("kT2", [P, 4, S], F32, share)
            v2 = sb("v2", [P, NT, S], F32, share)
            iqT = sb("iqT", [P, 4, S], F32, share)
            ikT = sb("ikT", [P, S], F32, share)
            bias2 = sb("bias2", [P, 10 * P], F32, share)
            ir = sb("ir", [P, 2, S], F32, share)
            pu = sb("pu", [P, 2, S], F32, share)
            turn2 = sb("turn2_in", [P, 2, S], F32, share)
            pdH = sb("pdH", [P, 4, S], F32R, share)
            pdL = sb("pdL", [P, 4, S], F32R, share)
            iw = sb("iw", [P, NT, 8], F32, share)
            top8 = sb("top8", [P, 3, 8], F32, share)
            sc2 = sb("sc2", [P, 2, S], F32, share)
            pt2 = sb("pt2", [P, 2, S], F32, share)
            ao2 = sb("ao2", [P, 2, P], F32, share)
            st2 = sb("st2", [P, 17], F32, share)
        with ExitStack() as share:
            posi = sb("posi", [P, S], I32, share)
            ang = sb("ang", [P, 4, S], F32, share)

        bank = [ctx.enter_context(nc.psum_tensor(f"bank{i}", [P, S], F32)) for i in range(8)]
        ACC = bank[0:2]
        STAT = bank[2]
        DB = bank[0:3]
        SC = bank[3:5]
        PT, OA, TRO = bank[5:8]

        def cst(name, a=0, b=None):
            o, n = CAT[name]
            return const[:, o + a:o + (n if b is None else b)]

        def prm(w, name, a, b):
            o = (PA2 if w.b else PA1)[name][0]
            return par[:, o + a:o + b]

        def prmd(w, name, i):
            return par[:, bass.ds(i + (PA2 if w.b else PA1)[name][0], 1)]

        loaded = [signal(f"loaded{s}", 16 * U1 // 2, 16 * U2 // 2) for s in range(2)]
        w_hi = signal("w_hi", U1, U2, 2)
        w_lo = signal("w_lo", U1, U2, 2)
        unit_done = signal("unit_done", U1, U2, 2)
        acc_free = [signal(f"acc_free{b}", GROUPS[0] // 2, (GROUPS[1] + 1 - b) // 2, 1) for b in range(2)]
        piece_ready = signal("piece_ready", *PIECES)
        piece_hi = signal("piece_hi", *PIECES)
        piece_lo = signal("piece_lo", *PIECES, 2)
        sq_ready = signal("sq_ready", 44, 32)
        sq_used = signal("sq_used", 44, 32, 2)
        sq_summed = signal("sq_summed", 2, 2)
        out_summed = signal("out_summed", 2, 2)
        rstd_ready = signal("rstd_ready", 2, 2)
        stat_free = signal("stat_free", 2, 2)
        root_ready = signal("root_ready", 2, 2)
        root_inv = signal("root_inv", 2, 2)
        spread = signal("spread", 2, 2)
        x_ready = [signal(f"x_ready{m}", 8, 8, 4) for m in range(2)]
        out_scaled = signal("out_scaled", 8, 8)
        par_loaded = signal("par_loaded", 16, 16)
        par_in = signal("par_in", 1, 1)
        gw_hi = signal("gw_hi", 1, 1)
        gw_lo = signal("gw_lo", 1, 1)
        gates_raw = signal("gates_raw", 1, 1)
        gates_copied = signal("gates_copied", 1, 1)
        gates_done = signal("gates_done", 1, 1)
        turned = signal("turned", 12, 17)
        turn_done = signal("turn_done", 12, 17, 2)
        sc_done = signal("sc_done", 32, 32)
        sc_read = signal("sc_read", 32, 32, 2)
        nmax = signal("nmax", 32, 32)
        prob = signal("prob", 32, 32)
        pt_done = signal("pt_done", 32, 32)
        pt_copied = signal("pt_copied", 32, 32)
        pv_done = signal("pv_done", 32, 32)
        oa_read = signal("oa_read", 32, 32)
        tro_done = signal("tro_done", 16, 16)
        conv_in = signal("conv_in", 12, 0)
        dn_act = signal("dn_act", 12, 0)
        l2_copied = signal("l2_copied", 8, 0)
        l2_rstd = signal("l2_rstd", 2, 0)
        l2_done = signal("l2_done", 2, 0)
        dn_root = signal("dn_root", 1, 0)
        dn_inv = signal("dn_inv", 1, 0)
        dn_rstd = signal("dn_rstd", 4, 0)
        z_ready = signal("z_ready", 4, 0)
        gate_a = signal("gate_a", 1, 0)
        gate_b = signal("gate_b", 1, 0)
        g_ready = signal("g_ready", 1, 0)
        kd_in = signal("kd_in", 1, 0)
        kd_out = signal("kd_out", 1, 0)
        state_zero = signal("state_zero", 1, 0)
        d_done = signal("d_done", EVENTS, 0)
        d_free = [signal(f"d_free{b}", len(range(b, EVENTS, 3)), 0) for b in range(3)]
        gr_exp = signal("gr_exp", 4, 0)
        e_in = signal("e_in", 4, 0)
        e_ready = signal("e_ready", 4, 0)
        qdec_ready = signal("qdec_ready", 4, 0)
        xt_ready = signal("xt_ready", 4, 0)
        lt_ready = signal("lt_ready", 20, 0)
        glu_in = signal("glu_in", 2 * NJ, 0)
        gelu_done = signal("gelu_done", NJ, 0)
        ix_done = signal("ix_done", 0, 32)
        ix_relu = signal("ix_relu", 0, 32)
        ix_used = signal("ix_used", 0, 32, 2)
        pool_done = signal("pool_done", 0, 4)
        cos_done = signal("cos_done", 0, 13)
        const_in = ctx.enter_context(nc.semaphore("const_in"))
        const_rest = ctx.enter_context(nc.semaphore("const_rest"))
        x_in = [ctx.enter_context(nc.semaphore(f"x_in{q}")) for q in range(4)]
        pos_in = ctx.enter_context(nc.semaphore("pos_in"))
        rope_sin_in = ctx.enter_context(nc.semaphore("rope_sin_in"))
        rope_ready = ctx.enter_context(nc.semaphore("rope_ready"))
        stored = ctx.enter_context(nc.semaphore("stored"))

        def heads(ap):
            return ap.rearrange("p (h c) -> p h c", c=P)

        def state_of(c):
            return sq[:, 0, :].rearrange("p (h c) -> p h c", c=P) if c % 2 else state[:, :, :]

        def per_head(ap, n=P):
            return ap.unsqueeze(2).broadcast_to([P, HN, n])

        def over_heads(ap, h=HN):
            return ap.unsqueeze(1).broadcast_to([P, h, ap.shape[-1]])

        def gcol(a, b=None):
            return gv[:, a:a + 16 if b is None else b]

        BA, XA, AX, E1, EBV, SP_, BETA, G_, SM, KDI, KD_, EG, GLB, BG, EA = (
            0, 32, 48, 64, 80, 96, 112, 128, 144, 208, 224, 240, 256, 288, 304)

        def tile4(a, t):
            return gv[:, a + 4 * t:a + 4 * t + 4]

        ATT = ((qT1, kT1, v1, sc1, pt1, ao1, st1, 0, N_ATT1), (qT2, kT2, v2, sc2, pt2, ao2, st2, 4, N_ATT2))
        MX, NMX, SUM, RS = 0, 4, 8, 12

        def bias_of(b, i):
            if b == 0:
                return cst("count", S - P * (i + 1), S)
            o = P * (i * (i + 1) // 2)
            return bias2[:, o:o + P * (i + 1)]

        def att_step(n):
            return n // 2 % 4, n // 8, n % 2

        def att_place(w, i, dst):
            f0 = ATT[w.b][7]
            return dst[:, f0:f0 + 4, i * P:i * P + P]

        def xconv(c):
            return xb[c % 2][:, :, :].rearrange("p h c -> p (h c)")

        def turn_src(b, j):
            if b == 0:
                return mb[j % 2][:, :, :].rearrange("p h c -> p (h c)")
            return turn2[:, j % 2, :]

        def turn_dst(b, j):
            if b == 0:
                return (qT1, kT1)[j // 4][:, j % 4, :]
            if j == 0:
                return ikT[:, :]
            return (iqT, qT2, kT2)[(j - 1) // 4][:, (j - 1) % 4, :]

        def l2_stat(i):
            return (kdec, qkT)[i][:, :, :, :]

        DSTAT = bank[3:7]

        def gates_place(b):
            return pu[0:8, 0, :] if b else eb[0][0:8, :, :].rearrange("p h c -> p (h c)")

        def turn_of(b, u):
            if b == 0:
                return u if u < 12 else None
            if u < POOL_U:
                return u
            return u - 4 if POOL_U + 4 <= u < 21 else None

        N_ROT = (8, 13)
        MT = (mT1, mT2)
        SQ_SUM = (sq_sum1, sq_sum2)

        block = ctx.enter_context(nc.Block())

        @block.sync
        def _(sp):
            sp.dma_start(const[:, 0:CONST_FIRST], d["const"][:, 0:CONST_FIRST]).then_inc(const_in, 16)

            def load(w, src, i2, s):
                sp.wait_ge(w_hi.sem, w_hi.at(w, 2 * i2 + s - 1))
                sp.wait_ge(w_lo.sem, w_lo.at(w, 2 * i2 + s - 1))
                sp.dma_start(raw[:, s, :], src).then_inc(loaded[s].sem, 16)

            for s in range(2):
                load(Where(0, 0), d["w0"][s], 0, s)
            for q in range(4):
                sp.dma_start(x[:, 2 * q:2 * q + 2, :], d["x"][:, 2 * q:2 * q + 2, :]).then_inc(x_in[q], 16)
            sp.dma_start(const[:, CONST_FIRST:CONST_W], d["const"][:, CONST_FIRST:CONST_W]).then_inc(const_rest, 16)
            with sp.Fori(1, U1 // 2) as i:
                for s in range(2):
                    load(Where(0, 0), d["w0"][i * 2 + s], i, s)
            for b in range(2):
                with sp.Fori(1 - b, LAYERS) as L:
                    w = Where(b, L)
                    with sp.Fori(0, UNITS[b] // 2) as i:
                        for s in range(2):
                            load(w, d[f"w{b}"][L * UNITS[b] + i * 2 + s], i, s)
            for s in range(2):
                load(Where(1, LAYERS), d["w1"][s], 0, s)
            for m in range(2):
                sp.wait_ge(x_ready[m].sem, x_ready[m].at(Where(1, LAYERS), 0))
            sp.dma_start(d["out"], x[:, :, :]).then_inc(stored, 16)
            sp.wait_ge(stored, 16)
            for s in range(2):
                sp.wait_ge(loaded[s].sem, loaded[s].at(Where(1, LAYERS), 16))
            sp.wait_ge(par_loaded.sem, par_loaded.at(Where(1, LAYERS), 16))

        @block.gpsimd
        def _(pool):
            for ring in (w_lo, piece_lo):
                pool.nop().then_inc(ring.sem, ring.credit)

            def w_low(w, i2, s):
                pool.wait_ge(w_hi.sem, w_hi.at(w, 2 * i2 + s + 1))
                pool.wait_ge(unit_done.sem, unit_done.at(w, 2 * i2 + s - 1))
                pool.tensor_tensor(wL[:, s, :], raw[:, s, :], wH[:, s, :].bitcast(F32),
                                   ALU.subtract).then_inc(w_lo.sem, 1)

            def next_low(w, i2, s):
                w_low(w, i2 + 1, s)

            def piece_low(w, n, s, dst, hi, shape=lambda ap: ap):
                pool.wait_ge(piece_hi.sem, piece_hi.at(w, n + 1))
                pool.tensor_tensor(dst, shape(piece[:, s, :]), hi.bitcast(F32), ALU.subtract).then_inc(piece_lo.sem, 1)

            def layer_params(w):
                pool.wait_ge(par_in.sem, par_in.at(w, 1))
                pool.dma_start(par_next[:, :], d["par"][w.L + (w.b * LAYERS + 1)]).then_inc(par_loaded.sem, 16)
                pool.wait_ge(gw_hi.sem, gw_hi.at(w, 1))
                pool.tensor_tensor(gwL[:, :], prm(w, "gates", 0, KD * 8), gwH[:, :].bitcast(F32),
                                   ALU.subtract).then_inc(gw_lo.sem, 1)

            def residual_odd(w, half):
                for k in range(1, KD, 2):
                    pool.wait_ge(out_scaled.sem, out_scaled.at(w, 4 * half + k // 2 + 1))
                    pool.tensor_tensor(x[:, k, :], x[:, k, :], MT[w.b][:, k, :], ALU.add).then_inc(x_ready[1].sem, 1)

            def level(w, t, l):
                pool.tensor_tensor(eb[t % 2][:, :, :], ab[t % 2][:, :, :],
                                   over_heads(cst("level", l * P, l * P + P)), ALU.mult).then_inc(lt_ready.sem, 1)

            def norm_pieces(w, n0):
                for k in range(KD):
                    piece_low(w, n0 + k, (n0 + k) % 2, hL[:, k, :], hH[:, k, :])

            pool.dma_start(posi[:, :], d["pos"].partition_broadcast(P)).then_inc(pos_in, 16)
            pool.dma_start(par_next[:, :], d["par"][0]).then_inc(par_loaded.sem, 16)
            for s in range(2):
                w_low(Where(0, 0), 0, s)
            with pool.Fori(0, LAYERS) as L:
                w = Where(0, L)
                layer_params(w)
                norm_pieces(w, N_H1)
                for u in range(28):
                    if u == 1:
                        pool.wait_ge(const_rest, 16)
                    next_low(w, u // 2, u % 2)
                for kind, a, k in ORDER:
                    if kind == "att" and a % 8 == 2 and a >= 10:
                        f = (a - 10) // 8
                        piece_low(w, N_ATT1 + f, f % 2, att_place(w, f, hL), att_place(w, f, hH), heads)
                    if kind == "pre" and k == 4:
                        for t in (2 * a, 2 * a + 1):
                            pool.wait_ge(xt_ready.sem, xt_ready.at(w, t + 1))
                            level(w, t, 1)
                    if kind == "pre" and k in (5, 8, 11, 14):
                        l = (k - 5) // 3 + 1
                        for t in (2 * a, 2 * a + 1):
                            pool.wait_ge(d_done.sem, d_done.at(w, ev_pre(t, k) + 1))
                            level(w, t, l + 1)
                for h in range(HN):
                    piece_low(w, N_DN1 + h, h % 2, hL[:, 4 + h, :], hH[:, 4 + h, :])
                with pool.Fori(0, 4) as i:
                    for s in range(2):
                        next_low(w, 14 + i, s)
                residual_odd(w, 0)
                norm_pieces(w, N_HF1)
                with pool.Fori(0, NJ // 2) as i:
                    for q in range(2):
                        for s in range(2):
                            next_low(w, 18 + i * 2 + q, s)
                        piece_low(w, N_HID1 + i * 2 + q, q, hidL1[:, bass.ds(i * 2 + q, 1), :],
                                  hidH1[:, bass.ds(i * 2 + q, 1), :])
                with pool.Fori(0, 12) as i:
                    for s in range(2):
                        next_low(w, 40 + i, s)
                residual_odd(w, 1)

            with pool.Fori(0, LAYERS) as L:
                w = Where(1, L)
                layer_params(w)
                norm_pieces(w, N_H2)
                for u in range(21):
                    next_low(w, u // 2, u % 2)
                    j = turn_of(1, u)
                    if j is not None and j < N_ROT[1]:
                        pool.wait_ge(acc_free[u % 2].sem, acc_free[u % 2].at(w, u // 2 + 1))
                        pool.wait_ge(turn_done.sem, turn_done.at(w, j - 1))
                        pool.tensor_tensor(pt2[:, j % 2, :], turn_src(1, j), rope2[:, 0, :],
                                           ALU.mult).then_inc(cos_done.sem, 1)
                    if 0 < u - POOL_U <= 4:
                        g = u - POOL_U - 1
                        piece_low(w, N_PD2 + g, g % 2, pdL[:, g, :], pdH[:, g, :])
                for g in range(4):
                    piece_low(w, N_PY2 + g, g % 2, hL[:, g, :], hH[:, g, :])
                next_low(w, 10, 1)
                for f in range(4):
                    piece_low(w, N_ATT2 + f, f % 2, att_place(w, f, hL), att_place(w, f, hH), heads)
                with pool.Fori(0, 4) as i:
                    for s in range(2):
                        next_low(w, 11 + i, s)
                residual_odd(w, 0)
                norm_pieces(w, N_HF2)
                for c in range(FCHUNKS):
                    with pool.Fori(0, HCH // 2) as i:
                        for s in range(2):
                            next_low(w, 15 + 16 * c + i, s)
                            piece_low(w, N_HID2 + HCH * c + i * 2 + s, s, hidL2[:, bass.ds(i * 2 + s, 1), :],
                                      hidH2[:, bass.ds(i * 2 + s, 1), :])
                    with pool.Fori(0, KD) as i:
                        for s in range(2):
                            next_low(w, 23 + 16 * c + i, s)
                residual_odd(w, 1)

        @block.scalar
        def _(act):
            for ring in (w_hi, unit_done, *acc_free, sq_used, sc_read, turn_done, ix_used):
                act.nop().then_inc(ring.sem, ring.credit)

            def w_high(w, i2, s):
                act.wait_ge(loaded[s].sem, loaded[s].at(w, 16 * (i2 + 1)))
                act.wait_ge(unit_done.sem, unit_done.at(w, 2 * i2 + s - 1))
                act.activation(wH[:, s, :], raw[:, s, :], ACT.Copy).then_inc(w_hi.sem, 1)

            def next_high(w, i2, s):
                w_high(w, i2 + 1, s)

            def use_table(name):
                act.preload_act_table_set(name)

            def unit_wait(w, i2, s):
                act.wait_ge(unit_done.sem, unit_done.at(w, 2 * i2 + s + 1))

            def piece_high(w, n, s, dst, shape=lambda ap: ap):
                act.wait_ge(piece_ready.sem, piece_ready.at(w, n + 1))
                act.activation(dst, shape(piece[:, s, :]), ACT.Copy).then_inc(piece_hi.sem, 1)

            def square(w, r, s, src):
                act.wait_ge(sq_used.sem, sq_used.at(w, r - 1))
                act.activation(sq[:, s, :], src, ACT.Square).then_inc(sq_ready.sem, 1)

            def output_root(w, half):
                act.wait_ge(out_summed.sem, out_summed.at(w, half + 1))
                act.activation(root[:, 0, 0:NT], TRO[:, 0:NT], ACT.Sqrt, bias=cst("eps"),
                               scale=1.0 / D).then_inc(root_ready.sem, 1)
                use_table("natural_log")

            def norm(w, r0, half, n0, x0):
                for k in range(KD):
                    act.wait_ge(x_ready[k % 2].sem, x_ready[k % 2].at(w, x0 // 2 + k // 2 + 1))
                    square(w, r0 + k, k % 2, x[:, k, :])
                if half == 0:
                    act.wait_ge(par_loaded.sem, par_loaded.at(w, 16))
                    act.activation(par[:, :], par_next[:, :], ACT.Copy).then_inc(par_in.sem, 1)
                act.wait_ge(sq_used.sem, sq_used.at(w, r0 + KD))
                act.activation(rstd[:, :], STAT[:, :], ACT.Ln, bias=cst("eps"),
                               scale=1.0 / D).then_inc(stat_free.sem, 1)
                use_table("exp_and_others")
                act.drain()
                act.activation(rstd[:, :], rstd[:, :], ACT.Exp, scale=-0.5).then_inc(rstd_ready.sem, 1)
                if half == 0:
                    narrow_gates(w)
                for k in range(KD):
                    piece_high(w, n0 + k, (n0 + k) % 2, hH[:, k, :])

            def narrow_gates(w):
                act.wait_ge(par_in.sem, par_in.at(w, 1))
                act.activation(gwH[:, :], prm(w, "gates", 0, KD * 8), ACT.Copy).then_inc(gw_hi.sem, 1)

            def turn_input(w, j, i2, s, bank_i, a2, scale):
                unit_wait(w, i2, s)
                act.wait_ge(turn_done.sem, turn_done.at(w, j - 1))
                act.activation(turn_src(w.b, j), ACC[bank_i][:, :], ACT.Copy,
                               scale=scale).then_inc(acc_free[bank_i].sem, 1)

            def attention(w, n):
                q, k, v, sc, pt, ao, st, _, _ = ATT[w.b]
                if n < 32:
                    act.wait_ge(nmax.sem, nmax.at(w, n + 1))
                    wd = P * (att_step(n)[1] + 1)
                    act.activation(sc[:, n % 2, 0:wd], sc[:, n % 2, 0:wd], ACT.Exp,
                                   bias=st[:, NMX + n % 4:NMX + n % 4 + 1],
                                   accum_out=st[:, SUM + n % 4:SUM + n % 4 + 1]).then_inc(prob.sem, 1)
                m = n - 1
                if 0 <= m < 32:
                    act.wait_ge(pt_done.sem, pt_done.at(w, m + 1))
                    if m >= 2:
                        act.wait_ge(pv_done.sem, pv_done.at(w, m - 1))
                    wd = P * (att_step(m)[1] + 1)
                    act.activation(pt[:, m % 2, 0:wd], PT[:, 0:wd], ACT.Copy).then_inc(pt_copied.sem, 1)
                if n % 8 == 2 and n >= 10:
                    f = (n - 10) // 8
                    piece_high(w, ATT[w.b][8] + f, f % 2, att_place(w, f, hH), heads)

            def out_unit(w, i, s, j2, r, a2, bank_i):
                unit_wait(w, j2, s)
                square(w, r, s, ACC[bank_i][:, :])
                act.activation(MT[w.b][:, bass.ds(i, 1), :], ACC[bank_i][:, :], ACT.Copy)
                act.drain().then_inc(acc_free[bank_i].sem, 1)
                next_high(w, j2, s)

            def gate_functions(w):
                act.wait_ge(gate_a.sem, gate_a.at(w, 1))
                act.activation(gcol(E1, E1 + 16), gcol(AX, AX + 16), ACT.Exp, scale=-1.0)
                act.activation(gv[:, EBV:EBV + 16].rearrange("p (t h) -> p t h", h=4),
                               gv[:, BA:BA + 32].rearrange("p (t c) -> p t c", c=8)[:, :, 0:4], ACT.Exp, scale=-1.0)
                act.activation(gcol(EA, EA + 4), prm(w, "alog", 0, 4), ACT.Exp)
                act.drain()
                act.activation(gcol(SP_, SP_ + 16), gcol(E1, E1 + 16), ACT.Ln, bias=cst("one"))
                act.drain().then_inc(gate_b.sem, 1)

            for s in range(2):
                w_high(Where(0, 0), 0, s)
            act.wait_ge(const_in, 16)
            act.wait_ge(rope_sin_in, 1)
            act.activation(rope2[:, 1, :], ang[:, 2, :], ACT.Sin)
            act.activation(rope2[:, 0, :], ang[:, 3, :], ACT.Sin, bias=cst("halfpi"), scale=-1.0)
            act.drain().then_inc(rope_ready, 1)
            use_table("natural_log")
            for q in range(4):
                act.wait_ge(x_in[q], 16)
                for m in range(2):
                    act.nop().then_inc(x_ready[m].sem, 1)
            with act.Fori(0, LAYERS) as L:
                w = Where(0, L)
                norm(w, 0, 0, N_H1, -KD)
                for u in range(28):
                    if u == 12:
                        use_table("silu_and_others")
                    if u < 12:
                        turn_input(w, u, u // 2, u % 2, u % 2, u // 2, HD ** -0.5 if u < 4 else 1.0)
                    elif u < 24:
                        c = u - 12
                        if c >= 2:
                            act.wait_ge(dn_act.sem, dn_act.at(w, c - 1))
                        unit_wait(w, u // 2, u % 2)
                        act.activation(xconv(c), ACC[u % 2][:, :], ACT.Copy,
                                       scale=prm(w, "dconv", 4 * c + 3, 4 * c + 4)).then_inc(conv_in.sem, 1)
                    else:
                        unit_wait(w, u // 2, u % 2)
                        act.activation(zT[:, u - 24, :], ACC[u % 2][:, :], ACT.Copy).then_inc(acc_free[u % 2].sem, 1)
                    next_high(w, u // 2, u % 2)
                    if 13 <= u < 25:
                        c = u - 13
                        act.wait_ge(acc_free[(u - 1) % 2].sem, acc_free[(u - 1) % 2].at(w, (u - 1) // 2 + 1))
                        act.activation((dq, dk, dv)[c // 4][:, c % 4, :], xconv(c), ACT.Silu).then_inc(dn_act.sem, 1)
                        if c < 8:
                            act.wait_ge(dn_act.sem, dn_act.at(w, c + 1))
                            square(w, 8 + c, c % 2, (dq, dk)[c // 4][:, c % 4, :])
                    if u == 5:
                        use_table("exp_and_others")
                    if u == 6:
                        gate_functions(w)
                    if u in (24, 25):
                        if u == 24:
                            use_table("natural_log")
                        act.wait_ge(l2_copied.sem, l2_copied.at(w, 4 * (u - 23)))
                        act.activation(l2_stat(u - 24), l2_stat(u - 24), ACT.Ln, bias=cst("eps"))
                    if u in (26, 27):
                        if u == 26:
                            act.drain()
                            use_table("exp_and_others")
                        act.activation(l2_stat(u - 26), l2_stat(u - 26), ACT.Exp,
                                       bias=cst("qscale") if u == 26 else 0.0, scale=-0.5).then_inc(l2_rstd.sem, 1)
                for kind, a, k in ORDER:
                    if kind == "att":
                        attention(w, a)
                        if a == 32:
                            use_table("silu_and_others")
                            for h in range(HN):
                                act.activation(zT[:, h, :], zT[:, h, :], ACT.Silu).then_inc(z_ready.sem, 1)
                    elif kind == "small":
                        act.wait_ge(kd_in.sem, kd_in.at(w, 1))
                        act.activation(gcol(KD_, KD_ + 16), gcol(KDI, KDI + 16), ACT.Exp)
                        act.activation(gcol(EG, EG + 16), gcol(SM, SM + 16), ACT.Exp)
                        act.activation(gcol(GLB, GLB + 32), gcol(SM + 32, SM + 64), ACT.Exp)
                        act.drain().then_inc(kd_out.sem, 1)
                    elif kind == "pre":
                        for t in (2 * a, 2 * a + 1):
                            e = ev_pre(t, k)
                            free = d_free[e % 3]
                            if k in (0, 4, 5, 8, 11, 14, 17, 21, 22):
                                act.wait_ge(d_done.sem, d_done.at(w, e + 1))
                            if k == 0:
                                act.activation(xtb[t % 2][:, :, :], heads(DB[e % 3][:, :]), ACT.Exp).then_inc(gr_exp.sem, 1)
                                act.wait_ge(e_in.sem, e_in.at(w, t + 1))
                                act.activation(eb[t % 2][:, :, :], eb[t % 2][:, :, :], ACT.Exp).then_inc(e_ready.sem, 1)
                            elif k == 4:
                                act.activation(xb[t % 2][:, :, :], heads(DB[e % 3][:, :]), ACT.Copy).then_inc(free.sem, 1)
                            elif k in (5, 8, 11, 14, 17):
                                act.activation(mb[t % 2][:, :, :], heads(DB[e % 3][:, :]), ACT.Copy).then_inc(free.sem, 1)
                            elif k == 21:
                                act.activation(dv[:, :, t * P:t * P + P], heads(DB[e % 3][:, :]), ACT.Copy).then_inc(free.sem, 1)
                            elif k == 22:
                                act.activation(dk[:, :, t * P:t * P + P], heads(DB[e % 3][:, :]), ACT.Copy).then_inc(free.sem, 1)
                    elif k == 2:
                        e = ev_scan(a, 2)
                        act.wait_ge(d_done.sem, d_done.at(w, e + 1))
                        act.activation(dq[:, :, a * CH:a * CH + CH],
                                       DB[e % 3][:, 0:HN * CH].rearrange("p (h c) -> p h c", c=CH),
                                       ACT.Copy).then_inc(d_free[e % 3].sem, 1)
                act.drain()
                use_table("sqrt_and_others")
                for h in range(HN):
                    square(w, 16 + h, h % 2, dq[:, h, :])
                act.wait_ge(sq_used.sem, sq_used.at(w, 16 + HN))
                act.activation(root[:, 0, :], TRO[:, 0:4 * NT], ACT.Sqrt, bias=cst("eps"),
                               scale=1.0 / P).then_inc(dn_root.sem, 1)
                for h in range(HN):
                    piece_high(w, N_DN1 + h, h % 2, hH[:, 4 + h, :])
                use_table("sqrt_and_others")
                with act.Fori(0, 4) as i:
                    for s in range(2):
                        out_unit(w, i * 2 + s, s, i + 14, i * 2 + 20 + s, i + 14, s)
                output_root(w, 0)
                norm(w, 28, 1, N_HF1, 0)
                use_table("gelu_apprx_tanh_and_others")
                with act.Fori(0, NJ // 2) as i:
                    for q in range(2):
                        i2 = i * 2 + q + 18
                        for s in range(2):
                            unit_wait(w, i2, s)
                            act.activation(mT1[:, 2 * q + s, :], ACC[s][:, :], ACT.Identity,
                                           bias=prmd(w, "fbias", i * 4 + 2 * q + s),
                                           scale=prmd(w, "fconv", i * 12 + 6 * q + 3 * s + 2)).then_inc(glu_in.sem, 1)
                            next_high(w, i2, s)
                            if s == 0:
                                act.wait_ge(acc_free[0].sem, acc_free[0].at(w, i2 + 1))
                                act.activation(mT1[:, 2 * q, :], mT1[:, 2 * q, :],
                                               ACT.Gelu_apprx_tanh).then_inc(gelu_done.sem, 1)
                        piece_high(w, N_HID1 + i * 2 + q, q, hidH1[:, bass.ds(i * 2 + q, 1), :])
                use_table("sqrt_and_others")
                with act.Fori(0, 4) as i:
                    for m in range(2):
                        for u in range(2):
                            y = 3 * m + u
                            next_high(w, i * 3 + 40 + y // 2, y % 2)
                        y = 3 * m + 2
                        unit_wait(w, i * 3 + 40 + y // 2, y % 2)
                        square(w, i * 2 + 36 + m, m, ACC[m][:, :])
                        act.activation(mT1[:, bass.ds(i * 2 + m, 1), :], ACC[m][:, :], ACT.Copy)
                        act.drain().then_inc(acc_free[m].sem, 1)
                        next_high(w, i * 3 + 40 + y // 2, y % 2)
                output_root(w, 1)

            with act.Fori(0, LAYERS) as L:
                w = Where(1, L)
                norm(w, 0, 0, N_H2, -KD)
                for u in range(21):
                    for y in IX_AT.get(u, ()):
                        wd = P * (y // 8 + 1)
                        act.wait_ge(ix_done.sem, ix_done.at(w, y + 1))
                        act.wait_ge(ix_used.sem, ix_used.at(w, y - 1))
                        act.activation(ir[:, y % 2, 0:wd], (PT, OA)[y % 2][:, 0:wd], ACT.Relu,
                                       scale=HD ** -0.5).then_inc(ix_relu.sem, 1)
                    j = turn_of(1, u)
                    if j is not None:
                        turn_input(w, j, u // 2, u % 2, u % 2, u // 2, HD ** -0.5 if 5 <= j < 9 else 1.0)
                    else:
                        g = u - POOL_U
                        unit_wait(w, u // 2, u % 2)
                        if g >= 2:
                            act.wait_ge(piece_ready.sem, piece_ready.at(w, N_PD2 + g - 1))
                        act.activation(pu[:, g % 2, :], ACC[u % 2][:, :], ACT.Copy).then_inc(acc_free[u % 2].sem, 1)
                    next_high(w, u // 2, u % 2)
                    if 0 < u - POOL_U <= 4:
                        g = u - POOL_U - 1
                        piece_high(w, N_PD2 + g, g % 2, pdH[:, g, :])
                for g in range(4):
                    piece_high(w, N_PY2 + g, g % 2, hH[:, g, :])
                next_high(w, 10, 1)
                use_table("exp_and_others")
                for n in range(SLOTS):
                    attention(w, n)
                use_table("sqrt_and_others")
                with act.Fori(0, 4) as i:
                    for s in range(2):
                        out_unit(w, i * 2 + s, s, i + 11, i * 2 + 8 + s, i + 12, (25 + s) % 2)
                output_root(w, 0)
                norm(w, 16, 1, N_HF2, 0)
                for c in range(FCHUNKS):
                    with act.Fori(0, HCH // 2) as i:
                        for s in range(2):
                            bk = (33 + s) % 2
                            unit_wait(w, i + 15 + 16 * c, s)
                            act.activation(relu[:, s, :], ACC[bk][:, :], ACT.Relu).then_inc(acc_free[bk].sem, 1)
                            next_high(w, i + 15 + 16 * c, s)
                            piece_high(w, N_HID2 + HCH * c + i * 2 + s, s, hidH2[:, bass.ds(i * 2 + s, 1), :])
                    with act.Fori(0, KD // 2) as i:
                        for m in range(2):
                            bk = (49 + m) % 2
                            next_high(w, i * 2 + 23 + 16 * c + m, 0)
                            unit_wait(w, i * 2 + 23 + 16 * c + m, 1)
                            if c == 0:
                                act.activation(mT2[:, bass.ds(i * 2 + m, 1), :], ACC[bk][:, :],
                                               ACT.Copy).then_inc(acc_free[bk].sem, 1)
                            else:
                                act.wait_ge(acc_free[bk].sem, acc_free[bk].at(w, i + 12 * c + 24 + m + 1))
                                square(w, i * 2 + 24 + m, m, mT2[:, bass.ds(i * 2 + m, 1), :])
                            next_high(w, i * 2 + 23 + 16 * c + m, 1)
                output_root(w, 1)

        @block.vector
        def _(dve):

            def new_piece(w, n):
                dve.wait_ge(piece_lo.sem, piece_lo.at(w, n - 1))

            def norm(w, half, n0, name):
                if half == 0:
                    dve.wait_ge(par_in.sem, par_in.at(w, 1))
                dve.wait_ge(rstd_ready.sem, rstd_ready.at(w, half + 1))
                for k in range(KD):
                    new_piece(w, n0 + k)
                    dve.scalar_tensor_tensor(piece[:, k % 2, :], x[:, k, :], prm(w, name, k, k + 1),
                                             rstd[:, :], ALU.mult, ALU.mult).then_inc(piece_ready.sem, 1)

            def sum_output(w, k, r0, of_bank=None):
                dve.memset(SQ_SUM[w.b][:, :], 0.0)
                dve.drain()
                with dve.Fori(0, KD // 2) as i:
                    for m in range(2):
                        if of_bank:
                            of_bank(i, m)
                        dve.wait_ge(sq_ready.sem, sq_ready.at(w, i * 2 + r0 + m + 1))
                        dve.tensor_tensor(SQ_SUM[w.b][:, :], SQ_SUM[w.b][:, :], sq[:, m, :], ALU.add).then_inc(sq_used.sem, 1)
                        dve.drain()
                dve.drain().then_inc(sq_summed.sem, 1)

            def copy_gates(w):
                dve.wait_ge(gates_raw.sem, gates_raw.at(w, 1))
                dve.tensor_copy(gates_place(w.b), TRO[0:8, :]).then_inc(gates_copied.sem, 1)

            def residual(w, half, name):
                m = MT[w.b]
                dve.wait_ge(root_ready.sem, root_ready.at(w, half + 1))
                dve.reciprocal(root[:, 1, 0:NT], root[:, 0, 0:NT]).then_inc(root_inv.sem, 1)
                dve.wait_ge(spread.sem, spread.at(w, half + 1))

                for k in range(0, KD, 2):
                    for m_ in (1, 0):
                        op = dve.scalar_tensor_tensor(m[:, k + m_, :], m[:, k + m_, :], prm(w, name, k + m_, k + m_ + 1),
                                                      PT[:, :], ALU.mult, ALU.mult)
                        if m_:
                            op.then_inc(out_scaled.sem, 1)
                    dve.drain()
                    dve.tensor_tensor(x[:, k, :], x[:, k, :], m[:, k, :], ALU.add).then_inc(x_ready[0].sem, 1)

            def turn_finish(w, j):
                t1, t2 = ATT[w.b][3][:, 0, :], ATT[w.b][3][:, 1, :]
                cos, sin = (rope2[:, 0, :], rope2[:, 1, :]) if w.b else (cst("cos1"), cst("sin1"))
                dve.wait_ge(turned.sem, turned.at(w, j + 1))
                if j < N_ROT[w.b]:
                    if w.b:
                        t2 = pt2[:, j % 2, :]
                        dve.wait_ge(cos_done.sem, cos_done.at(w, j + 1))
                    dve.tensor_tensor(t1, SC[j % 2][:, :], sin, ALU.mult)
                    if w.b == 0:
                        dve.tensor_tensor(t2, turn_src(w.b, j), cos, ALU.mult)
                    dve.drain()
                    dve.tensor_tensor(turn_dst(w.b, j), t1, t2, ALU.add).then_inc(turn_done.sem, 1)
                    dve.drain()
                else:
                    f = j - N_ROT[w.b]
                    dve.tensor_copy(ATT[w.b][2][:, :, f * P:f * P + P], heads(SC[j % 2][:, :])).then_inc(turn_done.sem, 1)

            def attention(w, n):
                q, k, v, sc, pt, ao, st, _, n0 = ATT[w.b]
                if n < 32:
                    wd = P * (att_step(n)[1] + 1)
                    c = n % 4
                    dve.wait_ge(sc_done.sem, sc_done.at(w, n + 1))
                    if n >= 2:
                        dve.wait_ge(pt_done.sem, pt_done.at(w, n - 1))
                    dve.memset(st[:, 16:17], 0.0)
                    dve.tensor_tensor_reduce(sc[:, n % 2, 0:wd], SC[n % 2][:, 0:wd], bias_of(w.b, att_step(n)[1]),
                                             1.0, NEG, ALU.add, ALU.max,
                                             st[:, MX + c:MX + c + 1]).then_inc(sc_read.sem, 1)
                    dve.drain()
                    dve.tensor_scalar(st[:, NMX + c:NMX + c + 1], st[:, MX + c:MX + c + 1], -1.0, None,
                                      ALU.mult).then_inc(nmax.sem, 1)
                m = n - 2
                if 0 <= m < 32:
                    c, p = m % 4, m // 2
                    dve.wait_ge(pv_done.sem, pv_done.at(w, m + 1))
                    dve.reciprocal(st[:, RS + c:RS + c + 1], st[:, SUM + c:SUM + c + 1])
                    dve.drain()
                    if p >= 2:
                        dve.wait_ge(tro_done.sem, tro_done.at(w, p - 1))
                    dve.tensor_scalar(ao[:, p % 2, m % 2 * HD:m % 2 * HD + HD], OA[:, 0:HD],
                                      st[:, RS + c:RS + c + 1], None, ALU.mult).then_inc(oa_read.sem, 1)
                if n % 8 == 2 and n >= 10:
                    f = (n - 10) // 8
                    dve.wait_ge(tro_done.sem, tro_done.at(w, 4 * f + 4))
                    new_piece(w, n0 + f)
                    dve.tensor_copy(piece[:, f % 2, :], TRO[:, :]).then_inc(piece_ready.sem, 1)

            def convolve(w, c):
                u = c + 12
                dve.wait_ge(conv_in.sem, conv_in.at(w, c + 1))
                for lag in (1, 2, 3):
                    last = dve.scalar_tensor_tensor(xconv(c)[:, lag:S], ACC[u % 2][:, 0:S - lag],
                                                    prm(w, "dconv", 4 * c + 3 - lag, 4 * c + 4 - lag),
                                                    xconv(c)[:, lag:S], ALU.mult, ALU.add)
                    if lag < 3:
                        dve.drain()
                last.then_inc(acc_free[u % 2].sem, 1)

            def by_head(ap):
                return ap.rearrange("p (t h) -> p t h", h=4)

            def delta_gates(w):
                ba = gv[:, BA:BA + 32].rearrange("p (t c) -> p t c", c=8)

                dve.wait_ge(gates_done.sem, gates_done.at(w, 1))
                dve.tensor_copy(gv[:, BA:BA + 32], OA[:, 0:32])
                dve.drain()
                dve.tensor_tensor(by_head(gcol(XA, XA + 16)), ba[:, :, 4:8],
                                  over_heads(prm(w, "dt", 0, 4)), ALU.add)
                dve.drain()
                dve.tensor_scalar(gcol(AX, AX + 16), gcol(XA, XA + 16), -1.0, None, ALU.mult)
                dve.drain()
                dve.tensor_tensor(gcol(AX, AX + 16), gcol(AX, AX + 16), gcol(XA, XA + 16), ALU.max)
                dve.drain().then_inc(gate_a.sem, 1)
                dve.tensor_scalar(gcol(XA, XA + 16), gcol(XA, XA + 16), 0.0, None, ALU.max)

            def delta_gates_end(w):
                dve.wait_ge(gate_b.sem, gate_b.at(w, 1))
                dve.tensor_scalar(gcol(EBV, EBV + 16), gcol(EBV, EBV + 16), 1.0, None, ALU.add)
                dve.drain()
                dve.reciprocal(gcol(BETA, BETA + 16), gcol(EBV, EBV + 16))
                dve.tensor_tensor(gcol(G_, G_ + 16), gcol(SP_, SP_ + 16), gcol(XA, XA + 16), ALU.add)
                dve.drain()
                dve.tensor_tensor(by_head(gcol(G_, G_ + 16)), by_head(gcol(G_, G_ + 16)),
                                  over_heads(gcol(EA, EA + 4)), ALU.mult)
                dve.drain()
                dve.tensor_scalar(gcol(G_, G_ + 16), gcol(G_, G_ + 16), -1.0, None, ALU.mult)
                dve.drain().then_inc(g_ready.sem, 1)

            def delta_small(w):
                dve.wait_ge(d_done.sem, d_done.at(w, 1))
                dve.tensor_copy(gcol(SM, SM + 64), DB[0][:, 0:64]).then_inc(d_free[0].sem, 1)
                dve.drain()
                dve.tensor_tensor(gcol(KDI, KDI + 16), gcol(SM + 16, SM + 32), gcol(SM, SM + 16), ALU.subtract)
                dve.drain().then_inc(kd_in.sem, 1)
                dve.wait_ge(kd_out.sem, kd_out.at(w, 1))
                dve.tensor_tensor(gcol(BG, BG + 16), gcol(BETA, BETA + 16), gcol(EG, EG + 16), ALU.mult)
                dve.drain()

            def delta_pre(w, t, k):
                e = ev_pre(t, k)
                psum, free = heads(DB[e % 3][:, :]), d_free[e % 3].sem
                E, A, X, XT = (r[t % 2][:, :, :] for r in (eb, ab, xb, xtb))
                if k in (4, 5, 8, 11, 14, 17, 21, 22):
                    return
                if k > 4 or k == 2:
                    dve.drain()
                dve.wait_ge(d_done.sem, d_done.at(w, e + 1))
                if k == 0:
                    dve.wait_ge(gr_exp.sem, gr_exp.at(w, t + 1))
                    dve.tensor_tensor(E, psum, over_heads(cst("causal")), ALU.add).then_inc(free, 1)
                    dve.drain()
                    dve.tensor_tensor(E, E, per_head(tile4(SM, t)), ALU.subtract).then_inc(e_in.sem, 1)
                elif k == 1:
                    dve.wait_ge(e_ready.sem, e_ready.at(w, t + 1))
                    dve.tensor_tensor(A, psum, E, ALU.mult).then_inc(free, 1)
                elif k == 2:
                    dve.tensor_tensor(A, psum, A, ALU.mult).then_inc(free, 1)
                elif k == 3:
                    dve.tensor_tensor(qkT[:, t, :, :], psum, E, ALU.mult).then_inc(free, 1)
                    dve.tensor_tensor(dq[:, :, t * P:t * P + P], dq[:, :, t * P:t * P + P], XT,
                                      ALU.mult).then_inc(qdec_ready.sem, 1)
                    dve.drain()
                    dve.tensor_tensor(E, A, over_heads(cst("level", 0, P)), ALU.mult)
                    dve.drain()
                    dve.tensor_tensor(XT, over_heads(cst("ident")), E, ALU.subtract).then_inc(xt_ready.sem, 1)
                elif k in (6, 9, 12, 15):
                    dve.tensor_tensor(X, X, psum, ALU.subtract).then_inc(free, 1)
                elif k in (7, 10, 13, 16, 18):
                    dve.tensor_tensor(XT, XT, psum, ALU.subtract).then_inc(free, 1)
                elif k == 19:
                    dve.tensor_tensor(kdec[:, t, :, :], psum, per_head(tile4(KD_, t)), ALU.mult)
                    dve.tensor_tensor(A, psum, per_head(tile4(BG, t)), ALU.mult)
                    dve.drain().then_inc(free, 1)
                elif k == 20:
                    dve.tensor_tensor(E, psum, per_head(tile4(BETA, t)), ALU.mult).then_inc(free, 1)

            def delta_scan(w, c, j):
                t, p0 = c // 2, c % 2 * CH
                e = ev_scan(c, j)
                if j == 0:
                    dve.wait_ge(d_done.sem, d_done.at(w, e + 1))
                    dve.tensor_tensor(vn[p0:p0 + CH, :, :], dv[p0:p0 + CH, :, t * P:t * P + P],
                                      DB[e % 3][p0:p0 + CH, :].rearrange("p (h c) -> p h c", c=P),
                                      ALU.subtract).then_inc(d_free[e % 3].sem, 1)
                elif j == 1:
                    dve.drain()
                    dve.wait_ge(d_done.sem, d_done.at(w, e + 1))
                    for h in range(HN):
                        a = GLB + 16 * (c % 2) + 4 * t + h
                        dve.scalar_tensor_tensor(state_of(c + 1)[:, h, :], state_of(c)[:, h, :], gv[:, a:a + 1],
                                                 DB[e % 3][:, h * P:h * P + P], ALU.mult, ALU.add)
                    dve.drain().then_inc(d_free[e % 3].sem, 1)

            def delta_out(w, h):
                dve.wait_ge(dn_rstd.sem, dn_rstd.at(w, h + 1))
                dve.wait_ge(z_ready.sem, z_ready.at(w, h + 1))
                new_piece(w, N_DN1 + h)
                dve.scalar_tensor_tensor(piece[:, h % 2, :], dq[:, h, :], prm(w, "dnorm", 0, 1),
                                         DSTAT[h][:, :], ALU.mult, ALU.mult)
                dve.drain()
                dve.tensor_tensor(piece[:, h % 2, :], piece[:, h % 2, :], zT[:, h, :],
                                  ALU.mult).then_inc(piece_ready.sem, 1)

            R, N, T, A = (ang[:, i, :] for i in (2, 1, 0, 3))
            dve.wait_ge(const_in, 16)
            dve.wait_ge(pos_in, 16)
            dve.tensor_copy(T, posi[:, :])
            dve.drain()
            dve.tensor_scalar(T, T, cst("invf"), None, ALU.mult)
            dve.drain()
            dve.tensor_scalar(N, T, 1.0 / (2 * math.pi), None, ALU.mult)
            dve.drain()
            dve.tensor_scalar(N, N, 12582912.0, None, ALU.add)
            dve.drain()
            dve.tensor_scalar(N, N, -12582912.0, None, ALU.add)
            dve.drain()
            for part in TWO_PI:
                dve.scalar_tensor_tensor(T, N, -part, T, ALU.mult, ALU.add)
                dve.drain()
            dve.tensor_scalar(R, T, PI_BELOW, -PI_BELOW, ALU.min, ALU.max)
            dve.drain()
            dve.tensor_scalar(A, R, -1.0, None, ALU.mult)
            dve.drain()
            dve.tensor_tensor(A, A, R, ALU.max)
            dve.drain().then_inc(rope_sin_in, 1)

            with dve.Fori(0, LAYERS) as L:
                w = Where(0, L)
                norm(w, 0, N_H1, "pre")
                dve.memset(state[:, :, :], 0.0).then_inc(state_zero.sem, 1)
                dve.wait_ge(const_rest, 16)
                for u in range(24):
                    if u < 12:
                        turn_finish(w, u)
                    if u == 2:
                        copy_gates(w)
                    if 15 <= u < 23:
                        c = u - 15
                        dve.wait_ge(sq_used.sem, sq_used.at(w, 8 + c + 1))
                        dve.tensor_copy(l2_stat(c // 4)[:, c % 4, :, :], heads(STAT[:, :])).then_inc(l2_copied.sem, 1)
                    if u >= 12:
                        convolve(w, u - 12)
                    if u == 4:
                        delta_gates(w)
                    if u == 6:
                        delta_gates_end(w)
                for i in range(2):
                    tile = (dq, dk)[i][:, :, :]
                    dve.wait_ge(l2_rstd.sem, l2_rstd.at(w, i + 1))
                    dve.tensor_tensor(tile, tile, l2_stat(i).rearrange("p t h c -> p t (h c)"),
                                      ALU.mult).then_inc(l2_done.sem, 1)
                dve.drain()
                for kind, a, k in ORDER:
                    if kind == "att":
                        attention(w, a)
                    elif kind == "small":
                        delta_small(w)
                    elif kind == "pre":
                        delta_pre(w, 2 * a, k)
                        delta_pre(w, 2 * a + 1, k)
                    else:
                        delta_scan(w, a, k)
                dve.wait_ge(dn_root.sem, dn_root.at(w, 1))
                dve.reciprocal(root[:, 1, :], root[:, 0, :]).then_inc(dn_inv.sem, 1)
                for h in range(HN):
                    delta_out(w, h)
                sum_output(w, 0, 20)
                residual(w, 0, "post")
                norm(w, 1, N_HF1, "preff")
                with dve.Fori(0, NJ // 2) as i:
                    for q in range(2):
                        for s in range(2):
                            buf = mT1[:, 2 * q + s, :]
                            dve.wait_ge(glu_in.sem, glu_in.at(w, i * 4 + 2 * q + s + 1))
                            for lag in (1, 2):
                                last = dve.scalar_tensor_tensor(
                                    buf[:, lag:S], ACC[s][:, 0:S - lag],
                                    prmd(w, "fconv", i * 12 + 6 * q + 3 * s + 2 - lag), buf[:, lag:S],
                                    ALU.mult, ALU.add)
                                if lag == 1:
                                    dve.drain()
                            last.then_inc(acc_free[s].sem, 1)
                        dve.drain()
                        dve.wait_ge(gelu_done.sem, gelu_done.at(w, i * 2 + q + 1))
                        new_piece(w, i * 2 + N_HID1 + q)
                        dve.tensor_tensor(piece[:, q, :], mT1[:, 2 * q, :], mT1[:, 2 * q + 1, :],
                                          ALU.mult).then_inc(piece_ready.sem, 1)
                sum_output(w, 1, 36)
                residual(w, 1, "postff")

            def index_score(w, y):
                i, h = y // 8, y % 8
                score, r = bias_of(1, i), ir[:, y % 2, 0:P * (i + 1)]
                dve.wait_ge(ix_relu.sem, ix_relu.at(w, y + 1))
                if h == 0:
                    dve.tensor_scalar(score, r, iw[:, i, 0:1], None, ALU.mult).then_inc(ix_used.sem, 1)
                else:
                    dve.scalar_tensor_tensor(score, r, iw[:, i, h:h + 1], score, ALU.mult,
                                             ALU.add).then_inc(ix_used.sem, 1)
                dve.drain()
                if h == 7:
                    dve.memset(score[0:64, P * i + 64:P * i + P], REMOVED)
                    dve.drain()
                    if i == 0:
                        dve.tensor_scalar(score, score, 0.1 * REMOVED, NEG, ALU.is_le, ALU.mult)
                        dve.drain()

            def top_round(rounds):
                for i, r in rounds:
                    dve.max(top8[:, i - 1, :], bias_of(1, i))
                dve.drain()
                for i, r in rounds:
                    dve.match_replace(bias_of(1, i), top8[:, i - 1, :], bias_of(1, i), REMOVED)
                dve.drain()
                for i in [i for i, r in rounds if r == TOPK // 8 - 1]:
                    score = bias_of(1, i)
                    dve.tensor_scalar(score, score, 0.1 * REMOVED, NEG, ALU.is_gt, ALU.mult)
                    dve.drain()
                    dve.memset(score[0:64, P * i + 64:P * i + P], NEG)
                    dve.drain()

            def gate_scale(w):
                dve.wait_ge(gates_done.sem, gates_done.at(w, 1))
                dve.tensor_scalar(iw[:, :, :], OA[:, 0:32].rearrange("p (t h) -> p t h", h=8),
                                  8 ** -0.5, None, ALU.mult)
                dve.drain()

            def pool_window(w, g):
                win = 2 << g
                u = pu[:, g % 2, :]
                dve.wait_ge(acc_free[(POOL_U + g) % 2].sem, acc_free[(POOL_U + g) % 2].at(w, (POOL_U + g) // 2 + 1))
                src = u
                for step in range(g + 1):
                    lag, dst = 1 << step, sc2[:, step % 2, :]
                    dve.tensor_tensor(dst[:, lag:S], src[:, lag:S], src[:, 0:S - lag], ALU.add)
                    dve.tensor_copy(dst[:, 0:lag], src[:, 0:lag])
                    dve.drain()
                    src = dst
                other = sc2[:, (g + 1) % 2, 0:win]
                dve.tensor_tensor(other, src[:, 0:win], cst("icnt", 0, win), ALU.mult)
                new_piece(w, N_PD2 + g)
                dve.scalar_tensor_tensor(piece[:, g % 2, :], src, 1.0 / win, u, ALU.mult, ALU.subtract)
                dve.drain()
                dve.tensor_tensor(piece[:, g % 2, 0:win], other, u[:, 0:win], ALU.subtract)
                dve.drain().then_inc(piece_ready.sem, 1)

            with dve.Fori(0, LAYERS) as L:
                w = Where(1, L)
                norm(w, 0, N_H2, "pre")
                dve.wait_ge(rope_ready, 1)
                for u in range(21):
                    if u == 0:
                        copy_gates(w)
                    if u == 2:
                        gate_scale(w)
                    for y in IX_AT.get(u + 1, ()):
                        index_score(w, y)
                    j = turn_of(1, u)
                    if j is not None:
                        turn_finish(w, j)
                    else:
                        pool_window(w, u - POOL_U)
                    for rounds in TOP_AT.get(u, ()):
                        top_round(rounds)
                for g in range(4):
                    a = 21 + g
                    dve.wait_ge(pool_done.sem, pool_done.at(w, g + 1))
                    new_piece(w, N_PY2 + g)
                    dve.tensor_scalar(piece[:, g % 2, :], ACC[a % 2][:, :], prm(w, "pscale", g, g + 1), None,
                                      ALU.mult).then_inc(acc_free[a % 2].sem, 1)
                    dve.drain().then_inc(piece_ready.sem, 1)
                for n in range(SLOTS):
                    attention(w, n)
                    if n in TOP_STEPS:
                        top_round(TOP_STEPS[n])
                sum_output(w, 0, 8)
                residual(w, 0, "post")
                norm(w, 1, N_HF2, "preff")
                for c in range(FCHUNKS):
                    with dve.Fori(0, HCH // 2) as i:
                        for s in range(2):
                            bk = (33 + s) % 2
                            dve.wait_ge(acc_free[bk].sem, acc_free[bk].at(w, i + 12 * c + 16 + s + 1))
                            new_piece(w, i * 2 + N_HID2 + HCH * c + s)
                            dve.tensor_tensor(piece[:, s, :], relu[:, s, :], relu[:, s, :],
                                              ALU.mult).then_inc(piece_ready.sem, 1)

                def add_chunk(i, m):
                    bk = (49 + m) % 2
                    dve.wait_ge(unit_done.sem, unit_done.at(w, i * 4 + 46 + 32 * (FCHUNKS - 1) + 2 * m + 2))
                    dve.tensor_tensor(mT2[:, bass.ds(i * 2 + m, 1), :], mT2[:, bass.ds(i * 2 + m, 1), :],
                                      ACC[bk][:, :].unsqueeze(1), ALU.add).then_inc(acc_free[bk].sem, 1)

                sum_output(w, 1, 24, add_chunk)
                residual(w, 1, "postff")

        @block.tensor
        def _(pe):
            pe.wait_ge(const_in, 16)
            ident = cst("ident")

            def unit(w, i2, s, bk, a2, tiles, rhs_hi, rhs_lo, first=True, last=True, pieces=None, w0=0, done=True,
                     between=(), whole=(0, 0)):
                pe.wait_ge(w_lo.sem, w_lo.at(w, 2 * i2 + s + 1))
                if first:
                    pe.wait_ge(acc_free[bk].sem, acc_free[bk].at(w, a2))
                for k in range(tiles):
                    if pieces is not None:
                        n = whole[1] if whole[0] <= k < whole[1] else k + 1
                        pe.wait_ge(piece_lo.sem, piece_lo.at(w, pieces + n))
                    c = (w0 + k) * P
                    for j, (wt, rhs) in enumerate(((wH, rhs_hi(k)), (wL, rhs_hi(k)), (wH, rhs_lo(k)))):
                        mm = pe.matmul(ACC[bk][:, :], wt[:, s, c:c + P], rhs, start=first and k == 0 and j == 0,
                                       stop=last and k == tiles - 1 and j == 2)
                    for n, small in enumerate(between):
                        if k == n + tiles - 1 - len(between):
                            small()
                if done is None:
                    return mm
                mm.then_inc(unit_done.sem, 1)

            def h_hi(k):
                return hH[:, k, :]

            def h_lo(k):
                return hL[:, k, :]

            def token_sums(out, squares, **group):
                for t in range(NT):
                    mm = pe.matmul(out(t), squares[:, t * P:t * P + P], cst("ones", 0, 1), **group)
                return mm

            def norm_sum(w, r0):
                for k in range(KD):
                    pe.wait_ge(sq_ready.sem, sq_ready.at(w, r0 + k + 1))
                    pe.matmul(STAT[:, :], cst("ones"), sq[:, k % 2, :], start=k == 0,
                              stop=k == KD - 1).then_inc(sq_used.sem, 1)

            def output_sum(w, half):
                keep_warm(OA, 8)
                pe.wait_ge(sq_summed.sem, sq_summed.at(w, half + 1))
                token_sums(lambda t: TRO[:, t:t + 1], SQ_SUM[w.b], start=True, stop=True).then_inc(out_summed.sem, 1)
                pe.wait_ge(root_inv.sem, root_inv.at(w, half + 1))
                for t in range(NT):
                    mm = pe.matmul(PT[:, t * P:t * P + P], root[:, 1, t:t + 1].broadcast_to([P, P]), ident,
                                   start=True, stop=True)
                mm.then_inc(spread.sem, 1)
                keep_warm(OA, 14)

            def l2_sum(w, c):
                if c == 0:
                    pe.wait_ge(stat_free.sem, stat_free.at(w, 1))
                else:
                    pe.wait_ge(l2_copied.sem, l2_copied.at(w, c))
                pe.wait_ge(sq_ready.sem, sq_ready.at(w, 8 + c + 1))
                pe.matmul(STAT[:, :], cst("ones"), sq[:, c % 2, :], start=True, stop=True).then_inc(sq_used.sem, 1)

            def index_logits(w, y):
                i, h = y // 8, y % 8
                if y == 0:
                    pe.wait_ge(turn_done.sem, turn_done.at(w, 5))
                if y >= 2:
                    pe.wait_ge(ix_relu.sem, ix_relu.at(w, y - 1))
                p0 = h % 2 * HD
                pe.matmul((PT, OA)[y % 2][:, 0:P * (i + 1)], iqT[p0:p0 + HD, h // 2, i * P:i * P + P],
                          ikT[p0:p0 + HD, 0:P * (i + 1)], start=True, stop=True).then_inc(ix_done.sem, 1)

            def turn(w, j):
                src = turn_src(w.b, j)
                u = j if w.b == 0 or j < POOL_U else j + 4
                pe.wait_ge(acc_free[u % 2].sem, acc_free[u % 2].at(w, u // 2 + 1))
                if j < N_ROT[w.b]:
                    pe.matmul(SC[j % 2][:, :], cst("turn2" if w.b else "turn1"), src, start=True,
                              stop=True).then_inc(turned.sem, 1)
                else:
                    for t in range(NT):
                        tr = pe.transpose(SC[j % 2][:, t * P:t * P + P], src[:, t * P:t * P + P], ident)
                    tr.then_inc(turned.sem, 1)

            def narrow(w):
                pe.wait_ge(gw_lo.sem, gw_lo.at(w, 1))
                for k in range(KD):
                    for j, (a, g) in enumerate(((hH, gwH), (hH, gwL), (hL, gwH))):
                        mm = pe.matmul(TRO[0:8, :], g[:, k * 8:k * 8 + 8], a[:, k, :],
                                       start=k == 0 and j == 0, stop=k == KD - 1 and j == 2)
                mm.then_inc(gates_raw.sem, 1)

            def narrow_turn(w):
                for t in range(NT):
                    tr = pe.transpose(OA[:, t * 8:t * 8 + 8], gates_place(w.b)[:, t * P:t * P + P], ident[0:8, 0:8])
                tr.then_inc(gates_done.sem, 1)

            def keep_warm(free, n):
                for _ in range(n):
                    pe.matmul(free[:, 0:P], cst("ones"), ident, start=True, stop=True)

            def attention(w, n):
                q, k, v, sc, pt, ao, st, _, n0 = ATT[w.b]
                for n_ in (n,) if n < 32 else ():
                    f, i, h = att_step(n_)
                    if n_ == 0:
                        pe.wait_ge(turn_done.sem, turn_done.at(w, (12, 17)[w.b]))
                    if 1:
                        pe.wait_ge(sc_read.sem, sc_read.at(w, n - 1))
                    pe.matmul(SC[n_ % 2][:, 0:P * (i + 1)], q[h * HD:h * HD + HD, f, i * P:i * P + P],
                              k[h * HD:h * HD + HD, f, 0:P * (i + 1)], start=True, stop=True).then_inc(sc_done.sem, 1)
                m = n - 1
                if 0 <= m < 32:
                    f, i, h = att_step(m)
                    pe.wait_ge(prob.sem, prob.at(w, m + 1))
                    if m:
                        pe.wait_ge(pt_copied.sem, pt_copied.at(w, m))
                    for j in range(i + 1):
                        tr = pe.transpose(PT[:, j * P:j * P + P], sc[:, m % 2, j * P:j * P + P], ident)
                    tr.then_inc(pt_done.sem, 1)
                m = n - 2
                if 0 <= m < 32:
                    f, i, h = att_step(m)
                    pe.wait_ge(pt_copied.sem, pt_copied.at(w, m + 1))
                    if m:
                        pe.wait_ge(oa_read.sem, oa_read.at(w, m))
                    for j in range(i + 1):
                        mm = pe.matmul(OA[:, 0:HD], pt[:, m % 2, j * P:j * P + P],
                                       v[:, j, (2 * f + h) * HD:(2 * f + h) * HD + HD], start=j == 0, stop=j == i)
                    mm.then_inc(pv_done.sem, 1)
                if n >= 4 and n % 2 == 0:
                    p = (n - 4) // 2
                    pe.wait_ge(oa_read.sem, oa_read.at(w, 2 * p + 2))
                    if p % 4 == 0 and p >= 4:
                        pe.wait_ge(piece_ready.sem, piece_ready.at(w, n0 + p // 4))
                    pe.transpose(TRO[:, p % 4 * P:p % 4 * P + P], ao[:, p % 2, :], ident).then_inc(tro_done.sem, 1)

            def start(w, e, *operands):
                latest = {}
                for x_ in (e - 3, *operands):
                    latest[x_ % 3] = max(latest.get(x_ % 3, x_), x_)
                for b_, x_ in latest.items():
                    if x_ >= 0:
                        pe.wait_ge(d_free[b_].sem, d_free[b_].at(w, x_ // 3 + 1))
                return DB[e % 3]

            def delta_small(w):
                pe.wait_ge(g_ready.sem, g_ready.at(w, 1))
                for b in range(2):
                    pe.wait_ge(acc_free[b].sem, acc_free[b].at(w, 14))
                pe.wait_ge(l2_copied.sem, l2_copied.at(w, 8))
                out = start(w, 0)
                pe.matmul(out[:, 0:16], cst("upto"), gcol(G_, G_ + 16), start=True, stop=True)
                for i, name in enumerate(("even", "odd")):
                    pe.matmul(out[i * CH:i * CH + CH, 16:32], cst(name).broadcast_to([P, CH]), gcol(G_, G_ + 16),
                              start=True, stop=True)
                    mm = pe.matmul(out[:, 32 + 16 * i:48 + 16 * i], cst(name).broadcast_to([P, P]),
                                   gcol(G_, G_ + 16), start=True, stop=True)
                mm.then_inc(d_done.sem, 1)

            def delta_pre(w, t, k):
                operands = {5: (4,), 6: (5,), 7: (5,), 18: (17, 16), 21: (20, 18), 22: (19,)}.get(k, ())
                if k in (8, 11, 14, 17):
                    operands = (k - 2,)
                elif k in (9, 12, 15, 10, 13, 16):
                    operands = ((k - 1, k - 2) if k % 3 == 0 else (k - 2, k - 3))
                e = ev_pre(t, k)
                out = start(w, e, *(ev_pre(t, o) for o in operands))
                tc = slice(t * P, t * P + P)
                LT, A, X, XT, M = (r[t % 2] for r in (eb, ab, xb, xtb, mb))
                two = {}
                if k == 0:
                    two = {h: (gv[:, G_ + 4 * t + h:G_ + 4 * t + h + 1].broadcast_to([P, P]), cst("upto")) for h in range(HN)}
                elif k == 1:
                    two = {h: (gv[:, BETA + 4 * t + h:BETA + 4 * t + h + 1].broadcast_to([P, P]), ident) for h in range(HN)}
                elif k == 2:
                    pe.wait_ge(l2_done.sem, l2_done.at(w, 2))
                    two = {h: (dk[:, h, tc], dk[:, h, tc]) for h in range(HN)}
                elif k == 3:
                    two = {h: (dk[:, h, tc], dq[:, h, tc]) for h in range(HN)}
                elif k == 4:
                    pe.wait_ge(xt_ready.sem, xt_ready.at(w, t + 1))
                elif k in (5, 8, 11, 14, 17):
                    l = (k - 5) // 3 + 1
                    pe.wait_ge(lt_ready.sem, lt_ready.at(w, 10 * (t // 2) + 2 * (l - 1) + t % 2 + 1))
                    two = {h: (LT[:, h, :], X[:, h, :]) for h in range(HN)}
                elif k in (6, 9, 12, 15):
                    two = {h: (XT[:, h, :], M[:, h, :]) for h in range(HN)}
                elif k in (7, 10, 13, 16, 18):
                    two = {h: (M[:, h, :], XT[:, h, :]) for h in range(HN)}
                elif k == 20:
                    pe.wait_ge(dn_act.sem, dn_act.at(w, 12))
                elif k == 21:
                    two = {h: (XT[:, h, :], LT[:, h, :]) for h in range(HN)}
                elif k == 22:
                    two = {h: (A[:, h, :], XT[:, h, :]) for h in range(HN)}
                for h in range(HN):
                    o = out[:, h * P:h * P + P]
                    if h in two:
                        mm = pe.matmul(o, two[h][0], two[h][1], start=True, stop=True)
                    elif k == 4:
                        mm = pe.transpose(o, XT[:, h, :], ident)
                    else:
                        mm = pe.transpose(o, (dk if k == 19 else dv)[:, h, tc], ident)
                mm.then_inc(d_done.sem, 1)

            def delta_scan(w, c, j):
                t, p0 = c // 2, c % 2 * CH
                cc = slice(c * CH, c * CH + CH)
                e = ev_scan(c, j)
                old = state_of(c)
                if j == 0:
                    last_state = (ev_scan(c - 1, 1),) if c else ()
                    out = start(w, e, ev_pre(t, 21), ev_pre(t, 22), *last_state)
                    if c == 0:
                        pe.wait_ge(state_zero.sem, state_zero.at(w, 1))
                    for h in range(HN):
                        mm = pe.matmul(out[p0:p0 + CH, h * P:h * P + P], dk[:, h, cc], old[:, h, :],
                                       start=True, stop=True)
                elif j == 1:
                    out = start(w, e, ev_scan(c, 0))
                    for h in range(HN):
                        mm = pe.matmul(out[:, h * P:h * P + P], kdec[p0:p0 + CH, t, h, :], vn[p0:p0 + CH, h, :],
                                       start=True, stop=True)
                else:
                    out = start(w, e)
                    pe.wait_ge(qdec_ready.sem, qdec_ready.at(w, t + 1))
                    for h in range(HN):
                        o = out[:, h * CH:h * CH + CH]
                        pe.matmul(o, old[:, h, :], dq[:, h, cc], start=True, stop=False)
                        mm = pe.matmul(o, vn[p0:p0 + CH, h, :], qkT[p0:p0 + CH, t, h, p0:p0 + CH],
                                       start=False, stop=True)
                mm.then_inc(d_done.sem, 1)

            with pe.Fori(0, LAYERS) as L:
                w = Where(0, L)
                norm_sum(w, 0)
                for u in range(28):
                    unit(w, u // 2, u % 2, u % 2, u // 2, KD, h_hi, h_lo, pieces=N_H1 if u == 0 else None)
                    if u == 1:
                        pe.wait_ge(const_rest, 16)
                    if u == 5:
                        pe.wait_ge(gates_copied.sem, gates_copied.at(w, 1))
                    if 1 <= u <= 12:
                        turn(w, u - 1)
                    if u == 5:
                        narrow_turn(w)
                    if u == 3:
                        narrow(w)
                    if 14 <= u < 22:
                        l2_sum(w, u - 14)
                for kind, a, k in ORDER:
                    if kind == "att":
                        attention(w, a)
                    elif kind == "small":
                        delta_small(w)
                    elif kind == "pre":
                        delta_pre(w, 2 * a, k)
                        delta_pre(w, 2 * a + 1, k)
                    else:
                        delta_scan(w, a, k)
                start(w, EVENTS, EVENTS - 2, EVENTS - 1)
                keep_warm(ACC[0], 14)
                pe.wait_ge(piece_ready.sem, piece_ready.at(w, N_ATT1 + 4))
                for h in range(HN):
                    pe.wait_ge(sq_ready.sem, sq_ready.at(w, 16 + h + 1))
                    token_sums(lambda t, h=h: TRO[:, 4 * t + h:4 * t + h + 1], sq[:, h % 2, :], start=True,
                               stop=True).then_inc(sq_used.sem, 1)
                pe.wait_ge(dn_inv.sem, dn_inv.at(w, 1))
                for h in range(HN):
                    for t in range(NT):
                        mm = pe.matmul(DSTAT[h][:, t * P:t * P + P],
                                       root[:, 1, 4 * t + h:4 * t + h + 1].broadcast_to([P, P]), ident,
                                       start=True, stop=True)
                    mm.then_inc(dn_rstd.sem, 1)
                with pe.Fori(0, KD // 2) as i:
                    for s in range(2):
                        unit(w, i + 14, s, s, i + 14, KD, h_hi, h_lo, pieces=(N_ATT1, None)[s], whole=(0, 4))
                output_sum(w, 0)
                norm_sum(w, 28)
                with pe.Fori(0, NJ) as i:
                    for s in range(2):
                        unit(w, i + 18, s, s, i + 18, KD, h_hi, h_lo, pieces=(N_HF1, None)[s])
                with pe.Fori(0, KD // 2) as i:
                    for m in range(2):
                        for u in range(3):
                            y = 3 * m + u
                            unit(w, i * 3 + 40 + y // 2, y % 2, m, i + 40, min(8, NJ - 8 * u),
                                 lambda k, u=u: hidH1[:, 8 * u + k, :], lambda k, u=u: hidL1[:, 8 * u + k, :],
                                 first=u == 0, last=u == 2, pieces=N_HID1 + 8 * u if m == 0 else None)
                output_sum(w, 1)

            with pe.Fori(0, LAYERS) as L:
                w = Where(1, L)
                norm_sum(w, 0)
                for u in range(21):
                    unit(w, u // 2, u % 2, u % 2, u // 2, KD, h_hi, h_lo, pieces=N_H2 if u == 0 else None,
                         between=[lambda y=y: index_logits(w, y) for y in IX_AT.get(u, ())])
                    if u == 2:
                        pe.wait_ge(gates_copied.sem, gates_copied.at(w, 1))
                    if u and turn_of(1, u - 1) is not None:
                        turn(w, turn_of(1, u - 1))
                    if u == 0:
                        narrow(w)
                    if u == 2:
                        narrow_turn(w)
                turn(w, turn_of(1, 20))
                for g in range(4):
                    a = 21 + g
                    mm = unit(w, 10, 1, a % 2, a // 2, 1, lambda k, g=g: pdH[:, g, :], lambda k, g=g: pdL[:, g, :],
                              pieces=N_PD2 + g, w0=g, done=None)
                    mm.then_inc(pool_done.sem, 1)
                pe.wait_ge(pool_done.sem, pool_done.at(w, 4))
                pe.nop().then_inc(unit_done.sem, 1)
                for n in range(SLOTS):
                    attention(w, n)
                    keep_warm(STAT, 3)
                with pe.Fori(0, KD // 2) as i:
                    for s in range(2):
                        unit(w, i + 11, s, (25 + s) % 2, i + 12 + s, KD, h_hi, h_lo, pieces=(N_PY2, None)[s],
                             whole=(4, 8))
                output_sum(w, 0)
                norm_sum(w, 16)
                for c in range(FCHUNKS):
                    with pe.Fori(0, HCH // 2) as i:
                        for s in range(2):
                            unit(w, i + 15 + 16 * c, s, (33 + s) % 2, i + 12 * c + 16 + s, KD, h_hi, h_lo,
                                 pieces=(N_HF2, None)[s])
                    with pe.Fori(0, KD // 2) as i:
                        for m in range(2):
                            for s in range(2):
                                unit(w, i * 2 + 23 + 16 * c + m, s, (49 + m) % 2, i + 12 * c + 24 + m, KD,
                                     lambda k, s=s: hidH2[:, 8 * s + k, :], lambda k, s=s: hidL2[:, 8 * s + k, :],
                                     first=s == 0, last=s == 1,
                                     pieces=N_HID2 + HCH * c + 8 * s if m == 0 else None)
                output_sum(w, 1)


def tiles(a):
    return a.reshape(a.shape[0] // P, P, a.shape[1]).transpose(1, 0, 2)


def unit_of(a):
    u = tiles(a).reshape(P, -1)
    return np.pad(u, ((0, 0), (0, KD * P - u.shape[1])))


def columns(a, order):
    return [unit_of(a[:, c * P:c * P + P]) for c in order]


def channel_cols(a):
    return a.reshape(-1, P).T


def kernel(**inputs):
    import concourse.bacc as bacc
    from concourse.bass_utils import run_bass_kernel_spmd

    z = {k: np.ascontiguousarray(v) for k, v in inputs.items()}
    interleave = [c for j in range(NJ) for c in (j, NJ + j)]
    w0, w1, par0, par1 = [], [], [], []
    for l in range(LAYERS):
        win = z["w_in"][l]
        w0 += columns(win, range(28)) + columns(z["w_out"][l], range(KD)) + columns(z["ffn_w_in"][l], interleave)
        down = z["ffn_w_out"][l]
        for m in range(KD):
            w0 += [unit_of(down[r * P:min(r + 8, NJ) * P, m * P:m * P + P]) for r in (0, 8, 16)]
        fconv = z["ffn_conv_w"][l].reshape(FCONV, 2 * NJ, P)[:, interleave]
        par0.append(np.concatenate([
            channel_cols(z["norm_pre_mix"][l]), channel_cols(z["norm_post_mix"][l]),
            channel_cols(z["norm_pre_ffn"][l]), channel_cols(z["norm_post_ffn"][l]),
            z["dn_conv_w"][l].reshape(DCONV, 12, P).transpose(2, 1, 0).reshape(P, -1),
            z["dn_norm_w"][l][:, None],
            np.broadcast_to(z["dn_a_log"][l], (P, 4)), np.broadcast_to(z["dn_dt_bias"][l], (P, 4)),
            fconv.transpose(2, 1, 0).reshape(P, -1),
            z["ffn_conv_b"][l].reshape(2 * NJ, P)[interleave].T,
            tiles(win[:, 28 * P:]).reshape(P, -1)], axis=1))
        win = z["w_in_2"][l]
        ik = win[:, 20 * P:20 * P + 64]
        w1 += [unit_of(np.concatenate([ik, ik], axis=1))]
        w1 += columns(win, [*range(16, 20), *range(4), *range(4, 16)])
        wp = z["w_pool_2"][l]
        w1 += [unit_of(wp.reshape(4 * P, P))]
        w1 += columns(z["w_out_2"][l], range(KD))
        for c in range(FCHUNKS):
            w1 += columns(z["w_ff1_2"][l], range(HCH * c, HCH * c + HCH))
            down = z["w_ff2_2"][l][HCH * P * c:HCH * P * (c + 1)]
            for m in range(KD):
                w1 += [unit_of(down[r * D:r * D + D, m * P:m * P + P]) for r in range(2)]
        par1.append(np.concatenate([
            channel_cols(z["g_pre_mix_2"][l]), channel_cols(z["g_post_mix_2"][l]),
            channel_cols(z["g_pre_ffn_2"][l]), channel_cols(z["g_post_ffn_2"][l]),
            channel_cols(z["pool_scale_2"][l]), tiles(win[:, 20 * P + 64:]).reshape(P, -1)], axis=1))
    arrays = {
        "x_dram": np.ascontiguousarray(tiles(z["x"][0].T)),
        "w0_dram": np.stack(w0), "w1_dram": np.stack(w1),
        "par_dram": np.stack([np.pad(p, ((0, 0), (0, PAR_W - p.shape[1]))) for p in (*par0, *par1, par1[-1])]),
        "pos_dram": z["positions_2"][0], "const_dram": constants(),
    }
    nc = bacc.Bacc("TRN2", target_bir_lowering=False, num_devices=1)
    d = {n[:-5]: nc.dram_tensor(n, a.shape, mybir.dt.from_np(a.dtype), kind="ExternalInput").ap()
         for n, a in arrays.items()}
    d["out"] = nc.dram_tensor("out_dram", (P, KD, S), F32, kind="ExternalOutput").ap()
    build(nc, d)
    r = run_bass_kernel_spmd(nc, [arrays], core_ids=[0])
    out = r.results[0]["out_dram"]
    return np.ascontiguousarray(out.transpose(1, 0, 2).reshape(D, S).T).reshape(1, S, D)
```
